# Optimizing a Trainium2 kernel written in Bass

```python
import jax, jax.numpy as jnp
from jax import lax
import numpy as np

D_MODEL = 1024
BATCH = 1
SEQ = 256
DEPTH = 1

N_MIXERS = 2
ATT_HEADS = 8
ATT_HEAD_DIM = D_MODEL // ATT_HEADS
MOBA_BLOCK = 256
MOBA_TOPK = 3
MOBA_QUERY_CHUNK = 32
MLSTM_HEADS = 8
MLSTM_DV = D_MODEL // MLSTM_HEADS
MLSTM_DQK = MLSTM_DV // 2
MLSTM_CHUNK = 64
GATE_SOFTCAP = 15.0
D_FF = 4 * D_MODEL
RMS_EPS = 1e-6
N_ATTN_LAYERS = (DEPTH + N_MIXERS - 1) // N_MIXERS
N_MLSTM_LAYERS = DEPTH // N_MIXERS


def rms_norm(x, gain):
    xf = x.astype(jnp.float32)
    y = xf * lax.rsqrt(jnp.mean(xf * xf, axis=-1, keepdims=True) + RMS_EPS)
    return (y * gain.astype(jnp.float32)).astype(x.dtype)

def alibi_slopes(n_heads):
    return jnp.exp2(-8.0 * jnp.arange(1, n_heads + 1, dtype=jnp.float32) / n_heads)

def soft_cap(z):
    return GATE_SOFTCAP * jnp.tanh(z / GATE_SOFTCAP)

def moba_attention(x, w_qkv, w_o):
    bsz, seq, _ = x.shape
    H, dh, blk, qlen = ATT_HEADS, ATT_HEAD_DIM, MOBA_BLOCK, MOBA_QUERY_CHUNK
    f32 = jnp.float32
    q, k, v = jnp.split(x @ w_qkv, 3, axis=-1)

    def to_heads(t):
        return t.reshape(bsz, seq, H, dh).transpose(0, 2, 1, 3)

    q = to_heads(q) * (dh ** -0.5)
    k = to_heads(k)
    v = to_heads(v)
    n_blk = -(-seq // blk)
    pad = n_blk * blk - seq
    k_blk = jnp.pad(k, ((0, 0), (0, 0), (0, pad), (0, 0))).reshape(bsz, H, n_blk, blk, dh)
    v_blk = jnp.pad(v, ((0, 0), (0, 0), (0, pad), (0, 0))).reshape(bsz, H, n_blk, blk, dh)

    k_mean = jnp.mean(k_blk.astype(f32), axis=3)
    gate = jnp.einsum('bhsd,bhnd->bhsn', q.astype(f32), k_mean)
    n_past = jnp.arange(seq) // blk
    is_past = jnp.arange(n_blk)[None, :] < n_past[:, None]
    gate = jnp.where(is_past, gate, -jnp.inf)
    top = min(MOBA_TOPK, n_blk)
    _, sel = lax.top_k(gate, top)
    sel = sel.astype(jnp.int32)

    n_chunk = seq // qlen
    q_c = jnp.moveaxis(q.reshape(bsz, H, n_chunk, qlen, dh), 2, 0)
    sel_c = jnp.moveaxis(sel.reshape(bsz, H, n_chunk, qlen, top), 2, 0)
    slopes = alibi_slopes(H)
    b_idx = jnp.arange(bsz)[:, None, None, None]
    h_idx = jnp.arange(H)[None, :, None, None]
    offs = jnp.arange(blk)

    def attend_chunk(args):
        c, q_blk, sel_blk = args
        t = c * qlen + jnp.arange(qlen)
        own = (c * qlen) // blk
        k_own = lax.dynamic_index_in_dim(k_blk, own, axis=2, keepdims=False)
        v_own = lax.dynamic_index_in_dim(v_blk, own, axis=2, keepdims=False)
        dist_own = (t[:, None] - (own * blk + offs)[None, :]).astype(f32)
        s_own = jnp.einsum('bhqd,bhkd->bhqk', q_blk, k_own).astype(f32) - slopes[:, None, None] * dist_own
        s_own = jnp.where(dist_own >= 0, s_own, -jnp.inf)
        k_sel = k_blk[b_idx, h_idx, sel_blk]
        v_sel = v_blk[b_idx, h_idx, sel_blk]
        dist_sel = (t[:, None, None] - (sel_blk[..., None] * blk + offs)).astype(f32)
        s_sel = jnp.einsum('bhqd,bhqjkd->bhqjk', q_blk, k_sel).astype(f32) - slopes[:, None, None, None] * dist_sel
        slot_ok = jnp.arange(top)[None, :] < (t // blk)[:, None]
        s_sel = jnp.where(slot_ok[:, :, None], s_sel, -jnp.inf)
        scores = jnp.concatenate([s_own, s_sel.reshape(bsz, H, qlen, top * blk)], axis=-1)
        p = jax.nn.softmax(scores, axis=-1).astype(v_blk.dtype)
        p_own = p[..., :blk]
        p_sel = p[..., blk:].reshape(bsz, H, qlen, top, blk)
        return (jnp.einsum('bhqk,bhkd->bhqd', p_own, v_own)
                + jnp.einsum('bhqjk,bhqjkd->bhqd', p_sel, v_sel))

    o = lax.map(attend_chunk, (jnp.arange(n_chunk), q_c, sel_c))
    o = o.transpose(1, 0, 3, 2, 4).reshape(bsz, seq, H * dh)
    return o @ w_o

def mlstm_chunkwise(q, k, v, log_i, log_f):
    bsz, H, seq, dqk = q.shape
    dv = v.shape[-1]
    L = MLSTM_CHUNK
    n_chunk = seq // L

    def chunks(t):
        return jnp.moveaxis(t.reshape(bsz, H, n_chunk, L, *t.shape[3:]), 2, 0)

    causal = jnp.tril(jnp.ones((L, L), dtype=bool))

    def step(carry, inp):
        C, n, m = carry
        qc, kc, vc, ic, fc = inp
        b = jnp.cumsum(fc, axis=-1)
        log_d = jnp.where(causal, b[..., :, None] - b[..., None, :] + ic[..., None, :], -jnp.inf)
        log_inter = b + m[..., None]
        m_t = jnp.maximum(log_inter, jnp.max(log_d, axis=-1))
        d = jnp.exp(log_d - m_t[..., None])
        w_inter = jnp.exp(log_inter - m_t)
        s = jnp.einsum('bhtd,bhsd->bhts', qc, kc) * d
        num = (w_inter[..., None] * jnp.einsum('bhtd,bhdv->bhtv', qc, C)
               + jnp.einsum('bhts,bhsv->bhtv', s, vc))
        den = w_inter * jnp.einsum('bhtd,bhd->bht', qc, n) + jnp.sum(s, axis=-1)
        h = num / jnp.maximum(jnp.abs(den), jnp.exp(-m_t))[..., None]
        b_end = b[..., -1]
        log_w = b_end[..., None] - b + ic
        m_new = jnp.maximum(b_end + m, jnp.max(log_w, axis=-1))
        decay = jnp.exp(b_end + m - m_new)
        w = jnp.exp(log_w - m_new[..., None])
        C = decay[..., None, None] * C + jnp.einsum('bhs,bhsd,bhsv->bhdv', w, kc, vc)
        n = decay[..., None] * n + jnp.einsum('bhs,bhsd->bhd', w, kc)
        return (C, n, m_new), h

    f32 = jnp.float32
    init = (jnp.zeros((bsz, H, dqk, dv), f32), jnp.zeros((bsz, H, dqk), f32), jnp.zeros((bsz, H), f32))
    _, h = lax.scan(step, init, (chunks(q), chunks(k), chunks(v), chunks(log_i), chunks(log_f)))
    return jnp.moveaxis(h, 0, 2).reshape(bsz, H, seq, dv)

def mlstm_mixer(x, w_in, b_gates, norm_h, w_out):
    bsz, seq, _ = x.shape
    H, dqk, dv = MLSTM_HEADS, MLSTM_DQK, MLSTM_DV
    f32 = jnp.float32
    proj = x @ w_in
    q, k, v, o_pre, gate_pre = jnp.split(
        proj, [H * dqk, 2 * H * dqk, 2 * H * dqk + H * dv, 2 * H * dqk + 2 * H * dv], axis=-1)

    def to_heads(t, dim):
        return t.reshape(bsz, seq, H, dim).transpose(0, 2, 1, 3).astype(f32)

    q = to_heads(q, dqk)
    k = to_heads(k, dqk) * (dqk ** -0.5)
    v = to_heads(v, dv)
    gates = soft_cap(gate_pre.astype(f32) + b_gates.astype(f32)).transpose(0, 2, 1)
    log_i = gates[:, :H]
    log_f = jax.nn.log_sigmoid(gates[:, H:])
    h = mlstm_chunkwise(q, k, v, log_i, log_f)
    h = h * lax.rsqrt(jnp.mean(h * h, axis=-1, keepdims=True) + RMS_EPS)
    h = h.transpose(0, 2, 1, 3).reshape(bsz, seq, H * dv) * norm_h.astype(f32)
    y = (jax.nn.sigmoid(o_pre.astype(f32)) * h).astype(x.dtype)
    return y @ w_out

def squared_relu_mlp(x, w_up, w_down):
    return jnp.square(jax.nn.relu(x @ w_up)) @ w_down

def first_inputs(seed: int = 0) -> dict:
    key = jax.random.key(seed)
    ks = jax.random.split(key, 16)
    f32 = jnp.float32

    def dense(k, shape):
        return jax.random.normal(k, shape, f32) * shape[-2] ** -0.5

    def gain(k, shape):
        return 1.0 + 0.05 * jax.random.normal(k, shape, f32)

    H = MLSTM_HEADS
    mlstm_in = 2 * H * MLSTM_DQK + 2 * H * MLSTM_DV + 2 * H
    i_bias = 0.1 * jax.random.normal(ks[13], (N_MLSTM_LAYERS, H), f32)
    f_bias = 3.0 + 0.5 * jax.random.normal(ks[14], (N_MLSTM_LAYERS, H), f32)
    return {
        "x": jax.random.normal(ks[0], (BATCH, SEQ, D_MODEL), f32),
        "norm_mix_pre": gain(ks[1], (DEPTH, D_MODEL)),
        "norm_mix_post": gain(ks[2], (DEPTH, D_MODEL)),
        "norm_ffn_pre": gain(ks[3], (DEPTH, D_MODEL)),
        "norm_ffn_post": gain(ks[4], (DEPTH, D_MODEL)),
        "w_up": dense(ks[5], (DEPTH, D_MODEL, D_FF)),
        "w_down": dense(ks[6], (DEPTH, D_FF, D_MODEL)),
        "attn_w_qkv": dense(ks[7], (N_ATTN_LAYERS, D_MODEL, 3 * ATT_HEADS * ATT_HEAD_DIM)),
        "attn_w_o": dense(ks[8], (N_ATTN_LAYERS, ATT_HEADS * ATT_HEAD_DIM, D_MODEL)),
        "mlstm_w_in": dense(ks[9], (N_MLSTM_LAYERS, D_MODEL, mlstm_in)),
        "mlstm_b_gates": jnp.concatenate([i_bias, f_bias], axis=-1),
        "mlstm_norm_h": gain(ks[10], (N_MLSTM_LAYERS, H * MLSTM_DV)),
        "mlstm_w_out": dense(ks[11], (N_MLSTM_LAYERS, H * MLSTM_DV, D_MODEL)),
    }

def first_block(x, norm_mix_pre, norm_mix_post, norm_ffn_pre, norm_ffn_post, w_up, w_down,
              attn_w_qkv, attn_w_o, mlstm_w_in, mlstm_b_gates, mlstm_norm_h, mlstm_w_out):
    h = x
    for layer in range(DEPTH):
        j = layer // N_MIXERS
        u = rms_norm(h, norm_mix_pre[layer])
        if layer % N_MIXERS == 0:
            u = moba_attention(u, attn_w_qkv[j], attn_w_o[j])
        else:
            u = mlstm_mixer(u, mlstm_w_in[j], mlstm_b_gates[j], mlstm_norm_h[j], mlstm_w_out[j])
        h = h + rms_norm(u, norm_mix_post[layer])
        u = squared_relu_mlp(rms_norm(h, norm_ffn_pre[layer]), w_up[layer], w_down[layer])
        h = h + rms_norm(u, norm_ffn_post[layer])
    return h


DEPTH_2 = 2

N_A_LAYERS = DEPTH_2 // 2
N_B_LAYERS = DEPTH_2 - N_A_LAYERS
HGRN_EXPAND = 128
HGRN_HEADS = D_MODEL // HGRN_EXPAND
HGRN_DK = HGRN_EXPAND
HGRN_DV = D_MODEL // HGRN_HEADS
HGRN_D_KEY = HGRN_HEADS * HGRN_DK
HGRN_D_VAL = HGRN_HEADS * HGRN_DV
HGRN_CHUNK = 64
NSA_HEADS = 16
NSA_KV_HEADS = 4
NSA_GROUP = NSA_HEADS // NSA_KV_HEADS
NSA_HEAD_DIM = D_MODEL // NSA_HEADS
NSA_Q_WIDTH = NSA_HEADS * NSA_HEAD_DIM
N_BRANCH = 3
CMP_BLOCK = 32
CMP_STRIDE = 16
CMP_HIDDEN = 256
SEL_BLOCK = 64
N_SELECT = 16
WINDOW = 512
Q_BLOCK = 128
ROPE_THETA = 10000.0
FFN_HIDDEN = -(-8 * D_MODEL // (3 * 256)) * 256
EPS = 1e-6
NEG_INF = -1e30
FORCE_SCORE = 1e9


def rms_norm_2(x, gain):
    x32 = x.astype(jnp.float32)
    y = x32 * lax.rsqrt(jnp.mean(x32 * x32, axis=-1, keepdims=True) + EPS)
    return (y * gain.astype(jnp.float32)).astype(x.dtype)

def modulate(x, gain, shift, scale):
    return rms_norm_2(x, gain) * (1 + scale[:, None, :]) + shift[:, None, :]

def rope_tables(seq, dim):
    inv_freq = 1.0 / (ROPE_THETA ** (jnp.arange(0, dim, 2, dtype=jnp.float32) / dim))
    ang = jnp.arange(seq, dtype=jnp.float32)[:, None] * inv_freq[None, :]
    return jnp.cos(ang), jnp.sin(ang)

def apply_rope(x, cos, sin):
    x1, x2 = jnp.split(x, 2, axis=-1)
    cs = cos[None, :, None, :].astype(x.dtype)
    sn = sin[None, :, None, :].astype(x.dtype)
    return jnp.concatenate([x1 * cs - x2 * sn, x2 * cs + x1 * sn], axis=-1)

def masked_softmax(s, mask):
    p = jax.nn.softmax(jnp.where(mask, s.astype(jnp.float32), NEG_INF), axis=-1)
    return jnp.where(mask, p, 0.0)

def swiglu(h, w_in, w_out):
    a, b = jnp.split(h @ w_in, 2, axis=-1)
    return (jax.nn.silu(a) * b) @ w_out

def hgrn2_mixer(h, w_in, lower_bound, out_norm, w_out, first_layer):
    B, S, _ = h.shape
    q, f, i, g = jnp.split(h @ w_in, [HGRN_D_KEY, 2 * HGRN_D_KEY, 2 * HGRN_D_KEY + HGRN_D_VAL], axis=-1)
    q = jax.nn.silu(q)
    f32 = f.astype(jnp.float32)
    if first_layer:
        log_f = jax.nn.log_sigmoid(f32)
    else:
        lb = lower_bound.astype(jnp.float32)
        log_f = jnp.log(lb + (1.0 - lb) * jax.nn.sigmoid(f32))
    k = -jnp.expm1(log_f)
    nc = S // HGRN_CHUNK

    def to_chunks(t, d):
        return t.astype(jnp.float32).reshape(B, nc, HGRN_CHUNK, HGRN_HEADS, d).transpose(1, 0, 3, 2, 4)

    qc, kc, gc = to_chunks(q, HGRN_DK), to_chunks(k, HGRN_DK), to_chunks(log_f, HGRN_DK)
    vc = to_chunks(i, HGRN_DV)
    causal = jnp.tril(jnp.ones((HGRN_CHUNK, HGRN_CHUNK), dtype=bool))[:, :, None]

    def step(state, inp):
        q_, k_, v_, g_ = inp
        G = jnp.cumsum(g_, axis=2)
        o_inter = jnp.einsum('bhtk,bhkv->bhtv', q_ * jnp.exp(G), state)
        diff = G[:, :, :, None, :] - G[:, :, None, :, :]
        decay = jnp.where(causal, jnp.exp(jnp.where(causal, diff, 0.0)), 0.0)
        attn = jnp.einsum('bhtk,bhsk,bhtsk->bhts', q_, k_, decay)
        o_intra = jnp.einsum('bhts,bhsv->bhtv', attn, v_)
        G_last = G[:, :, -1:, :]
        new_state = jnp.exp(G_last[:, :, 0, :])[..., None] * state + jnp.einsum(
            'bhsk,bhsv->bhkv', k_ * jnp.exp(G_last - G), v_)
        return new_state, o_inter + o_intra

    s0 = jnp.zeros((B, HGRN_HEADS, HGRN_DK, HGRN_DV), jnp.float32)
    _, o = lax.scan(step, s0, (qc, kc, vc, gc))
    o = o.transpose(1, 0, 3, 2, 4).reshape(B, S, HGRN_HEADS, HGRN_DV)
    o = rms_norm_2(o, out_norm) * jax.nn.silu(g.reshape(B, S, HGRN_HEADS, HGRN_DV).astype(jnp.float32))
    return o.reshape(B, S, HGRN_D_VAL).astype(h.dtype) @ w_out

def nsa_shared_kv(h, w_kv, k_norm, cmp_pos, cmp_w1, cmp_w2, cos, sin):
    B, S, _ = h.shape
    kv = (h @ w_kv).reshape(B, S, 2 * N_BRANCH, NSA_KV_HEADS, NSA_HEAD_DIM)
    k_cmp, v_cmp, k_sel, v_sel, k_win, v_win = [kv[:, :, j] for j in range(2 * N_BRANCH)]
    n_sub = CMP_BLOCK // CMP_STRIDE
    n_cmp = S // CMP_STRIDE - n_sub + 1

    def compress(t, pos, w1, w2):
        r = t.reshape(B, S // CMP_STRIDE, CMP_STRIDE, NSA_KV_HEADS, NSA_HEAD_DIM)
        blocks = jnp.concatenate([r[:, j:j + n_cmp] for j in range(n_sub)], axis=2)
        blocks = blocks + pos[None, None, :, None, :]
        flat = blocks.transpose(0, 1, 3, 2, 4).reshape(B, n_cmp, NSA_KV_HEADS, CMP_BLOCK * NSA_HEAD_DIM)
        return jax.nn.silu(flat @ w1) @ w2

    kc = rms_norm_2(compress(k_cmp, cmp_pos[0], cmp_w1[0], cmp_w2[0]), k_norm[0])
    vc = compress(v_cmp, cmp_pos[1], cmp_w1[1], cmp_w2[1])
    n_sel = S // SEL_BLOCK
    ks = apply_rope(rms_norm_2(k_sel, k_norm[1]), cos, sin)
    ks_blocks = ks.reshape(B, n_sel, SEL_BLOCK, NSA_KV_HEADS, NSA_HEAD_DIM).transpose(0, 3, 1, 2, 4)
    vs_blocks = v_sel.reshape(B, n_sel, SEL_BLOCK, NSA_KV_HEADS, NSA_HEAD_DIM).transpose(0, 3, 1, 2, 4)
    kw = apply_rope(rms_norm_2(k_win, k_norm[2]), cos, sin)
    pad = ((0, 0), (WINDOW, 0), (0, 0), (0, 0))
    return (kc, vc, ks_blocks, vs_blocks, jnp.pad(kw, pad), jnp.pad(v_win, pad))

def nsa_mixer(h, w_q, q_norm, w_out, shared, cos, sin):
    B, S, _ = h.shape
    kc, vc, ks_blocks, vs_blocks, kw_pad, vw_pad = shared
    proj = h @ w_q
    q = rms_norm_2(proj[..., :NSA_Q_WIDTH].reshape(B, S, NSA_HEADS, NSA_HEAD_DIM), q_norm)
    gates = jax.nn.sigmoid(proj[..., NSA_Q_WIDTH:].astype(jnp.float32)).reshape(B, S, N_BRANCH, NSA_HEADS)
    q_rope = apply_rope(q, cos, sin)
    n_cmp = kc.shape[1]
    n_sel = ks_blocks.shape[2]
    n_top = min(N_SELECT, n_sel)
    cmp_end = jnp.arange(n_cmp) * CMP_STRIDE + CMP_BLOCK - 1
    sel_start = jnp.arange(n_sel) * SEL_BLOCK
    cs = np.arange(n_cmp) * CMP_STRIDE
    ss = np.arange(n_sel) * SEL_BLOCK
    overlap = jnp.asarray(((cs[:, None] < ss[None, :] + SEL_BLOCK) &
                           (cs[:, None] + CMP_BLOCK > ss[None, :])).astype(np.float32))
    scale = NSA_HEAD_DIM ** -0.5
    nb = S // Q_BLOCK
    bi = jnp.arange(B)[:, None, None, None]
    hi = jnp.arange(NSA_KV_HEADS)[None, :, None, None]
    blk_pos = jnp.arange(SEL_BLOCK)

    def blockify(t):
        return t.reshape(B, nb, Q_BLOCK, *t.shape[2:]).swapaxes(0, 1)

    def attend(args):
        blk, qp, qr, g = args
        t = blk * Q_BLOCK + jnp.arange(Q_BLOCK)
        qp = qp.reshape(B, Q_BLOCK, NSA_KV_HEADS, NSA_GROUP, NSA_HEAD_DIM)
        qr = qr.reshape(B, Q_BLOCK, NSA_KV_HEADS, NSA_GROUP, NSA_HEAD_DIM)
        s_c = jnp.einsum('bqhgd,bchd->bhgqc', qp, kc) * scale
        p_c = masked_softmax(s_c, cmp_end[None, :] <= t[:, None])
        o_c = jnp.einsum('bhgqc,bchd->bqhgd', p_c.astype(vc.dtype), vc)
        imp = jnp.einsum('bhgqc,cj->bhqj', p_c, overlap)
        cur = t // SEL_BLOCK
        j = jnp.arange(n_sel)[None, :]
        forced = (j == 0) | (j == cur[:, None]) | (j == cur[:, None] - 1)
        valid_blk = sel_start[None, :] <= t[:, None]
        imp = jnp.where(forced & valid_blk, FORCE_SCORE, jnp.where(valid_blk, imp, -1.0))
        top_val, top_idx = lax.top_k(imp, n_top)
        ks_g = ks_blocks[bi, hi, top_idx].reshape(B, NSA_KV_HEADS, Q_BLOCK, n_top * SEL_BLOCK, NSA_HEAD_DIM)
        vs_g = vs_blocks[bi, hi, top_idx].reshape(B, NSA_KV_HEADS, Q_BLOCK, n_top * SEL_BLOCK, NSA_HEAD_DIM)
        kpos = (top_idx[..., None] * SEL_BLOCK + blk_pos).reshape(B, NSA_KV_HEADS, Q_BLOCK, n_top * SEL_BLOCK)
        m_s = jnp.repeat(top_val >= 0, SEL_BLOCK, axis=-1) & (kpos <= t[None, None, :, None])
        s_s = jnp.einsum('bqhgd,bhqkd->bhgqk', qr, ks_g) * scale
        p_s = masked_softmax(s_s, m_s[:, :, None])
        o_s = jnp.einsum('bhgqk,bhqkd->bqhgd', p_s.astype(vs_g.dtype), vs_g)
        kw = lax.dynamic_slice_in_dim(kw_pad, blk * Q_BLOCK, Q_BLOCK + WINDOW, axis=1)
        vw = lax.dynamic_slice_in_dim(vw_pad, blk * Q_BLOCK, Q_BLOCK + WINDOW, axis=1)
        kpos_w = blk * Q_BLOCK - WINDOW + jnp.arange(Q_BLOCK + WINDOW)
        m_w = ((kpos_w[None, :] <= t[:, None]) & (kpos_w[None, :] > t[:, None] - WINDOW)
               & (kpos_w[None, :] >= 0))
        s_w = jnp.einsum('bqhgd,bkhd->bhgqk', qr, kw) * scale
        p_w = masked_softmax(s_w, m_w)
        o_w = jnp.einsum('bhgqk,bkhd->bqhgd', p_w.astype(vw.dtype), vw)
        g = g.reshape(B, Q_BLOCK, N_BRANCH, NSA_KV_HEADS, NSA_GROUP)[..., None]
        o = g[:, :, 0] * o_c + g[:, :, 1] * o_s + g[:, :, 2] * o_w
        return o.reshape(B, Q_BLOCK, NSA_Q_WIDTH).astype(h.dtype)

    out = lax.map(attend, (jnp.arange(nb), blockify(q), blockify(q_rope), blockify(gates)))
    return out.swapaxes(0, 1).reshape(B, S, NSA_Q_WIDTH) @ w_out

def second_inputs(seed: int = 0) -> dict:
    key = jax.random.key(seed)
    ks = jax.random.split(key, 24)
    D = D_MODEL

    def nrm(k, shape, scale):
        return jax.random.normal(k, shape, jnp.float32) * scale

    def gain(k, shape):
        return 1.0 + nrm(k, shape, 0.02)

    return {
        'x': nrm(ks[0], (BATCH, SEQ, D), 1.0),
        'c': nrm(ks[1], (BATCH, D), 1.0),
        'ada_w': nrm(ks[2], (2 * DEPTH_2, D, 3 * D), 0.5 * D ** -0.5),
        'ada_b': nrm(ks[3], (2 * DEPTH_2, 3 * D), 0.02),
        'norm_mix': gain(ks[4], (DEPTH_2, D)),
        'norm_ffn': gain(ks[5], (DEPTH_2, D)),
        'hgrn_w_in': nrm(ks[6], (N_A_LAYERS, D, 2 * HGRN_D_KEY + 2 * HGRN_D_VAL), D ** -0.5),
        'hgrn_lower_bounds': nrm(ks[7], (N_A_LAYERS, HGRN_D_KEY), 0.5),
        'hgrn_out_norm': gain(ks[8], (N_A_LAYERS, HGRN_DV)),
        'hgrn_w_out': nrm(ks[9], (N_A_LAYERS, HGRN_D_VAL, D), HGRN_D_VAL ** -0.5),
        'kv_ada_w': nrm(ks[10], (D, 2 * D), 0.5 * D ** -0.5),
        'kv_ada_b': nrm(ks[11], (2 * D,), 0.02),
        'kv_norm': gain(ks[12], (D,)),
        'nsa_w_kv': nrm(ks[13], (D, 2 * N_BRANCH * NSA_KV_HEADS * NSA_HEAD_DIM), D ** -0.5),
        'nsa_k_norm': gain(ks[14], (N_BRANCH, NSA_HEAD_DIM)),
        'cmp_pos': nrm(ks[15], (2, CMP_BLOCK, NSA_HEAD_DIM), 0.1),
        'cmp_w1': nrm(ks[16], (2, CMP_BLOCK * NSA_HEAD_DIM, CMP_HIDDEN), (CMP_BLOCK * NSA_HEAD_DIM) ** -0.5),
        'cmp_w2': nrm(ks[17], (2, CMP_HIDDEN, NSA_HEAD_DIM), CMP_HIDDEN ** -0.5),
        'nsa_w_q': nrm(ks[18], (N_B_LAYERS, D, NSA_Q_WIDTH + N_BRANCH * NSA_HEADS), D ** -0.5),
        'nsa_q_norm': gain(ks[19], (N_B_LAYERS, NSA_HEAD_DIM)),
        'nsa_w_out': nrm(ks[20], (N_B_LAYERS, NSA_Q_WIDTH, D), NSA_Q_WIDTH ** -0.5),
        'ffn_w_in': nrm(ks[21], (DEPTH_2, D, 2 * FFN_HIDDEN), D ** -0.5),
        'ffn_w_out': nrm(ks[22], (DEPTH_2, FFN_HIDDEN, D), FFN_HIDDEN ** -0.5),
    }

def second_block(x, c, ada_w, ada_b, norm_mix, norm_ffn, hgrn_w_in, hgrn_lower_bounds, hgrn_out_norm,
              hgrn_w_out, kv_ada_w, kv_ada_b, kv_norm, nsa_w_kv, nsa_k_norm, cmp_pos, cmp_w1, cmp_w2,
              nsa_w_q, nsa_q_norm, nsa_w_out, ffn_w_in, ffn_w_out):
    B, S, _ = x.shape
    cos, sin = rope_tables(S, NSA_HEAD_DIM)
    c_act = jax.nn.silu(c)
    mods = jnp.einsum('bd,lde->lbe', c_act, ada_w) + ada_b[:, None, :]
    lb = jax.nn.softmax(hgrn_lower_bounds.astype(jnp.float32), axis=0)
    lb = jnp.cumsum(lb, axis=0) - lb[0]
    shared = None
    for layer in range(DEPTH_2):
        shift, scale, gate = jnp.split(mods[2 * layer], 3, axis=-1)
        h = modulate(x, norm_mix[layer], shift, scale)
        if layer < N_A_LAYERS:
            y = hgrn2_mixer(h, hgrn_w_in[layer], lb[layer], hgrn_out_norm[layer], hgrn_w_out[layer], layer == 0)
        else:
            if layer == N_A_LAYERS:
                kv_shift, kv_scale = jnp.split(c_act @ kv_ada_w + kv_ada_b, 2, axis=-1)
                shared = nsa_shared_kv(modulate(x, kv_norm, kv_shift, kv_scale), nsa_w_kv, nsa_k_norm,
                                       cmp_pos, cmp_w1, cmp_w2, cos, sin)
            bl = layer - N_A_LAYERS
            y = nsa_mixer(h, nsa_w_q[bl], nsa_q_norm[bl], nsa_w_out[bl], shared, cos, sin)
        x = x + gate[:, None, :] * y
        shift, scale, gate = jnp.split(mods[2 * layer + 1], 3, axis=-1)
        h = modulate(x, norm_ffn[layer], shift, scale)
        x = x + gate[:, None, :] * swiglu(h, ffn_w_in[layer], ffn_w_out[layer])
    return x


def setup_inputs(seed=0):
    out = dict(first_inputs(seed))
    for name, value in second_inputs(seed + 1).items():
        if name != "x":
            out[name + "_2"] = value
    return out


def reference(
    x, norm_mix_pre, norm_mix_post, norm_ffn_pre, norm_ffn_post, w_up, w_down, attn_w_qkv,
    attn_w_o, mlstm_w_in, mlstm_b_gates, mlstm_norm_h, mlstm_w_out, c_2, ada_w_2, ada_b_2,
    norm_mix_2, norm_ffn_2, hgrn_w_in_2, hgrn_lower_bounds_2, hgrn_out_norm_2, hgrn_w_out_2,
    kv_ada_w_2, kv_ada_b_2, kv_norm_2, nsa_w_kv_2, nsa_k_norm_2, cmp_pos_2, cmp_w1_2, cmp_w2_2,
    nsa_w_q_2, nsa_q_norm_2, nsa_w_out_2, ffn_w_in_2, ffn_w_out_2,
):
    x = first_block(
        x, norm_mix_pre, norm_mix_post, norm_ffn_pre, norm_ffn_post, w_up, w_down, attn_w_qkv,
        attn_w_o, mlstm_w_in, mlstm_b_gates, mlstm_norm_h, mlstm_w_out,
    )
    return second_block(
        x, c_2, ada_w_2, ada_b_2, norm_mix_2, norm_ffn_2, hgrn_w_in_2, hgrn_lower_bounds_2,
        hgrn_out_norm_2, hgrn_w_out_2, kv_ada_w_2, kv_ada_b_2, kv_norm_2, nsa_w_kv_2,
        nsa_k_norm_2, cmp_pos_2, cmp_w1_2, cmp_w2_2, nsa_w_q_2, nsa_q_norm_2, nsa_w_out_2,
        ffn_w_in_2, ffn_w_out_2,
    )


_drawn_inputs = setup_inputs


def setup_inputs(seed=0):
    import zlib

    import numpy as np

    out = dict(_drawn_inputs(seed))
    spreads = {}
    factors = {'ada_b_2': 3.36,
     'norm_mix_2': 8.0,
     'norm_ffn_2': 8.0,
     'hgrn_out_norm_2': 8.0,
     'kv_ada_b_2': 8.0,
     'kv_norm_2': 28.311,
     'nsa_k_norm_2': 28.271,
     'cmp_pos_2': 34.426,
     'nsa_q_norm_2': 28.24}
    for name, (base, spread) in spreads.items():
        noise = np.random.default_rng([zlib.crc32(name.encode()), seed]).standard_normal(out[name].shape)
        drawn = base * np.exp(spread * noise) if base else spread * noise
        out[name] = __import__('jax').numpy.asarray(drawn.astype(out[name].dtype))
    for name, factor in factors.items():
        out[name] = (out[name] * factor).astype(out[name].dtype)
    return out
```

```python
from contextlib import ExitStack

import numpy as np
import concourse.bass as bass
from concourse import mybir

F32 = mybir.dt.float32
F32R = mybir.dt.float32r
ALU = mybir.AluOpType
ACT = mybir.ActivationFunctionType
AX = mybir.AxisListType.X

P = 128
T = 256
TT = T // P
D = 1024
KD = D // P
H1, DH1 = 8, 128
FF1 = 4 * D
HH, DK = 8, 128
LEVELS = [64, 32, 16, 8, 4, 2, 1]
NL = len(LEVELS)
NH, NKV, NG, DN = 16, 4, 4, 64
FFN = -(-8 * D // (3 * 256)) * 256
CB, CS = 32, 16
NCMP = T // CS - CB // CS + 1
CHID = 256
EPS = 1e-6
NEG = -1e30

N_QKV, N_ACC, N_FF1, N_HIN, N_FF2, N_KV, N_Q = 3, 1, FF1 // 512, 4, FFN // 256, 2, 1
Q_QKV = 0
Q_WO = Q_QKV + N_QKV
Q_FF1 = Q_WO + N_ACC
Q_HIN = Q_FF1 + N_FF1
Q_HOUT = Q_HIN + N_HIN
Q_F2A = Q_HOUT + N_ACC
Q_KV = Q_F2A + N_FF2
Q_NQ = Q_KV + N_KV
Q_CMP = Q_NQ + N_Q
Q_NOUT = Q_CMP + 1
Q_F2B = Q_NOUT + N_ACC
Q_END = Q_F2B + N_FF2

G_HIN = 2 * N_QKV
G_KV = G_HIN + 2 * N_HIN
G_Q = G_KV + 2 * N_KV
G_END = G_Q + 2 * N_Q
U_F2A = N_FF1
U_F2B = U_F2A + N_FF2
HT_F2A = 2 * N_FF1
HT_F2B = HT_F2A + N_FF2

M_L0, M_L1, M_L2, M_KV, M_L3, M_END = 0, 6, 12, 18, 22, 28
LCOL = {0: 4 * M_L0, 1: 4 * M_L1, 2: 4 * M_L2, "kv": 4 * M_KV, 3: 4 * M_L3}

VR = {"mix_pre": 0, "ffn_pre": 8, "mix2": 16, "ffn2": 32, "kvn": 48, "c": 56, "pos": 64}


def constants():
    t = np.arange(P)
    ident = np.eye(P, dtype=np.float32)
    q, k = t[:, None], t[None, :]
    dist = np.concatenate([np.where(k <= q, k - q, NEG), k - (q + P) + 0 * q, np.where(k <= q, k - q, NEG)], 1)
    caus = np.concatenate([np.where(k <= q, 0, NEG), 0.0 * (k + q), np.where(k <= q, 0, NEG)], 1)
    ml = np.zeros((P, NL + 2, P), np.float32)
    mask = np.zeros((P, NL + 1, P), np.float32)
    u, x = t[:, None], t[None, :]
    for i, m in enumerate(LEVELS):
        mid = x // (2 * m) * (2 * m) + m
        second = x >= mid
        ml[:, i] = np.where(second, (u >= mid) & (u <= x), (u > x) & (u < mid))
        mask[:, i] = (u // (2 * m) == x // (2 * m)) & (u < mid) & (x >= mid)
    mask[:, NL] = ident
    ml[:, NL] = u > x
    ml[:, NL + 1] = u <= x
    inv = 1.0 / (10000.0 ** (np.arange(0, DN, 2, dtype=np.float32) / np.float32(DN)))
    ang = np.arange(T, dtype=np.float32)[:, None] * inv[None, :].astype(np.float32)
    rope = np.stack([np.cos(ang), np.sin(ang)], 1).astype(np.float32)
    rope = rope.reshape(TT, P, 2 * (DN // 2)).transpose(1, 0, 2).reshape(P, -1)
    tok = np.arange(T).reshape(TT, P).T
    seen = (np.arange(NCMP) * CS + CB - 1)[None, None, :] <= tok[:, :, None]
    cmask = np.stack([np.where(seen, 0.0, NEG), seen.astype(np.float64)], 1).reshape(P, -1)
    selv = np.zeros((P, 2, 8, 16), np.float32)
    for c in range(NCMP):
        for h in range(NKV):
            for hq in range(NH):
                if hq // NG == h:
                    selv[c * NKV + h, hq // 8, hq % 8, c] = 1
    bm = (t[:, None] // 16 == np.arange(8)[None, :]).astype(np.float32)
    f = lambda a: np.ascontiguousarray(a.reshape(P, -1), dtype=np.float32)
    return {
        "k_small": f(np.concatenate([ident, caus, rope, cmask, bm, selv.reshape(P, -1)], 1)),
        "k_dist": f(dist),
        "k_levels": f(np.concatenate([ml.reshape(P, -1), mask.reshape(P, -1)], 1)),
    }


SMALL = {}
_o = 0
for _n, _w in (("ident", P), ("caus", 384), ("rope", TT * DN), ("cmask", 2 * TT * NCMP), ("bm", 8), ("selv", 256)):
    SMALL[_n] = (_o, _o + _w)
    _o += _w
SMALL_W = _o
LEV_W = (NL + 2) * P + (NL + 1) * P


def build(nc, a, out):
    with ExitStack() as ctx:
        def sb(name, shape, dt=F32):
            return ctx.enter_context(nc.sbuf_tensor(name, shape, dt))

        def sem(name):
            return ctx.enter_context(nc.semaphore(name))

        raw = sb("raw", [P, 4, 2048])
        whi = sb("whi", [P, 4, 2048], F32R)
        wlo = sb("wlo", [P, 4, 2048], F32R)
        adaw = sb("adaw", [P, 2, 2048])
        adaacc = sb("adaacc", [P, 512])
        xhi = sb("xhi", [P, KD, T], F32R)
        xlo = sb("xlo", [P, KD, T], F32R)
        hhi = sb("hhi", [P, 4, T], F32R)
        hlo = sb("hlo", [P, 4, T], F32R)
        res = sb("res", [P, TT, D])
        gain_b = sb("gain_b", [P, D])
        small = sb("small", [P, SMALL_W])
        vcol = sb("vcol", [P, 96])
        bcol = sb("bcol", [P, 4 * M_END])
        adacol = sb("adacol", [P, 4 * M_END])
        gs = sb("gs", [P, KD])
        sh = sb("sh", [P, KD])
        cact = sb("cact", [P, KD])
        ones = sb("ones", [P, 1])
        stat = sb("stat", [P, 64])
        ss = stat[:, 0:2]
        rstd = stat[:, 2:4]
        mhalf = stat[:, 4:36]
        onb = sb("onb", [P, DK])
        zrow = sb("zrow", [1, 512], mybir.dt.bfloat16)
        AR = 16592
        arena = sb("arena", [P, AR])
        psum = ctx.enter_context(nc.psum_tensor("psum", [P, 8, 512], F32))

        def cst(name):
            lo, hi_ = SMALL[name]
            return small[:, lo:hi_]
        ident = cst("ident")

        def area(lo, *shape):
            n = int(np.prod(shape))
            v = arena[:, lo:lo + n]
            if len(shape) == 1:
                return v
            names = "abcde"[:len(shape)]
            return v.rearrange(f"p ({' '.join(names)}) -> p {' '.join(names)}", **{k: s for k, s in zip(names, shape)})

        y = area(AR - 4096, TT, D)
        xf = area(AR - 2048, KD, T)
        vrow1 = area(11600, P)
        vrow2 = area(11728, P)
        dist = area(11860, 384)
        qkv = area(0, TT, 3 * D)
        qkT = area(6144, 2, 512)
        sc1 = area(7168, 2, 384)
        pb1 = area(7936, 2, 384)
        pT1 = area(8704, 2, 384)
        ob1 = area(9472, TT, D)
        st1 = area(11520, 2, 8)
        relu = area(0, TT, 512)
        sq = area(1024, 4, T)
        sil = area(2048, TT, T)
        gat = area(2560, TT, T)
        hin = area(0, 4, TT, D)
        hk = area(8192, TT, D)
        lev = area(10240, LEV_W)
        ML = lev[:, 0:(NL + 2) * P].rearrange("p (l t) -> p l t", t=P)
        MK = lev[:, (NL + 2) * P:LEV_W].rearrange("p (l t) -> p l t", t=P)
        ee = area(12416, NL + 1, P)
        qe = area(13440, NL + 1, P)
        pm = area(14464, NL + 1, P)
        qkTh = area(15488, 2, T)
        am = area(16000, 3, P)
        ke7 = area(16384, P)
        hs = area(16512, 64)
        kv = area(0, TT, 6, NKV, DN)
        nq = area(3072, TT, NH, DN)
        nqT = area(5120, 8, T)
        nkT = area(7168, 2, NKV, T)
        nqrT = area(9216, 8, T)
        nt1 = area(11264, 2048)
        kt2 = area(11264, 2, NKV, P)
        fl = area(5120, 2, CB // 2, NCMP, NKV)
        pT2 = area(5120, 2, 384)
        nqr = area(9216, TT, NH, DN)
        nkd = area(9216, TT, 2, NKV, 2, DN)
        hid = area(13312, 2, 2, NCMP * NKV)
        kcv = area(13552, 2, DN)
        kcd = area(13680, 2, DN)
        kcT = area(13808, NCMP * NKV)
        vbd = area(13872, 2, 8, DN)
        w2s = area(14896, 2, 2, DN)
        wgs = area(15152, KD, 48)
        gat3 = area(15536, TT, 48)
        knb = area(15632, 4, DN)
        nst = area(15888, 192)
        pc = area(11264, TT, NH, 16)
        sc2 = area(11776, 2, 384)
        pb2 = area(12544, 2, 384)
        pcT = area(16080, 4, P)
        ob2 = area(3072, TT, NH, DN)

        raw_full = [sem(f"raw_full{s}") for s in range(4)]
        hi_ready = [sem(f"hi_ready{s}") for s in range(4)]
        lo_ready = [sem(f"lo_ready{s}") for s in range(4)]
        used = [sem(f"used{s}") for s in range(4)]
        ada_full = [sem(f"ada_full{s}") for s in range(2)]
        ada_used = [sem(f"ada_used{s}") for s in range(2)]
        ada_step, ada_sum, ada_turned, ada_saved = sem("ada_step"), sem("ada_sum"), sem("ada_turned"), sem("ada_saved")
        consts_in, x_in, vec_in = sem("consts_in"), sem("x_in"), sem("vec_in")
        vec_turned, vec_saved, c_ready, ones_set = sem("vec_turned"), sem("vec_saved"), sem("c_ready"), sem("ones_set")
        gain_in, gain_free = sem("gain_in"), sem("gain_free")
        n_sq, n_ms, n_rstd, n_y, n_turned, n_affine, n_hi, n_x = [sem("n_" + s) for s in ("sq", "ms", "rstd", "y", "turned", "affine", "hi", "x")]
        aff_ready = sem("aff_ready")
        p_sq, p_ms, p_rstd, p_res = [sem("p_" + s) for s in ("sq", "ms", "rstd", "res")]
        proj_done, evac_a, evac_d = sem("proj_done"), sem("evac_a"), sem("evac_d")
        acc_done = sem("acc_done")
        up_done, act_done, gate_done, h_turned, h_sq, h_hi, h_lo = [sem(s) for s in ("up_done", "act_done", "gate_done", "h_turned", "h_sq", "h_hi", "h_lo")]
        bg_turned, bg_saved = sem("bg_turned"), sem("bg_saved")
        a_qk, a_qks, a_s, a_m, a_e, a_pt, a_pts, a_o, a_os = [sem("a_" + s) for s in ("qk", "qks", "s", "m", "e", "pt", "pts", "o", "os")]
        t_turned, t_hi, t_x = sem("t_turned"), sem("t_hi"), sem("t_x")
        lev_in, onb_in, dist_in = sem("lev_in"), sem("onb_in"), sem("dist_in")
        g_a, g_d, g_f = sem("g_a"), sem("g_d"), sem("g_f")
        r_qk, r_qks, r_e, r_ee, r_z, r_s, r_am, r_o, r_os = [sem("r_" + s) for s in ("qk", "qks", "e", "ee", "z", "s", "am", "o", "os")]
        r_ms, r_rs = sem("r_ms"), sem("r_rs")
        nsa_in = sem("nsa_in")
        dve, actc, poolc = sem("dve_chain"), sem("act_chain"), sem("pool_chain")
        k_ = {n: sem("k_" + n) for n in ("even", "evens", "flat", "hid", "hids", "kc", "kcs", "sq", "rs", "kcd", "kct", "kcts",
                                         "vb", "vbs", "krope", "kT", "kTs", "g", "gs", "qsq", "qrs", "qn", "qT", "qTs", "qr", "qrT", "qrTs",
                                         "cs", "cm", "ce", "cp", "cT", "cTs", "co", "cos")}
        w_s, w_m, w_e, w_pt, w_pts, w_o, w_os = [sem("w_" + s) for s in ("s", "m", "e", "pt", "pts", "o", "os")]
        out_done = sem("out_done")

        def wait(eng, s, v):
            if not isinstance(v, int) or v > 0:
                eng.wait_ge(s, v)

        class Chain:
            def __init__(self, eng, s):
                self.eng, self.s, self.n = eng, s, 0

            def __call__(self, ins):
                self.n += 1
                ins.then_inc(self.s, 1)
                self.eng.wait_ge(self.s, self.n)

        block = ctx.enter_context(nc.Block())

        @block.sync
        def _(sp):
            def free_slot(s, n):
                if isinstance(n, int) and n == Q_CMP + 1:
                    sp.wait_ge(used[s], n)
                elif not isinstance(n, int) or n > 0:
                    wait(sp, hi_ready[s], n)
                    wait(sp, lo_ready[s], n)

            def wide(w, s, n, nb, width=512):
                free_slot(s, n)
                v = w.rearrange("(h kt p) n -> h p kt n", h=2, p=P)[s % 2]
                dst = raw[:, s, 0:4 * width].rearrange("p (k n) -> p k n", k=4)
                sp.dma_start(dst, v[:, :, bass.ds(nb * width, width)]).then_inc(raw_full[s], 32)

            def deep(w, s, n, g, kt=2):
                free_slot(s, n)
                v = w.rearrange("(r p) n -> p r n", p=P)
                dst = raw[:, s, 0:kt * D].rearrange("p (k n) -> p k n", k=kt)
                sp.dma_start(dst, v[:, bass.ds(g * kt, kt), :]).then_inc(raw_full[s], 32)

            def gated(w, s, n, fb):
                free_slot(s, n)
                v = w.rearrange("(h kt p) n -> h p kt n", h=2, p=P)[s % 2]
                dst = raw[:, s, :].rearrange("p (k n) -> p k n", k=4)
                sp.dma_start(dst[:, :, 0:256], v[:, :, bass.ds(fb * 256, 256)]).then_inc(raw_full[s], 16)
                sp.dma_start(dst[:, :, 256:512], v[:, :, bass.ds(fb * 256 + FFN, 256)]).then_inc(raw_full[s], 16)

            def ada(w, half, m, nb):
                if not isinstance(m, int) or m > 0:
                    sp.wait_ge(ada_used[half], m)
                v = w.rearrange("(h kt p) n -> h p kt n", h=2, p=P)[half]
                dst = adaw[:, half, :].rearrange("p (k n) -> p k n", k=4)
                sp.dma_start(dst, v[:, :, bass.ds(nb * 512, 512)]).then_inc(ada_full[half], 16)

            sp.dma_start(res[:], a["x"][0].rearrange("(i p) d -> p i d", p=P)).then_inc(x_in, 16)
            sp.dma_start(small[:], a["k_small"]).then_inc(consts_in, 16)
            sp.dma_start(dist, a["k_dist"]).then_inc(dist_in, 16)
            w = a["attn_w_qkv"][0]
            for s in range(4):
                wide(w, s, 0, s // 2)
            with sp.Fori(1, N_QKV) as t:
                for s in range(4):
                    wide(w, s, t + Q_QKV, 2 * t + s // 2)
            for s in range(4):
                deep(a["attn_w_o"][0], s, Q_WO, s)
            up, dn = a["w_up"][0], a["w_down"][0]
            for s in (0, 1):
                wide(up, s, Q_FF1, 0)

            def mlp1(t, l, m, nb):
                wide(up, 0, t + Q_FF1 + 1, t + 1)
                ada(a["ada_w_2"][l], 0, m, nb)
                wide(up, 1, t + Q_FF1 + 1, t + 1)
                deep(dn, 2, t + Q_FF1, 2 * t)
                ada(a["ada_w_2"][l], 1, m, nb)
                deep(dn, 3, t + Q_FF1, 2 * t + 1)
            mlp1(0, 0, 0, 0)
            with sp.Fori(1, 6) as t:
                mlp1(t, 0, t, t)
            mlp1(6, 1, 6, 0)
            deep(dn, 2, Q_FF1 + 7, 14)
            ada(a["ada_w_2"][1], 0, 7, 1)
            deep(dn, 3, Q_FF1 + 7, 15)
            ada(a["ada_w_2"][1], 1, 7, 1)
            w = a["hgrn_w_in_2"][0]
            for t, sec in enumerate((1, 0, 2, 3)):
                for s in range(4):
                    wide(w, s, Q_HIN + t, 2 * sec + s // 2)
                    if s % 2:
                        ada(a["ada_w_2"][1], s // 2, M_L1 + 2 + t, 2 + t)
            for s in range(4):
                deep(a["hgrn_w_out_2"][0], s, Q_HOUT, s)

            def mlp2(layer, q0, t, ada_a=None, last=False):
                up2, dn2 = a["ffn_w_in_2"][layer], a["ffn_w_out_2"][layer]
                if not last:
                    gated(up2, 0, t + q0 + 1, t + 1)
                if ada_a:
                    ada(ada_a[0], 0, ada_a[1], ada_a[2])
                if not last:
                    gated(up2, 1, t + q0 + 1, t + 1)
                deep(dn2, 2, t + q0, 2 * t, kt=1)
                if ada_a:
                    ada(ada_a[0], 1, ada_a[1], ada_a[2])
                deep(dn2, 3, t + q0, 2 * t + 1, kt=1)

            gated(a["ffn_w_in_2"][0], 0, Q_F2A, 0)
            gated(a["ffn_w_in_2"][0], 1, Q_F2A, 0)
            with sp.Fori(0, 6) as t:
                mlp2(0, Q_F2A, t, (a["ada_w_2"][2], t + M_L2, t))
            with sp.Fori(6, 10) as t:
                mlp2(0, Q_F2A, t, (a["kv_ada_w_2"], t + M_L2, t - 6))
            mlp2(0, Q_F2A, 10, (a["ada_w_2"][3], M_L3, 0), last=True)
            w = a["nsa_w_kv_2"]
            for s in range(4):
                wide(w, s, Q_KV, s // 2, 384)
            ada(a["ada_w_2"][3], 0, M_L3 + 1, 1)
            ada(a["ada_w_2"][3], 1, M_L3 + 1, 1)
            for s in range(4):
                wide(w, s, Q_KV + 1, 2 + s // 2, 384)
            ada(a["ada_w_2"][3], 0, M_L3 + 2, 2)
            ada(a["ada_w_2"][3], 1, M_L3 + 2, 2)
            for s in range(4):
                wide(a["nsa_w_q_2"][0], s, Q_NQ, s // 2)
            for s in range(4):
                free_slot(s, Q_CMP)
                sp.dma_start(raw[:, s, :].rearrange("p (k n) -> p k n", k=8),
                             a["cmp_w1_2"][s // 2].rearrange("(g k p) n -> g p k n", g=2, p=P)[s % 2]).then_inc(raw_full[s], 32)
            ada(a["ada_w_2"][3], 0, M_L3 + 3, 3)
            ada(a["ada_w_2"][3], 1, M_L3 + 3, 3)
            for s in range(4):
                deep(a["nsa_w_out_2"][0], s, Q_NOUT, s)
            for b in (4, 5):
                ada(a["ada_w_2"][3], 0, M_L3 + b, b)
                ada(a["ada_w_2"][3], 1, M_L3 + b, b)
            gated(a["ffn_w_in_2"][1], 0, Q_F2B, 0)
            gated(a["ffn_w_in_2"][1], 1, Q_F2B, 0)
            with sp.Fori(0, 10) as t:
                mlp2(1, Q_F2B, t)
            mlp2(1, Q_F2B, 10, last=True)
            for i in range(TT):
                sp.wait_ge(p_res, 11 + i)
                sp.dma_start(out[0].rearrange("(i p) d -> p i d", p=P)[:, i, :], res[:, i, :]).then_inc(out_done, 16)
            sp.wait_ge(out_done, 32)

        @block.gpsimd
        def _(pool):
            gp = nc.gpsimd
            chain = Chain(pool, poolc)
            gp.memset(mhalf, -0.5)
            gp.memset(zrow[:], 0.0)
            chain(gp.memset(ones[:], 1.0))
            pool.nop().then_inc(ones_set, 1)
            for name, src in (("mix_pre", a["norm_mix_pre"]), ("ffn_pre", a["norm_ffn_pre"]), ("mix2", a["norm_mix_2"]),
                              ("ffn2", a["norm_ffn_2"]), ("c", a["c_2"])):
                r = src.rearrange("l (k p) -> (l k) p", p=P)
                gp.dma_start(vrow1[VR[name]:VR[name] + r.shape[0], :], r).then_inc(vec_in, 16)
            gp.dma_start(vrow1[VR["kvn"]:VR["kvn"] + 8, :], a["kv_norm_2"].rearrange("(k p) -> k p", p=P)).then_inc(vec_in, 16)
            gp.dma_start(vrow1[VR["pos"]:VR["pos"] + 32, :],
                         a["cmp_pos_2"].rearrange("j (a r) d -> (j a) (r d)", r=2)).then_inc(vec_in, 16)
            gp.dma_start(vrow2[0:72, :], a["ada_b_2"][0:3].rearrange("l (k p) -> (l k) p", p=P)).then_inc(vec_in, 16)
            gp.dma_start(vrow2[72:88, :], a["kv_ada_b_2"].rearrange("(k p) -> k p", p=P)).then_inc(vec_in, 16)
            gp.dma_start(vrow2[88:112, :], a["ada_b_2"][3:4].rearrange("l (k p) -> (l k) p", p=P)).then_inc(vec_in, 16)
            gp.dma_start(onb[:], a["hgrn_out_norm_2"][0].partition_broadcast(P)).then_inc(onb_in, 16)
            gp.dma_start(gain_b[:], a["norm_mix_post"][0].partition_broadcast(P)).then_inc(gain_in, 16)

            def rsqrt(src, dst, tmp, n, mean, done):
                chain(gp.tensor_scalar(tmp, src, mean, EPS, ALU.mult, ALU.add))
                gp.tensor_tensor(dst, tmp, n, ALU.pow).then_inc(done, 1)

            def norm(j):
                pool.wait_ge(n_sq, 2 * j + 2)
                rsqrt(ss, rstd, stat[:, 40:42], mhalf[:, 0:2], 1.0 / D, n_rstd)

            def post(k):
                pool.wait_ge(p_sq, 2 * k + 2)
                rsqrt(stat[:, 36:38], stat[:, 38:40], stat[:, 42:44], mhalf[:, 0:2], 1.0 / D, p_rstd)

            norm(0)
            post(0)
            pool.wait_ge(p_res, 2)
            gp.dma_start(gain_b[:], a["norm_ffn_post"][0].partition_broadcast(P)).then_inc(gain_in, 16)
            norm(1)
            post(1)
            pool.wait_ge(p_res, 4)
            gp.dma_start(lev, a["k_levels"]).then_inc(lev_in, 16)
            norm(2)
            pool.wait_ge(r_ms, 1)
            rsqrt(hs[:, 0:16], hs[:, 16:32], hs[:, 32:48], mhalf[:, 0:16], 1.0 / DK, r_rs)
            norm(3)
            norm(4)
            pool.wait_ge(n_x, 24)
            pool.wait_ge(n_turned, 24)
            with nc.allow_non_contiguous_dma(reason="small operands"):
                gp.dma_start(w2s, a["cmp_w2_2"].rearrange("j (h p) d -> p j h d", p=P)).then_inc(nsa_in, 16)
                gp.dma_start(wgs, a["nsa_w_q_2"][0].rearrange("(k p) n -> p k n", p=P)[:, :, D:D + 48]).then_inc(nsa_in, 16)
                gp.dma_start(knb[:, 0:3, :], a["nsa_k_norm_2"].rearrange("j d -> (j d)").partition_broadcast(P)
                             .rearrange("p (j d) -> p j d", d=DN)).then_inc(nsa_in, 16)
                gp.dma_start(knb[:, 3, :], a["nsa_q_norm_2"][0].partition_broadcast(P)).then_inc(nsa_in, 16)
            pool.wait_ge(k_["sq"], 1)
            rsqrt(nst[:, 16:32], nst[:, 32:48], nst[:, 48:64], mhalf[:, 0:16], 1.0 / DN, k_["rs"])
            pool.wait_ge(k_["sq"], 2)
            rsqrt(nst[0:60, 0:1], nst[0:60, 1:2], nst[0:60, 2:3], mhalf[0:60, 0:1], 1.0 / DN, k_["rs"])
            pool.wait_ge(k_["sq"], 3)
            rsqrt(nst[:, 64:96], nst[:, 96:128], nst[:, 128:160], mhalf[:, 0:32], 1.0 / DN, k_["rs"])
            norm(5)

        @block.scalar
        def _(act):
            sc = nc.scalar
            chain = Chain(act, actc)

            def split(s, n, width=2048):
                act.wait_ge(raw_full[s], 32 * n + 32)
                if not isinstance(n, int) or n > 0:
                    act.wait_ge(used[s], n)
                sc.copy(whi[:, s, 0:width], raw[:, s, 0:width]).then_inc(hi_ready[s], 1)

            def norm(k, j, fresh=True):
                if fresh:
                    for i in range(TT):
                        if j == 0:
                            act.wait_ge(x_in, 16)
                        else:
                            act.wait_ge(p_res, 2 * (j - 1) + i + 1)
                        sc.activation(y[:, i, :], res[:, i, :], ACT.Square, accum_out=ss[:, i:i + 1]).then_inc(n_sq, 1)
                else:
                    act.wait_ge(proj_done, G_Q)
                for b in range(4):
                    act.wait_ge(n_affine, 4 * k + b + 1)
                    sc.copy(xhi[:, 2 * b:2 * b + 2, :], xf[:, 2 * b:2 * b + 2, :]).then_inc(n_hi, 1)

            def post(k):
                act.wait_ge(acc_done, k + 1)
                for i in range(TT):
                    sc.activation(y[:, i, :], psum[:, 2 * i:2 * i + 2, :].rearrange("p b n -> p (b n)"), ACT.Square,
                                  accum_out=stat[:, 36 + i:37 + i]).then_inc(p_sq, 1)

            def turn(k):
                for b in range(4):
                    act.wait_ge(t_turned, 4 * k + b + 1)
                    sc.copy(xhi[:, 2 * b:2 * b + 2, :], psum[:, 4 + b, :].rearrange("p (k t) -> p k t", k=2)).then_inc(t_hi, 1)

            def evac(g, p, dst):
                act.wait_ge(proj_done, g + 1)
                sc.copy(dst, psum[:, 2 * p, 0:dst.shape[-1]]).then_inc(evac_a, 1)

            act.wait_ge(vec_turned, 1)
            sc.copy(vcol[:], psum[:, 0, 0:96]).then_inc(vec_saved, 1)
            sc.copy(bcol[:], psum[:, 0, 128:128 + 112]).then_inc(vec_saved, 1)
            act.wait_ge(vec_saved, 1)
            sc.activation(cact[:], vcol[:, VR["c"]:VR["c"] + 8], ACT.Silu).then_inc(c_ready, 1)
            norm(0, 0)
            for s in range(4):
                split(s, Q_QKV)
            with act.Fori(0, N_QKV) as t:
                for p in range(2):
                    split(2 * p, t + 1)
                    split(2 * p + 1, t + 1)
                    evac(2 * t + p, p, qkv[:, 0, bass.ds(t * 1024 + p * 512, 512)])

            for h in range(H1 + 1):
                if h < H1:
                    act.wait_ge(a_qk, h + 1)
                    if h >= 2:
                        act.wait_ge(a_s, h - 1)
                    sc.mul(qkT[:, h % 2, 0:T], psum[:, h % 2, 0:T], DH1 ** -0.5)
                    sc.copy(qkT[:, h % 2, T:2 * T], psum[:, h % 2, T:2 * T]).then_inc(a_qks, 1)
                if h >= 1:
                    g = h - 1
                    act.wait_ge(a_m, g + 1)
                    if g >= 2:
                        act.wait_ge(a_pts, g - 1)
                    m = st1[:, g % 2, :]
                    sc.activation(pb1[:, g % 2, 0:P], sc1[:, g % 2, 0:P], ACT.Exp, bias=m[:, 0:1], accum_out=m[:, 2:3])
                    sc.activation(pb1[:, g % 2, P:384], sc1[:, g % 2, P:384], ACT.Exp, bias=m[:, 1:2],
                                  accum_out=m[:, 3:4]).then_inc(a_e, 1)
            turn(0)
            split(0, Q_FF1)
            split(1, Q_FF1)
            post(0)
            norm(1, 1)
            split(2, Q_FF1)
            split(3, Q_FF1)

            def mlp1(t, first=False):
                split(0, t + (Q_FF1 + 1))
                act.wait_ge(up_done, t + 1)
                for i in range(TT):
                    sc.activation(relu[:, i, :], psum[:, 4 + i, :], ACT.Relu).then_inc(act_done, 1)
                split(1, t + (Q_FF1 + 1))
                if not first:
                    split(2, t + Q_FF1)
                    split(3, t + Q_FF1)
                for b in range(2):
                    act.wait_ge(h_turned, 2 * t + b + 1)
                    sc.activation(sq[:, 2 * b:2 * b + 2, :], psum[:, 6 + b, :].rearrange("p (k t) -> p k t", k=2),
                                  ACT.Square).then_inc(h_sq, 1)
                    act.wait_ge(h_sq, 2 * t + b + 1)
                    sc.copy(hhi[:, 2 * b:2 * b + 2, :], sq[:, 2 * b:2 * b + 2, :]).then_inc(h_hi, 1)
            mlp1(0, True)
            with act.Fori(1, N_FF1) as t:
                mlp1(t)
            for s in (2, 3):
                split(s, Q_HIN)
            post(1)
            norm(2, 2)
            tmp = area(12416, TT, D)
            for t, sec in enumerate((1, 0, 2, 3)):
                for p in range(2):
                    split(2 * p, Q_HIN + t + 1)
                    split(2 * p + 1, Q_HIN + t + 1)
                    evac(G_HIN + 2 * t + p, p, hin[:, sec, 0, p * 512:(p + 1) * 512])
                act.wait_ge(evac_d, G_HIN + 2 * t + 2)
                act.wait_ge(evac_a, G_HIN + 2 * t + 2)
                x = hin[:, sec, :, :]
                if sec == 1:
                    chain(sc.activation(tmp, x, ACT.Abs))
                    chain(sc.activation(tmp, tmp, ACT.Exp, scale=-1.0))
                    chain(sc.activation(tmp, tmp, ACT.Ln, bias=1.0))
                    sc.activation(hk, x, ACT.Sigmoid, scale=-1.0).then_inc(g_f, 1)
                elif sec != 2:
                    sc.activation(x, x, ACT.Silu).then_inc(g_f, 1)
            for h in range(HH):
                act.wait_ge(r_qk, h + 1)
                if h >= 1:
                    act.wait_ge(r_s, 2 * h)
                sc.copy(qkTh.rearrange("p j t -> p (j t)"), psum[:, 0, :]).then_inc(r_qks, 1)
                for i in range(TT):
                    n = 2 * h + i
                    act.wait_ge(r_e, n + 1)
                    if n >= 1:
                        act.wait_ge(r_s, n)
                    sc.activation(ee, psum[:, 1 + 2 * i:3 + 2 * i, :].rearrange("p b (l t) -> p (b l) t", t=P),
                                  ACT.Exp).then_inc(r_ee, 1)
                act.wait_ge(r_o, h + 1)
                sc.copy(hin[:, 0, :, h * DK:(h + 1) * DK], psum[:, 7, P:3 * P].rearrange("p (i d) -> p i d", i=2)).then_inc(r_os, 1)
            act.wait_ge(r_os, HH)
            act.wait_ge(r_am, 2 * HH)
            sc.activation(tmp, hin[:, 0, :, :], ACT.Square).then_inc(g_a, 1)
            turn(1)
            split(0, Q_F2A)
            split(1, Q_F2A)
            norm(3, 3)
            split(2, Q_F2A, 1024)
            split(3, Q_F2A, 1024)

            def mlp2(t, q0, u0, hb, first=False, nxt=2048, last=False):
                if not last:
                    split(0, t + (q0 + 1), nxt)
                act.wait_ge(up_done, t + (u0 + 1))
                for i in range(TT):
                    sc.activation(sil[:, i, :], psum[:, 4 + i, 0:256], ACT.Silu).then_inc(act_done, 1)
                if not last:
                    split(1, t + (q0 + 1), nxt)
                if not first:
                    split(2, t + q0, 1024)
                    split(3, t + q0, 1024)
                act.wait_ge(h_turned, t + (hb + 1))
                sc.copy(hhi[:, 0:2, :], psum[:, 6, :].rearrange("p (k t) -> p k t", k=2)).then_inc(h_hi, 1)
            mlp2(0, Q_F2A, U_F2A, HT_F2A, first=True)
            with act.Fori(1, N_FF2 - 1) as t:
                mlp2(t, Q_F2A, U_F2A, HT_F2A)
            mlp2(N_FF2 - 1, Q_F2A, U_F2A, HT_F2A, nxt=1536)
            for s in (2, 3):
                split(s, Q_KV, 1536)
            norm(4, 4)
            kvf = area(0, TT, 1536)
            for t in range(N_KV):
                for p in range(2):
                    if t == 0:
                        split(2 * p, Q_KV + 1, 1536)
                        split(2 * p + 1, Q_KV + 1, 1536)
                    evac(G_KV + 2 * t + p, p, kvf[:, 0, (2 * t + p) * 384:(2 * t + p + 1) * 384])
            norm(5, None, fresh=False)
            for s in range(4):
                split(s, Q_NQ)
            nqf = area(3072, TT, D)
            for p in range(2):
                evac(G_Q + p, p, nqf[:, 0, p * 512:(p + 1) * 512])
            act.wait_ge(k_["g"], 1)
            sc.activation(gat3, psum[:, 4, 0:96].rearrange("p (i n) -> p i n", i=2), ACT.Sigmoid).then_inc(k_["gs"], 1)
            act.wait_ge(k_["even"], 1)
            sc.copy(kt2.rearrange("p j h m -> p j (h m)"), psum[:, 5:7, :]).then_inc(k_["evens"], 1)
            act.wait_ge(k_["hid"], 1)
            sc.activation(hid.rearrange("p j h c -> p (j h c)"), psum[:, 7, 0:240], ACT.Silu).then_inc(k_["hids"], 1)
            for s in range(4):
                act.nop().then_inc(hi_ready[s], 1)
                split(s, Q_NOUT)
            act.wait_ge(evac_d, G_END)
            act.wait_ge(evac_a, G_END)
            act.wait_ge(k_["krope"], 1)
            sc.activation(nt1, nqf.rearrange("p i n -> p (i n)"), ACT.Square).then_inc(k_["qsq"], 1)
            act.wait_ge(k_["kT"], 1)
            for b in range(4):
                sc.copy(nkT.rearrange("p b h t -> p (b h) t")[:, 2 * b:2 * b + 2, :],
                        psum[:, b, :].rearrange("p (k t) -> p k t", k=2)).then_inc(k_["kTs"], 1)
            for j, (src, dst, b0) in enumerate((("qT", nqT, 0), ("qrT", nqrT, 4))):
                act.wait_ge(k_[src], 1)
                for b in range(4):
                    sc.copy(dst[:, 2 * b:2 * b + 2, :],
                            psum[:, b0 + b, :].rearrange("p (k t) -> p k t", k=2)).then_inc(k_[src + "s"], 1)
            act.wait_ge(k_["cm"], 1)
            for i in range(TT):
                last = sc.activation(pc[:, i, :, 0:NCMP], pc[:, i, :, 0:NCMP], ACT.Exp)
            last.then_inc(k_["ce"], 1)
            act.wait_ge(k_["cT"], 1)
            sc.copy(pcT.rearrange("p j t -> p (j t)"), psum[:, 2, :]).then_inc(k_["cTs"], 1)
            act.wait_ge(k_["co"], 1)
            for i in range(TT):
                sc.copy(ob2[:, i, :, :].rearrange("p h d -> p (h d)"),
                        psum[:, 4 + 2 * i:6 + 2 * i, :].rearrange("p b n -> p (b n)")).then_inc(k_["cos"], 1)
            for u in range(2 * NH):
                act.wait_ge(w_m, u + 1)
                if u >= 2:
                    act.wait_ge(w_pts, u - 1)
                m = nst[:, 8 * (u % 2):8 * (u % 2) + 8]
                sc.activation(pb2[:, u % 2, 0:P], sc2[:, u % 2, 0:P], ACT.Exp, bias=m[:, 0:1], accum_out=m[:, 2:3])
                sc.activation(pb2[:, u % 2, P:384], sc2[:, u % 2, P:384], ACT.Exp, bias=m[:, 1:2],
                              accum_out=m[:, 3:4]).then_inc(w_e, 1)
            turn(2)
            split(0, Q_F2B)
            split(1, Q_F2B)
            norm(6, 5)
            split(2, Q_F2B, 1024)
            split(3, Q_F2B, 1024)
            mlp2(0, Q_F2B, U_F2B, HT_F2B, first=True)
            with act.Fori(1, N_FF2 - 1) as t:
                mlp2(t, Q_F2B, U_F2B, HT_F2B)
            mlp2(N_FF2 - 1, Q_F2B, U_F2B, HT_F2B, last=True)

        @block.vector
        def _(v):
            ve = nc.vector
            chain = Chain(v, dve)

            def split(s, n, width=2048):
                v.wait_ge(hi_ready[s], n + 1)
                ve.tensor_tensor(wlo[:, s, 0:width], raw[:, s, 0:width], whi[:, s, 0:width].bitcast(F32),
                                 ALU.subtract).then_inc(lo_ready[s], 1)

            def ada(m, half):
                v.wait_ge(ada_full[half], 16 * m + 16)
                for k in range(4):
                    w = adaw[:, half, k * 512:(k + 1) * 512]
                    c = cact[:, 4 * half + k:4 * half + k + 1]
                    if k:
                        v.wait_ge(ada_step, 6 * m + 3 * half + k)
                    elif half:
                        v.wait_ge(ada_used[0], m + 1)
                    elif not isinstance(m, int) or m > 0:
                        v.wait_ge(ada_turned, m)
                    if half == 0 and k == 0:
                        ins = ve.tensor_scalar(adaacc[:], w, c, None, ALU.mult)
                    else:
                        ins = ve.scalar_tensor_tensor(adaacc[:], w, c, adaacc[:], ALU.mult, ALU.add)
                    ins.then_inc(ada_used[half] if k == 3 else ada_step, 1)

            def ada_save(m):
                v.wait_ge(ada_turned, m + 1)
                ve.tensor_copy(adacol[:, bass.ds(m * 4, 4)], psum[:, 4, 0:4]).then_inc(ada_saved, 1)

            def mods(key, gain, upto, n=24):
                c = LCOL[key]
                v.wait_ge(ada_saved, upto)
                v.wait_ge(vec_saved, 2)
                ve.tensor_tensor(adacol[:, c:c + n], adacol[:, c:c + n], bcol[:, c:c + n], ALU.add).then_inc(aff_ready, 1)
                v.wait_ge(aff_ready, ("order", 0, 1, 2, "kv", 3).index(key))
                affine_cols(c, gain)

            def affine_cols(c, gain):
                chain(ve.tensor_copy(sh[:], adacol[:, c:c + 8]))
                chain(ve.scalar_tensor_tensor(gs[:], adacol[:, c + 8:c + 16], 1.0, vcol[:, gain:gain + 8], ALU.add, ALU.mult))

            def norm(k, j, fresh=True, shift=True):
                if fresh:
                    v.wait_ge(n_rstd, j + 1)
                    for i in range(TT):
                        ve.tensor_scalar(y[:, i, :], res[:, i, :], rstd[:, i:i + 1], None, ALU.mult).then_inc(n_y, 1)
                for b in range(4):
                    v.wait_ge(n_turned, 4 * k + b + 1)
                    for q in range(2):
                        kt = 2 * b + q
                        src = psum[:, 4 + b, q * T:(q + 1) * T]
                        if shift:
                            ins = ve.tensor_scalar(xf[:, kt, :], src, gs[:, kt:kt + 1], sh[:, kt:kt + 1], ALU.mult, ALU.add)
                        else:
                            ins = ve.tensor_scalar(xf[:, kt, :], src, gs[:, kt:kt + 1], None, ALU.mult)
                    ins.then_inc(n_affine, 1)
                for b in range(4):
                    v.wait_ge(n_hi, 4 * k + b + 1)
                    ve.tensor_tensor(xlo[:, 2 * b:2 * b + 2, :], xf[:, 2 * b:2 * b + 2, :],
                                     xhi[:, 2 * b:2 * b + 2, :].bitcast(F32), ALU.subtract).then_inc(n_x, 1)

            def turn(k):
                for b in range(4):
                    v.wait_ge(t_hi, 4 * k + b + 1)
                    ve.tensor_tensor(xlo[:, 2 * b:2 * b + 2, :], psum[:, 4 + b, :].rearrange("p (k t) -> p k t", k=2),
                                     xhi[:, 2 * b:2 * b + 2, :].bitcast(F32), ALU.subtract).then_inc(t_x, 1)

            def evac(g, p, dst):
                v.wait_ge(proj_done, g + 1)
                ve.tensor_copy(dst, psum[:, 2 * p + 1, 0:dst.shape[-1]]).then_inc(evac_d, 1)

            def residual(k):
                v.wait_ge(acc_done, k + 1)
                if k < 2:
                    v.wait_ge(p_rstd, k + 1)
                    v.wait_ge(gain_in, 16 * k + 16)
                for i in range(TT):
                    acc = psum[:, 2 * i:2 * i + 2, :].rearrange("p b n -> p (b n)")
                    if k < 2:
                        chain(ve.scalar_tensor_tensor(y[:, i, :], acc, stat[:, 38 + i:39 + i], gain_b[:], ALU.mult, ALU.mult))
                    else:
                        chain(ve.tensor_tensor(y[:, i, :], acc, gain_b[:], ALU.mult))
                    ve.tensor_tensor(res[:, i, :], res[:, i, :], y[:, i, :], ALU.add).then_inc(p_res, 1)

            def gate_save(k):
                v.wait_ge(bg_turned, k + 1)
                ve.tensor_copy(gain_b[:, :], psum[:, 4:6, :].rearrange("p b n -> p (b n)")).then_inc(bg_saved, 1)

            v.wait_ge(vec_saved, 1)
            chain(ve.tensor_copy(gs[:], vcol[:, 0:8]))
            norm(0, 0, shift=False)
            for s in range(4):
                split(s, Q_QKV)
            with v.Fori(0, N_QKV) as t:
                for p in range(2):
                    split(2 * p, t + 1)
                    split(2 * p + 1, t + 1)
                    evac(2 * t + p, p, qkv[:, 1, bass.ds(t * 1024 + p * 512, 512)])

            v.wait_ge(dist_in, 16)
            for h in range(H1 + 3):
                if 1 <= h <= H1:
                    g = h - 1
                    m = st1[:, g % 2, :]
                    v.wait_ge(a_s, g + 1)
                    if g >= 2:
                        v.wait_ge(a_e, g - 1)
                    chain(ve.scalar_tensor_tensor(sc1[:, g % 2, :], dist, 2.0 ** -(8.0 * (g + 1) / H1), psum[:, 2 + g % 2, 0:384],
                                                  ALU.mult, ALU.add))
                    ve.tensor_reduce(m[:, 0:1], sc1[:, g % 2, 0:P], AX, ALU.max, negate=True)
                    ve.tensor_reduce(m[:, 1:2], sc1[:, g % 2, P:384], AX, ALU.max, negate=True).then_inc(a_m, 1)
                if 2 <= h <= H1 + 1:
                    g = h - 2
                    m = st1[:, g % 2, :]
                    v.wait_ge(a_e, g + 1)
                    wait(v, a_os, g - 1)
                    ve.reciprocal(m[:, 4:6], m[:, 2:4])
                    v.wait_ge(a_pt, g + 1)
                    if g >= 2:
                        v.wait_ge(a_o, g - 1)
                    ve.tensor_copy(pT1[:, g % 2, :], psum[:, 4 + g % 2, 0:384]).then_inc(a_pts, 1)
                if 3 <= h:
                    g = h - 3
                    m = st1[:, g % 2, :]
                    v.wait_ge(a_o, g + 1)
                    v.wait_ge(a_pts, g + 1)
                    for i in range(TT):
                        ins = ve.tensor_scalar(ob1[:, i, g * DH1:(g + 1) * DH1], psum[:, 6 + g % 2, i * P:(i + 1) * P],
                                               m[:, 4 + i:5 + i], None, ALU.mult)
                    ins.then_inc(a_os, 1)
            turn(0)
            split(0, Q_FF1)
            split(1, Q_FF1)
            residual(0)
            chain(ve.tensor_copy(gs[:], vcol[:, 8:16]))
            norm(1, 1, shift=False)
            split(2, Q_FF1)
            split(3, Q_FF1)

            def mlp1(t, first=False):
                split(0, t + (Q_FF1 + 1))
                ada(t, 0)
                split(1, t + (Q_FF1 + 1))
                if not first:
                    split(2, t + Q_FF1)
                    split(3, t + Q_FF1)
                ada(t, 1)
                ada_save(t)
                for b in range(2):
                    v.wait_ge(h_hi, 2 * t + b + 1)
                    ve.tensor_tensor(hlo[:, 2 * b:2 * b + 2, :], sq[:, 2 * b:2 * b + 2, :],
                                     hhi[:, 2 * b:2 * b + 2, :].bitcast(F32), ALU.subtract).then_inc(h_lo, 1)
            v.wait_ge(c_ready, 1)
            mlp1(0, True)
            with v.Fori(1, N_FF1) as t:
                mlp1(t)
            for s in (2, 3):
                split(s, Q_HIN)
            residual(1)
            mods(0, VR["mix2"], 6)
            norm(2, 2)
            tmp = area(12416, TT, D)
            for t, sec in enumerate((1, 0, 2, 3)):
                for p in range(2):
                    split(2 * p, Q_HIN + t + 1)
                    split(2 * p + 1, Q_HIN + t + 1)
                    evac(G_HIN + 2 * t + p, p, hin[:, sec, 1, p * 512:(p + 1) * 512])
                    ada(8 + t, p)
                ada_save(8 + t)
                if t == 1:
                    v.wait_ge(g_f, 1)
                    ve.scalar_tensor_tensor(hin[:, 1, :, :].rearrange("p i n -> p (i n)"), hin[:, 1, :, :].rearrange("p i n -> p (i n)"),
                                            0.0, tmp.rearrange("p i n -> p (i n)"), ALU.min, ALU.subtract).then_inc(g_d, 1)
            gate_save(0)
            v.wait_ge(lev_in, 16)
            v.wait_ge(g_d, 1)
            for h in range(HH):
                v.wait_ge(r_qks, h + 1)
                for i in range(TT):
                    n = 2 * h + i
                    v.wait_ge(r_ee, n + 1)
                    qTb = qkTh[:, 0, i * P:(i + 1) * P].unsqueeze(1).to_broadcast([P, NL + 1, P])
                    kTb = qkTh[:, 1, i * P:(i + 1) * P].unsqueeze(1).to_broadcast([P, NL + 1, P])
                    chain(ve.tensor_tensor(qe, ee, qTb, ALU.mult))
                    if i == 0:
                        chain(ve.tensor_tensor(ke7, ee[:, NL, :], qkTh[:, 1, 0:P], ALU.mult))
                    ve.tensor_tensor(ee, ee, kTb, ALU.mult).then_inc(r_z, 1)
                    v.wait_ge(r_s, n + 1)
                    chain(ve.tensor_tensor(pm, psum[:, 5:7, :].rearrange("p b (l t) -> p (b l) t", t=P), MK, ALU.mult))
                    if h and i == 0:
                        v.wait_ge(r_o, h)
                    ins = ve.tensor_reduce(am[:, i, :], pm.rearrange("p l t -> p t l"), AX, ALU.add)
                    if i == 1:
                        ins = ve.tensor_copy(am[:, 2, :], psum[:, 7, 0:P])
                    ins.then_inc(r_am, 1)
            v.wait_ge(g_f, 3)
            v.wait_ge(onb_in, 16)
            hg = hin[:, 3, :, :].rearrange("p i (h d) -> p (i h) d", d=DK)
            ho = hin[:, 0, :, :].rearrange("p i (h d) -> p (i h) d", d=DK)
            chain(ve.tensor_tensor(hg, hg, onb[:].unsqueeze(1).to_broadcast([P, 2 * HH, DK]), ALU.mult))
            v.wait_ge(g_a, 1)
            ve.tensor_reduce(hs[:, 0:16], tmp.rearrange("p i (h d) -> p (i h) d", d=DK), AX, ALU.add).then_inc(r_ms, 1)
            v.wait_ge(r_rs, 1)
            chain(ve.tensor_tensor(ho, ho, hs[:, 16:32].unsqueeze(2).to_broadcast([P, 2 * HH, DK]), ALU.mult))
            ve.tensor_tensor(ho, ho, hg, ALU.mult).then_inc(g_d, 1)
            turn(1)
            mods(1, VR["ffn2"], 12)

            split(0, Q_F2A)
            split(1, Q_F2A)
            residual(2)
            gate_save(1)
            norm(3, 3)
            split(2, Q_F2A, 1024)
            split(3, Q_F2A, 1024)

            def mlp2(t, q0, hb, gb, m=None, first=False, nxt=2048, last=False):
                if not last:
                    split(0, t + (q0 + 1), nxt)
                if m is not None:
                    ada(m, 0)
                for i in range(TT):
                    v.wait_ge(act_done, 2 * t + (gb + 16 + i + 1))
                    ve.tensor_tensor(gat[:, i, :], sil[:, i, :], psum[:, 4 + i, 256:512], ALU.mult).then_inc(gate_done, 1)
                if not last:
                    split(1, t + (q0 + 1), nxt)
                if not first:
                    split(2, t + q0, 1024)
                    split(3, t + q0, 1024)
                if m is not None:
                    ada(m, 1)
                    ada_save(m)
                v.wait_ge(h_hi, t + (hb + 1))
                ve.tensor_tensor(hlo[:, 0:2, :], psum[:, 6, :].rearrange("p (k t) -> p k t", k=2),
                                 hhi[:, 0:2, :].bitcast(F32), ALU.subtract).then_inc(h_lo, 1)
            mlp2(0, Q_F2A, HT_F2A, 0, M_L2, first=True)
            with v.Fori(1, N_FF2 - 1) as t:
                mlp2(t, Q_F2A, HT_F2A, 0, t + M_L2)
            mlp2(N_FF2 - 1, Q_F2A, HT_F2A, 0, M_L3, nxt=1536)
            for s in (2, 3):
                split(s, Q_KV, 1536)
            residual(3)
            mods(2, VR["mix2"] + 8, M_L3 + 1)
            mods("kv", VR["kvn"], M_L3 + 1, 16)
            norm(4, 4)
            kvf = area(0, TT, 1536)
            for t in range(N_KV):
                for p in range(2):
                    if t == 0:
                        split(2 * p, Q_KV + 1, 1536)
                        split(2 * p + 1, Q_KV + 1, 1536)
                    evac(G_KV + 2 * t + p, p, kvf[:, 1, (2 * t + p) * 384:(2 * t + p + 1) * 384])
                    ada(M_L3 + 1 + t, p)
                ada_save(M_L3 + 1 + t)
            affine_cols(LCOL[2], VR["mix2"] + 8)
            norm(5, None, fresh=False)
            for s in range(4):
                split(s, Q_NQ)
            nqf = area(3072, TT, D)
            for p in range(2):
                evac(G_Q + p, p, nqf[:, 1, p * 512:(p + 1) * 512])
            v.wait_ge(k_["evens"], 1)
            for j in range(2):
                for c in range(NCMP):
                    pos = vcol[:, VR["pos"] + 16 * j:VR["pos"] + 16 * j + 16].unsqueeze(2).to_broadcast([P, 16, NKV])
                    ins = ve.tensor_tensor(fl[:, j, :, c, :], kt2[:, j, :, 8 * c:8 * c + 16].rearrange("p h a -> p a h"), pos, ALU.add)
            ins.then_inc(k_["flat"], 1)
            v.wait_ge(k_["flat"], 1)
            v.wait_ge(nsa_in, 64)
            v.wait_ge(evac_a, G_Q)
            v.wait_ge(evac_d, G_Q)
            kk = kv[:, :, 2:6:2, :, :]
            k2 = nt1[:, 0:1024].rearrange("p (i b h d) -> p i b h d", i=2, b=2, h=4)
            for i in range(TT):
                for b in range(2):
                    ins = ve.tensor_tensor(k2[:, i, b], kv[:, i, 2 + 2 * b], kv[:, i, 2 + 2 * b], ALU.mult)
            chain(ins)
            ve.tensor_reduce(nst[:, 16:32], nt1[:, 0:1024].rearrange("p (g d) -> p g d", d=DN), AX, ALU.add).then_inc(k_["sq"], 1)
            v.wait_ge(k_["kc"], 1)
            ve.tensor_copy(kcv[0:60, :, :], psum[0:60, 4, 256:384].rearrange("p (j d) -> p j d", j=2)).then_inc(k_["kcs"], 1)
            v.wait_ge(k_["kcs"], 1)
            chain(ve.tensor_tensor(kcd[0:60, 0, :], kcv[0:60, 0, :], kcv[0:60, 0, :], ALU.mult))
            ve.tensor_reduce(nst[0:60, 0:1], kcd[0:60, 0, :], AX, ALU.add).then_inc(k_["sq"], 1)
            v.wait_ge(k_["rs"], 2)
            for j in range(2):
                ins = ve.scalar_tensor_tensor(kcd[0:60, j, :], kcv[0:60, 0, :], nst[0:60, 1:2], knb[0:60, 0, :], ALU.mult, ALU.mult)
            ins.then_inc(k_["kcd"], 1)
            v.wait_ge(k_["vb"], 1)
            for j in range(2):
                ins = ve.tensor_tensor(vbd[:, j, :, :], psum[:, 5 + j, 0:DN].unsqueeze(1).to_broadcast([P, 8, DN]),
                                       cst("bm").unsqueeze(2).to_broadcast([P, 8, DN]), ALU.mult)
            ins.then_inc(k_["vbs"], 1)
            v.wait_ge(k_["kct"], 1)
            ve.tensor_copy(kcT[:, :], psum[:, 7, 256:316]).then_inc(k_["kcts"], 1)

            rope = cst("rope").rearrange("p (i j d) -> p i j d", i=2, j=2)
            HD = DN // 2

            def turn_half(dst1, dst2, x1, x2, cos, sin, tmp1):
                ve.tensor_tensor(dst1, x1, cos, ALU.mult)
                chain(ve.tensor_tensor(tmp1, x2, sin, ALU.mult))
                ve.tensor_tensor(dst2, x2, cos, ALU.mult)
                chain(ve.tensor_tensor(dst1, dst1, tmp1, ALU.subtract))
                chain(ve.tensor_tensor(tmp1, x1, sin, ALU.mult))
                chain(ve.tensor_tensor(dst2, dst2, tmp1, ALU.add))

            for i in range(TT):
                for b in range(2):
                    r = nst[:, 32 + 8 * i + 4 * b:36 + 8 * i + 4 * b].unsqueeze(2).to_broadcast([P, NKV, DN])
                    x = kv[:, i, 2 + 2 * b, :, :]
                    chain(ve.tensor_tensor(x, x, r, ALU.mult))
                    chain(ve.tensor_tensor(x, x, knb[:, 1 + b, :].unsqueeze(1).to_broadcast([P, NKV, DN]), ALU.mult))
                    cos = rope[:, i, 0, :].unsqueeze(1).to_broadcast([P, NKV, HD])
                    sin = rope[:, i, 1, :].unsqueeze(1).to_broadcast([P, NKV, HD])
                    d = nkd[:, i, b, :, 0, :]
                    turn_half(d[:, :, 0:HD], d[:, :, HD:DN], x[:, :, 0:HD], x[:, :, HD:DN], cos, sin,
                              nt1[:, 1024:1024 + NKV * HD].rearrange("p (h d) -> p h d", h=NKV))
                    ins = ve.tensor_copy(nkd[:, i, b, :, 1, :], d)
            ins.then_inc(k_["krope"], 1)
            for s in range(4):
                v.nop().then_inc(lo_ready[s], 1)
                split(s, Q_NOUT)
            ada(M_L3 + 3, 0)
            ada(M_L3 + 3, 1)
            ada_save(M_L3 + 3)
            v.wait_ge(k_["qsq"], 1)
            ve.tensor_reduce(nst[:, 64:96], nt1.rearrange("p (g d) -> p g d", d=DN), AX, ALU.add).then_inc(k_["sq"], 1)
            chain(ve.tensor_scalar(knb[:, 3, :], knb[:, 3, :], DN ** -0.5, None, ALU.mult))
            v.wait_ge(k_["rs"], 3)
            qg = nq.rearrange("p i h d -> p (i h) d")
            chain(ve.tensor_tensor(qg, qg, nst[:, 96:128].unsqueeze(2).to_broadcast([P, 2 * NH, DN]), ALU.mult))
            ve.tensor_tensor(qg, qg, knb[:, 3, :].unsqueeze(1).to_broadcast([P, 2 * NH, DN]), ALU.mult).then_inc(k_["qn"], 1)
            v.wait_ge(k_["qn"], 1)
            v.wait_ge(k_["kT"], 1)
            for i in range(TT):
                cos = rope[:, i, 0, :].unsqueeze(1).to_broadcast([P, NH, HD])
                sin = rope[:, i, 1, :].unsqueeze(1).to_broadcast([P, NH, HD])
                turn_half(nqr[:, i, :, 0:HD], nqr[:, i, :, HD:DN], nq[:, i, :, 0:HD], nq[:, i, :, HD:DN], cos, sin,
                          nt1[:, 512 * i:512 * i + 512].rearrange("p (h d) -> p h d", h=NH))
            v.nop().then_inc(k_["qr"], 1)
            gate_save(2)
            cm = cst("cmask").rearrange("p (j i c) -> p j i c", j=2, i=2)
            v.wait_ge(k_["cs"], 1)
            chain(ve.memset(pc, 0.0))
            ng = nst[:, 128:160].rearrange("p (i h) -> p i h", i=2)
            for i in range(TT):
                x = pc[:, i, :, 0:NCMP]
                for r in range(2):
                    ins = ve.tensor_tensor(pc[:, i, r:NH:2, 0:NCMP],
                                           psum[:, 2 * i + r, 0:128].rearrange("p (h c) -> p h c", c=16)[:, :, 0:NCMP],
                                           cm[:, 0, i, :].unsqueeze(1).to_broadcast([P, NH // 2, NCMP]), ALU.add)
                chain(ins)
                chain(ve.tensor_reduce(ng[:, i, :], x, AX, ALU.max))
                ins = ve.tensor_tensor(x, x, ng[:, i, :].unsqueeze(2).to_broadcast([P, NH, NCMP]), ALU.subtract)
            ins.then_inc(k_["cm"], 1)
            v.wait_ge(k_["ce"], 1)
            for i in range(TT):
                x = pc[:, i, :, 0:NCMP]
                chain(ve.tensor_tensor(x, x, cm[:, 1, i, :].unsqueeze(1).to_broadcast([P, NH, NCMP]), ALU.mult))
                chain(ve.tensor_reduce(ng[:, i, :], x, AX, ALU.add))
            chain(ve.tensor_scalar(ng, ng, 1e-30, None, ALU.max))
            chain(ve.reciprocal(ng, ng))
            v.wait_ge(k_["gs"], 1)
            chain(ve.tensor_tensor(ng, ng, gat3[:, :, 0:NH], ALU.mult))
            for i in range(TT):
                x = pc[:, i, :, 0:NCMP]
                ins = ve.tensor_tensor(x, x, ng[:, i, :].unsqueeze(2).to_broadcast([P, NH, NCMP]), ALU.mult)
            ins.then_inc(k_["cp"], 1)
            v.wait_ge(k_["cos"], 2)
            caus = cst("caus")
            for w in range(2 * NH + 2):
                if w < 2 * NH:
                    u = w
                    m = nst[:, 8 * (u % 2):8 * (u % 2) + 8]
                    v.wait_ge(w_s, u + 1)
                    if u >= 2:
                        v.wait_ge(w_e, u - 1)
                    chain(ve.tensor_tensor(sc2[:, u % 2, :], psum[:, u % 2, 0:384], caus, ALU.add))
                    ve.tensor_reduce(m[:, 0:1], sc2[:, u % 2, 0:P], AX, ALU.max, negate=True)
                    ve.tensor_reduce(m[:, 1:2], sc2[:, u % 2, P:384], AX, ALU.max, negate=True).then_inc(w_m, 1)
                if 1 <= w <= 2 * NH:
                    u = w - 1
                    hq, b = u // 2, u % 2
                    m = nst[:, 8 * (u % 2):8 * (u % 2) + 8]
                    v.wait_ge(w_e, u + 1)
                    wait(v, w_os, u - 1)
                    chain(ve.reciprocal(m[:, 4:6], m[:, 2:4]))
                    ve.tensor_tensor(m[:, 4:6], m[:, 4:6], gat3[:, :, (1 + b) * NH + hq], ALU.mult)
                    v.wait_ge(w_pt, u + 1)
                    if u >= 2:
                        v.wait_ge(w_o, u - 1)
                    ve.tensor_copy(pT2[:, u % 2, :], psum[:, 2 + u % 2, 0:384]).then_inc(w_pts, 1)
                if 2 <= w:
                    u = w - 2
                    hq = u // 2
                    m = nst[:, 8 * (u % 2):8 * (u % 2) + 8]
                    v.wait_ge(w_o, u + 1)
                    v.wait_ge(w_pts, u + 1)
                    if u:
                        v.wait_ge(w_os, u)
                    for i in range(TT):
                        ins = ve.scalar_tensor_tensor(ob2[:, i, hq, :], psum[:, 4 + u % 2, i * DN:(i + 1) * DN],
                                                      m[:, 4 + i:5 + i], ob2[:, i, hq, :], ALU.mult, ALU.add)
                    ins.then_inc(w_os, 1)
            turn(2)
            for b in (4, 5):
                ada(M_L3 + b, 0)
                ada(M_L3 + b, 1)
                ada_save(M_L3 + b)
            mods(3, VR["ffn2"] + 8, M_END)
            split(0, Q_F2B)
            split(1, Q_F2B)
            residual(4)
            gate_save(3)
            norm(6, 5)
            split(2, Q_F2B, 1024)
            split(3, Q_F2B, 1024)
            mlp2(0, Q_F2B, HT_F2B, 22, first=True)
            with v.Fori(1, N_FF2 - 1) as t:
                mlp2(t, Q_F2B, HT_F2B, 22)
            mlp2(N_FF2 - 1, Q_F2B, HT_F2B, 22, last=True)
            residual(5)

        @block.tensor
        def _(pe):
            te = nc.tensor

            def mm(dst, lhsT, rhs, start=True, stop=True, open_=False):
                return te.matmul(dst, lhsT, rhs, start=start, stop=stop, skip_group_check=open_)

            def three(dst, lhi, llo, s, c0, n, start, stop, open_=False):
                wh, wl = whi[:, s, c0:c0 + n], wlo[:, s, c0:c0 + n]
                mm(dst, lhi, wh, start, False, open_)
                mm(dst, lhi, wl, False, False, open_)
                return mm(dst, llo, wh, False, stop, open_)

            def norm(k, j, ada_upto=0, gates=0):
                wait(pe, ada_saved, ada_upto)
                wait(pe, bg_saved, gates)
                for b in range(4):
                    if j is None:
                        pe.wait_ge(n_affine, 4 * k - 4 + b + 1)
                    for i in range(TT):
                        if j is not None and b == 0:
                            pe.wait_ge(n_y, 2 * j + i + 1)
                        for q in range(2):
                            kt = 2 * b + q
                            ins = te.transpose(psum[:, 4 + b, q * T + i * P:q * T + (i + 1) * P], y[:, i, kt * P:(kt + 1) * P], ident)
                    ins.then_inc(n_turned, 1)

            def turn(k, x):
                for b in range(4):
                    for q in range(2):
                        for i in range(TT):
                            kt = 2 * b + q
                            ins = te.transpose(psum[:, 4 + b, q * T + i * P:q * T + (i + 1) * P], x[:, i, kt * P:(kt + 1) * P], ident)
                    ins.then_inc(t_turned, 1)

            def item_ready(s, n):
                pe.wait_ge(lo_ready[s], n + 1)

            def project(n, g, width=512):
                for p in range(2):
                    if not isinstance(g, int) or g >= 2:
                        pe.wait_ge(evac_a, g + p - 1)
                        pe.wait_ge(evac_d, g + p - 1)
                    for half in range(2):
                        s = 2 * p + half
                        item_ready(s, n)
                        for i in range(TT):
                            for k in range(4):
                                kt = 4 * half + k
                                ins = three(psum[:, 2 * p + i, 0:width], xhi[:, kt, i * P:(i + 1) * P], xlo[:, kt, i * P:(i + 1) * P],
                                            s, k * width, width, kt == 0, kt == KD - 1)
                        ins.then_inc(used[s], 1)
                    pe.wait_ge(used[2 * p + 1], n + 1)
                    pe.nop().then_inc(proj_done, 1)

            def accumulate(n, k_acc):
                for s in range(4):
                    item_ready(s, n)
                    for i in range(TT):
                        for f in range(2):
                            for k in range(2):
                                kt = 2 * s + k
                                ins = three(psum[:, 2 * i + f, :], xhi[:, kt, i * P:(i + 1) * P], xlo[:, kt, i * P:(i + 1) * P],
                                            s, k * D + f * 512, 512, kt == 0, kt == KD - 1)
                    ins.then_inc(used[s], 1)
                pe.wait_ge(used[3], n + 1)
                pe.nop().then_inc(acc_done, 1)

            def ada(m):
                pe.wait_ge(ada_used[1], m + 1)
                for c in range(4):
                    ins = mm(psum[:, 4, c:c + 1], adaacc[:, c * P:(c + 1) * P], ones[:])
                ins.then_inc(ada_turned, 1)

            def gate(key, k):
                pe.wait_ge(aff_ready, ("order", 0, 1, 2, "kv", 3).index(key))
                for kt in range(KD):
                    c = LCOL[key] + 16 + kt
                    ins = mm(psum[:, 4 + kt // 4, (kt % 4) * P:(kt % 4 + 1) * P], adacol[:, c:c + 1].to_broadcast([P, P]), ident)
                ins.then_inc(bg_turned, 1)

            def open_acc():
                for b in range(4):
                    mm(psum[:, b, :], zrow[0:1, 0:P], zrow[0:1, :], True, False, True)

            pe.wait_ge(consts_in, 16)
            pe.wait_ge(vec_in, 16 * 10)
            te.transpose(psum[:, 0, 0:96], vrow1[0:96, :], ident[0:96, 0:96])
            te.transpose(psum[:, 0, 128:240], vrow2[0:112, :], ident[0:112, 0:112]).then_inc(vec_turned, 1)
            pe.wait_ge(ones_set, 1)
            norm(0, 0)
            pe.wait_ge(n_x, 4)
            pe.wait_ge(vec_saved, 2)
            project(Q_QKV, 0)
            with pe.Fori(1, N_QKV) as t:
                project(t + Q_QKV, 2 * t)

            pe.wait_ge(evac_a, G_HIN)
            pe.wait_ge(evac_d, G_HIN)
            for h in range(H1 + 3):
                if h < H1:
                    if h >= 2:
                        pe.wait_ge(a_qks, h - 1)
                    for j in range(2):
                        for i in range(TT):
                            ins = te.transpose(psum[:, h % 2, j * T + i * P:j * T + (i + 1) * P],
                                               qkv[:, i, j * D + h * DH1:j * D + (h + 1) * DH1], ident)
                    ins.then_inc(a_qk, 1)
                if 1 <= h <= H1:
                    g = h - 1
                    pe.wait_ge(a_qks, g + 1)
                    if g >= 2:
                        pe.wait_ge(a_m, g - 1)
                    x = qkT[:, g % 2, :]
                    mm(psum[:, 2 + g % 2, 0:P], x[:, 0:P], x[:, T:T + P])
                    mm(psum[:, 2 + g % 2, P:384], x[:, P:T], x[:, T:2 * T]).then_inc(a_s, 1)
                if 2 <= h <= H1 + 1:
                    g = h - 2
                    pe.wait_ge(a_e, g + 1)
                    if g >= 2:
                        pe.wait_ge(a_pts, g - 1)
                    for b in range(3):
                        ins = te.transpose(psum[:, 4 + g % 2, b * P:(b + 1) * P], pb1[:, g % 2, b * P:(b + 1) * P], ident)
                    ins.then_inc(a_pt, 1)
                if 3 <= h:
                    g = h - 3
                    pe.wait_ge(a_pts, g + 1)
                    if g >= 2:
                        pe.wait_ge(a_os, g - 1)
                    o = psum[:, 6 + g % 2, :]
                    vv = qkv[:, :, 2 * D + g * DH1:2 * D + (g + 1) * DH1]
                    mm(o[:, 0:P], pT1[:, g % 2, 0:P], vv[:, 0, :])
                    mm(o[:, P:T], pT1[:, g % 2, P:T], vv[:, 0, :], True, False)
                    mm(o[:, P:T], pT1[:, g % 2, T:384], vv[:, 1, :], False, True).then_inc(a_o, 1)
            pe.wait_ge(a_os, H1)
            turn(0, ob1)
            pe.wait_ge(t_x, 4)
            accumulate(Q_WO, 0)
            norm(1, 1)
            pe.wait_ge(n_x, 8)

            def up(n, u, width_fn=None):
                for s in range(2):
                    item_ready(s, n)
                    for i in range(TT):
                        for k in range(4):
                            kt = 4 * s + k
                            ins = three(psum[:, 4 + i, :], xhi[:, kt, i * P:(i + 1) * P], xlo[:, kt, i * P:(i + 1) * P],
                                        s, k * 512, 512, kt == 0, kt == KD - 1)
                    ins.then_inc(used[s], 1)
                pe.wait_ge(used[1], n + 1)
                pe.nop().then_inc(up_done, 1)

            def down(n, kts, last=False):
                for s in (2, 3):
                    item_ready(s, n)
                    for i in range(TT):
                        for f in range(2):
                            for k in range(kts):
                                kt = kts * (s - 2) + k
                                ins = three(psum[:, 2 * i + f, :], hhi[:, kt, i * P:(i + 1) * P], hlo[:, kt, i * P:(i + 1) * P],
                                            s, k * D + f * 512, 512, False, last and kt == 2 * kts - 1, True)
                    ins.then_inc(used[s], 1)

            def hidden1(t):
                pe.wait_ge(act_done, 2 * t + 2)
                for b in range(2):
                    for q in range(2):
                        for i in range(TT):
                            kt = 2 * b + q
                            ins = te.transpose(psum[:, 6 + b, q * T + i * P:q * T + (i + 1) * P], relu[:, i, kt * P:(kt + 1) * P], ident)
                    ins.then_inc(h_turned, 1)
            open_acc()
            up(Q_FF1, 0)
            pe.wait_ge(act_done, 2)
            ada(0)
            hidden1(0)
            with pe.Fori(1, N_FF1) as t:
                pe.wait_ge(ada_saved, t)
                up(t + Q_FF1, t)
                pe.wait_ge(h_lo, 2 * t)
                down(t + (Q_FF1 - 1), 2)
                pe.wait_ge(act_done, 2 * t + 2)
                ada(t)
                hidden1(t)
            pe.wait_ge(h_lo, 2 * N_FF1)
            down(Q_FF1 + N_FF1 - 1, 2, last=True)
            pe.wait_ge(used[3], Q_FF1 + N_FF1)
            pe.nop().then_inc(acc_done, 1)
            norm(2, 2, ada_upto=8)
            pe.wait_ge(n_x, 12)
            for t in range(N_HIN):
                project(Q_HIN + t, G_HIN + 2 * t)
                wait(pe, ada_saved, 8 + t)
                ada(8 + t)

            pe.wait_ge(ada_saved, 12)
            gate(0, 0)
            pe.wait_ge(lev_in, 16)
            pe.wait_ge(evac_a, G_KV)
            pe.wait_ge(evac_d, G_KV)
            pe.wait_ge(g_f, 2)
            pe.wait_ge(g_d, 1)
            pe.wait_ge(bg_saved, 1)
            for h in range(HH):
                c = slice(h * DK, (h + 1) * DK)
                if h:
                    pe.wait_ge(r_qks, h)
                for j, src in enumerate((hin[:, 0, :, c], hk[:, :, c])):
                    for i in range(TT):
                        ins = te.transpose(psum[:, 0, j * T + i * P:j * T + (i + 1) * P], src[:, i, :], ident)
                ins.then_inc(r_qk, 1)
                for i in range(TT):
                    n = 2 * h + i
                    if h:
                        pe.wait_ge(r_ee, n - 1)
                    e = psum[:, 1 + 2 * i:3 + 2 * i, :].rearrange("p b n -> p (b n)")
                    g = hin[:, 1, i, c]
                    mm(e[:, 0:512], g, ML[:, 0:4, :].rearrange("p l t -> p (l t)"))
                    mm(e[:, 512:896], g, ML[:, 4:7, :].rearrange("p l t -> p (l t)"))
                    mm(e[:, 896:1024], g, ML[:, NL + i, :]).then_inc(r_e, 1)
                for i in range(TT):
                    n = 2 * h + i
                    pe.wait_ge(r_z, n + 1)
                    if n:
                        pe.wait_ge(r_am, n)
                    for l in range(NL):
                        mm(psum[:, 5 + l // 4, (l % 4) * P:(l % 4 + 1) * P], ee[:, l, :], qe[:, l, :])
                    if i == 1:
                        wait(pe, r_os, h)
                        mm(psum[:, 7, 0:P], ke7, qe[:, NL, :])
                    mm(psum[:, 6, 384:512], qkTh[:, 1, i * P:(i + 1) * P], qkTh[:, 0, i * P:(i + 1) * P]).then_inc(r_s, 1)
                pe.wait_ge(r_am, 2 * h + 2)
                mm(psum[:, 7, P:2 * P], am[:, 0, :], hin[:, 2, 0, c])
                mm(psum[:, 7, 2 * P:3 * P], am[:, 1, :], hin[:, 2, 1, c], True, False)
                mm(psum[:, 7, 2 * P:3 * P], am[:, 2, :], hin[:, 2, 0, c], False, True).then_inc(r_o, 1)
            pe.wait_ge(g_d, 2)
            turn(1, hin[:, 0, :, :])
            pe.wait_ge(t_x, 8)
            accumulate(Q_HOUT, 2)
            pe.wait_ge(p_res, 6)
            gate(1, 1)
            norm(3, 3, gates=2)
            pe.wait_ge(n_x, 16)

            def mlp2_hidden(t, gb):
                pe.wait_ge(gate_done, 2 * t + (gb + 2))
                for q in range(2):
                    for i in range(TT):
                        ins = te.transpose(psum[:, 6, q * T + i * P:q * T + (i + 1) * P], gat[:, i, q * P:(q + 1) * P], ident)
                ins.then_inc(h_turned, 1)

            def mlp2(q0, u0, hb, gb, m0=None):
                open_acc()
                up(q0, u0)
                pe.wait_ge(gate_done, gb + 2)
                if m0 is not None:
                    ada(m0)
                mlp2_hidden(0, gb)
                with pe.Fori(1, N_FF2) as t:
                    if m0 is not None:
                        pe.wait_ge(ada_saved, t + m0)
                    up(t + q0, t + u0)
                    pe.wait_ge(h_lo, t + hb)
                    down(t + (q0 - 1), 1)
                    pe.wait_ge(gate_done, 2 * t + (gb + 2))
                    if m0 is not None:
                        ada(t + m0)
                    mlp2_hidden(t, gb)
                pe.wait_ge(h_lo, hb + N_FF2)
                down(q0 + N_FF2 - 1, 1, last=True)
                pe.wait_ge(used[3], q0 + N_FF2)
                pe.nop().then_inc(acc_done, 1)

            mlp2(Q_F2A, U_F2A, HT_F2A, 0, M_L2)
            norm(4, 4, ada_upto=M_L3 + 1)
            pe.wait_ge(n_x, 20)
            for t in range(N_KV):
                project(Q_KV + t, G_KV + 2 * t, 384)
                wait(pe, ada_saved, M_L3 + 1 + t)
                ada(M_L3 + 1 + t)
            norm(5, None, ada_upto=M_L3 + 3)
            pe.wait_ge(evac_a, G_Q)
            pe.wait_ge(evac_d, G_Q)
            pe.wait_ge(n_x, 24)
            project(Q_NQ, G_Q)
            for j in range(2):
                for h in range(NKV):
                    for i in range(TT):
                        for r in range(2):
                            ins = mm(psum[64 * r:64 * r + 64, 5 + j, h * P + i * 64:h * P + i * 64 + 64],
                                     kv[:, i, j, h, :], ident[:, r:P:2])
            ins.then_inc(k_["even"], 1)
            pe.wait_ge(nsa_in, 64)
            for i in range(TT):
                for k in range(KD):
                    for x in (xhi, xlo):
                        ins = mm(psum[:, 4, 48 * i:48 * i + 48], x[:, k, i * P:(i + 1) * P].bitcast(F32), wgs[:, k, :],
                                 k == 0 and x is xhi, k == KD - 1 and x is xlo)
            ins.then_inc(k_["g"], 1)
            pe.wait_ge(k_["flat"], 1)
            for s in range(4):
                pe.wait_ge(raw_full[s], 32 * Q_CMP + 32)
            for j in range(2):
                for hh in range(2):
                    for k in range(16):
                        w1 = raw[:, 2 * j + k // 8, :].rearrange("p (k n) -> p k n", k=8)[:, k % 8, hh * P:(hh + 1) * P]
                        ins = mm(psum[:, 7, (2 * j + hh) * 60:(2 * j + hh + 1) * 60], w1,
                                 fl[:, j, k, :, :].rearrange("p c h -> p (c h)"), k == 0, k == 15)
                        if hh == 1 and k % 8 == 7:
                            ins.then_inc(used[2 * j + k // 8], 1)
            pe.wait_ge(used[3], Q_CMP + 1)
            pe.nop().then_inc(k_["hid"], 1)
            pe.wait_ge(k_["hids"], 1)
            pe.wait_ge(k_["gs"], 1)
            for j in range(2):
                for hh in range(2):
                    ins = mm(psum[0:60, 4, 256 + 64 * j:320 + 64 * j], hid[:, j, hh, :], w2s[:, j, hh, :], hh == 0, hh == 1)
            ins.then_inc(k_["kc"], 1)
            pe.wait_ge(k_["kcs"], 1)
            selv = cst("selv").rearrange("p (h m) -> p h m", h=2)
            for j in range(2):
                ins = mm(psum[:, 5 + j, 0:DN], selv[0:60, j, :], kcv[0:60, 1, :])
            ins.then_inc(k_["vb"], 1)
            pe.wait_ge(k_["kcd"], 1)
            te.transpose(psum[:, 7, 256:316], kcd[0:60, :, :].rearrange("p j d -> p (j d)"), ident[0:60, 0:60]).then_inc(k_["kct"], 1)
            ada(M_L3 + 3)
            pe.wait_ge(k_["krope"], 1)
            for b in range(2):
                for h in range(NKV):
                    for i in range(TT):
                        x = b * NKV + h
                        ins = te.transpose(psum[:, x // 2, (x % 2) * T + i * P:(x % 2) * T + (i + 1) * P],
                                           nkd[:, i, b, h, :, :].rearrange("p r d -> p (r d)"), ident)
            ins.then_inc(k_["kT"], 1)
            for j, (src, x, b0) in enumerate((("qn", nq, 0), ("qr", nqr, 4))):
                pe.wait_ge(k_[src], 1)
                if j == 0:
                    pe.wait_ge(k_["kTs"], 4)
                else:
                    pe.wait_ge(k_["kcts"], 1)
                    pe.wait_ge(k_["vbs"], 1)
                    pe.wait_ge(ada_saved, M_L3 + 4)
                for a2 in range(8):
                    for i in range(TT):
                        ins = te.transpose(psum[:, b0 + a2 // 2, (a2 % 2) * T + i * P:(a2 % 2) * T + (i + 1) * P],
                                           x[:, i, 2 * a2:2 * a2 + 2, :].rearrange("p h d -> p (h d)"), ident)
                ins.then_inc(k_["qT" if j == 0 else "qrT"], 1)
            pe.wait_ge(k_["qrTs"], 4)
            gate(2, 2)
            pe.wait_ge(k_["qTs"], 4)
            pe.wait_ge(k_["kcts"], 1)
            for i in range(TT):
                for hq in range(NH):
                    r = 64 * (hq % 2)
                    ins = mm(psum[:, 2 * i + hq % 2, hq // 2 * 16:hq // 2 * 16 + NCMP], nqT[r:r + 64, hq // 2, i * P:(i + 1) * P],
                             kcT[r:r + 64, :].rearrange("p (c h) -> p h c", h=NKV)[:, hq // NG, :])
            ins.then_inc(k_["cs"], 1)
            pe.wait_ge(k_["cp"], 1)
            for i in range(TT):
                for j in range(2):
                    ins = te.transpose(psum[:, 2, (2 * i + j) * P:(2 * i + j + 1) * P],
                                       pc[:, i, 8 * j:8 * j + 8, :].rearrange("p h c -> p (h c)"), ident)
            ins.then_inc(k_["cT"], 1)
            pe.wait_ge(k_["cTs"], 1)
            pe.wait_ge(k_["vbs"], 1)
            pe.wait_ge(bg_saved, 3)
            for i in range(TT):
                for j in range(2):
                    ins = mm(psum[:, 4 + 2 * i + j, :], pcT[:, 2 * i + j, :], vbd[:, j, :, :].rearrange("p h d -> p (h d)"))
            ins.then_inc(k_["co"], 1)
            pe.wait_ge(k_["cos"], 2)
            for w in range(2 * NH + 2):
                if w < 2 * NH:
                    u = w
                    hq, b = u // 2, u % 2
                    r = 64 * (hq % 2)
                    if u >= 2:
                        pe.wait_ge(w_m, u - 1)
                    kT = nkT[r:r + 64, b, hq // NG, :]
                    mm(psum[:, u % 2, 0:P], nqrT[r:r + 64, hq // 2, 0:P], kT[:, 0:P])
                    mm(psum[:, u % 2, P:384], nqrT[r:r + 64, hq // 2, P:T], kT).then_inc(w_s, 1)
                if 1 <= w <= 2 * NH:
                    u = w - 1
                    pe.wait_ge(w_e, u + 1)
                    if u >= 2:
                        pe.wait_ge(w_pts, u - 1)
                    for b in range(3):
                        ins = te.transpose(psum[:, 2 + u % 2, b * P:(b + 1) * P], pb2[:, u % 2, b * P:(b + 1) * P], ident)
                    ins.then_inc(w_pt, 1)
                if 2 <= w:
                    u = w - 2
                    hq, b = u // 2, u % 2
                    pe.wait_ge(w_pts, u + 1)
                    if u >= 2:
                        pe.wait_ge(w_os, u - 1)
                    o = psum[:, 4 + u % 2, :]
                    vv = kv[:, :, 3 + 2 * b, hq // NG, :]
                    mm(o[:, 0:DN], pT2[:, u % 2, 0:P], vv[:, 0, :])
                    mm(o[:, DN:2 * DN], pT2[:, u % 2, P:T], vv[:, 0, :], True, False)
                    mm(o[:, DN:2 * DN], pT2[:, u % 2, T:384], vv[:, 1, :], False, True).then_inc(w_o, 1)
            pe.wait_ge(w_os, 2 * NH)
            turn(2, ob2.rearrange("p i h d -> p i (h d)"))
            pe.wait_ge(t_x, 12)
            accumulate(Q_NOUT, 4)
            for b in (4, 5):
                wait(pe, ada_saved, M_L3 + b)
                ada(M_L3 + b)
            pe.wait_ge(p_res, 10)
            pe.wait_ge(ada_saved, M_END)
            gate(3, 3)
            norm(6, 5, gates=4)
            pe.wait_ge(n_x, 28)
            mlp2(Q_F2B, U_F2B, HT_F2B, 22)


_INS = ["x", "norm_mix_pre", "norm_mix_post", "norm_ffn_pre", "norm_ffn_post", "w_up", "w_down", "attn_w_qkv", "attn_w_o",
        "c_2", "ada_w_2", "ada_b_2", "norm_mix_2", "norm_ffn_2", "hgrn_w_in_2", "hgrn_out_norm_2", "hgrn_w_out_2",
        "kv_ada_w_2", "kv_ada_b_2", "kv_norm_2", "nsa_w_kv_2", "nsa_k_norm_2", "cmp_pos_2", "cmp_w1_2", "cmp_w2_2",
        "nsa_w_q_2", "nsa_q_norm_2", "nsa_w_out_2", "ffn_w_in_2", "ffn_w_out_2"]


def kernel(**inputs):
    import concourse.bacc as bacc
    from concourse.bass_utils import run_bass_kernel_spmd as run

    nc = bacc.Bacc("TRN2", target_bir_lowering=False, num_devices=1, dynamic_dma_scratch_size=2048)
    arrays, args = {}, {}
    given = {n: np.ascontiguousarray(inputs[n]) for n in _INS}
    for name, x in {**given, **constants()}.items():
        arrays["in_" + name] = x
        args[name] = nc.dram_tensor("in_" + name, x.shape, mybir.dt.from_np(x.dtype), kind="ExternalInput").ap()
    out = nc.dram_tensor("out_0", (1, T, D), F32, kind="ExternalOutput").ap()
    build(nc, args, out)
    r = run(nc, [arrays], core_ids=[0])
    return r.results[0]["out_0"]
```

```python
from contextlib import ExitStack

import numpy as np
import concourse.bass as bass
from concourse import mybir

F32 = mybir.dt.float32
F32R = mybir.dt.float32r
BF16 = mybir.dt.bfloat16
ALU = mybir.AluOpType
ACT = mybir.ActivationFunctionType
AX = mybir.AxisListType.X

P = 128
T = 256
TT = T // P
D = 1024
KD = D // P
H1, DH1 = 8, 128
FF1 = 4 * D
HH, DK = 8, 128
LEVELS = [64, 32, 16, 8, 4, 2, 1]
NL = len(LEVELS)
HIN_ORDER = (1, 0, 3, 2)
NH, NKV, NG, DN = 16, 4, 4, 64
FFN = -(-8 * D // (3 * 256)) * 256
CB, CS = 32, 16
NCMP = T // CS - CB // CS + 1
CHID = 256
EPS = 1e-6
NEG = -1e30

N_QKV, N_ACC, N_FF1, N_HIN, N_FF2, N_KV, N_Q = 3, 1, FF1 // 512, 4, FFN // 256, 2, 1
Q_QKV = 0
Q_WO = Q_QKV + N_QKV
Q_FF1 = Q_WO + N_ACC
Q_HIN = Q_FF1 + N_FF1
Q_HOUT = Q_HIN + N_HIN
Q_F2A = Q_HOUT + N_ACC
Q_KV = Q_F2A + N_FF2
Q_NQ = Q_KV + N_KV
Q_CMP = Q_NQ + N_Q
Q_NOUT = Q_CMP + 1
Q_F2B = Q_NOUT + N_ACC
Q_END = Q_F2B + N_FF2

G_HIN = 2 * N_QKV
G_KV = G_HIN + 2 * N_HIN
G_Q = G_KV + 2 * N_KV
G_END = G_Q + 2 * N_Q
U_F2A = N_FF1
U_F2B = U_F2A + N_FF2
HT_F2A = 2 * N_FF1
HT_F2B = HT_F2A + N_FF2

M_L0, M_L1, M_L2, M_KV, M_L3, M_END = 0, 6, 12, 18, 22, 28
LCOL = {0: 4 * M_L0, 1: 4 * M_L1, 2: 4 * M_L2, "kv": 4 * M_KV, 3: 4 * M_L3}

VR = {"mix_pre": 0, "ffn_pre": 8, "mix2": 16, "ffn2": 32, "kvn": 48, "c": 56, "pos": 64}


def constants():
    t = np.arange(P)
    ident = np.eye(P, dtype=np.float32)
    q, k = t[:, None], t[None, :]
    dist = np.concatenate([np.where(k <= q, k - q, NEG), k - (q + P) + 0 * q, np.where(k <= q, k - q, NEG)], 1)
    caus = np.concatenate([np.where(k <= q, 0, NEG), 0.0 * (k + q), np.where(k <= q, 0, NEG)], 1)
    ml = np.zeros((P, NL + 2, P), np.float32)
    mask = np.zeros((P, NL + 1, P), np.float32)
    u, x = t[:, None], t[None, :]
    for i, m in enumerate(LEVELS):
        mid = x // (2 * m) * (2 * m) + m
        second = x >= mid
        ml[:, i] = np.where(second, (u >= mid) & (u <= x), (u > x) & (u < mid))
        mask[:, i] = (u // (2 * m) == x // (2 * m)) & (u < mid) & (x >= mid)
    mask[:, NL] = ident
    ml[:, NL] = u > x
    ml[:, NL + 1] = u <= x
    inv = 1.0 / (10000.0 ** (np.arange(0, DN, 2, dtype=np.float32) / np.float32(DN)))
    ang = np.arange(T, dtype=np.float32)[:, None] * inv[None, :].astype(np.float32)
    rope = np.stack([np.cos(ang), np.sin(ang)], 1).astype(np.float32)
    rope = rope.reshape(TT, P, 2 * (DN // 2)).transpose(1, 0, 2).reshape(P, -1)
    tok = np.arange(T).reshape(TT, P).T
    seen = (np.arange(NCMP) * CS + CB - 1)[None, None, :] <= tok[:, :, None]
    cmask = np.stack([np.where(seen, 0.0, NEG), seen.astype(np.float64)], 1).reshape(P, -1)
    selv = np.zeros((P, 2, 8, 16), np.float32)
    for c in range(NCMP):
        for h in range(NKV):
            for hq in range(NH):
                if hq // NG == h:
                    selv[c * NKV + h, hq // 8, hq % 8, c] = 1
    bm = (t[:, None] // 16 == np.arange(8)[None, :]).astype(np.float32)
    f = lambda a: np.ascontiguousarray(a.reshape(P, -1), dtype=np.float32)
    return {
        "k_small": f(np.concatenate([ident, rope, cmask, bm, selv.reshape(P, -1)], 1)),
        "k_dist": f(np.concatenate([dist, caus], 1)),
        "k_levels": f(np.concatenate([ml.reshape(P, -1), mask.reshape(P, -1)], 1)),
    }


SMALL = {}
_o = 0
for _n, _w in (("ident", P), ("rope", TT * DN), ("cmask", 2 * TT * NCMP), ("bm", 8), ("selv", 256)):
    SMALL[_n] = (_o, _o + _w)
    _o += _w
SMALL_W = _o
LEV_W = (NL + 2) * P + (NL + 1) * P


def build(nc, a, out):
    with ExitStack() as ctx:
        def sb(name, shape, dt=F32):
            return ctx.enter_context(nc.sbuf_tensor(name, shape, dt))

        def sem(name):
            return ctx.enter_context(nc.semaphore(name))

        raw = sb("raw", [P, 4, 2048])
        whi = sb("whi", [P, 4, 2048], F32R)
        wlo = sb("wlo", [P, 4, 2048], F32R)
        adaw = sb("adaw", [P, 2, 2048])
        adaacc = sb("adaacc", [P, 512])
        xhi = sb("xhi", [P, KD, T], F32R)
        xlo = sb("xlo", [P, KD, T], F32R)
        hhi = sb("hhi", [P, 4, T], F32R)
        hlo = sb("hlo", [P, 4, T], F32R)
        res = sb("res", [P, TT, D])
        gain_b = sb("gain_b", [P, D])
        small = sb("small", [P, SMALL_W])
        vcol = sb("vcol", [P, 96])
        bcol = sb("bcol", [P, 4 * M_END])
        adacol = sb("adacol", [P, 4 * M_END])
        gs = sb("gs", [P, KD])
        sh = sb("sh", [P, KD])
        cact = sb("cact", [P, KD])
        ones = sb("ones", [P, 1])
        stat = sb("stat", [P, 64])
        ss = stat[:, 0:2]
        rstd = stat[:, 2:4]
        mhalf = stat[:, 4:36]
        onb = sb("onb", [P, DK])
        zrow = sb("zrow", [1, 512], BF16)
        identb = sb("identb", [P, P], BF16)
        causb = sb("causb", [P, 384], BF16)
        AR = 16592
        arena = sb("arena", [P, AR])
        psum = ctx.enter_context(nc.psum_tensor("psum", [P, 8, 512], F32))

        def cst(name):
            lo, hi_ = SMALL[name]
            return small[:, lo:hi_]
        ident = cst("ident")

        def area(lo, *shape):
            n = int(np.prod(shape))
            v = arena[:, lo:lo + n]
            if len(shape) == 1:
                return v
            names = "abcde"[:len(shape)]
            return v.rearrange(f"p ({' '.join(names)}) -> p {' '.join(names)}", **{k: s for k, s in zip(names, shape)})

        y = area(AR - 4096, TT, D)
        xf = area(AR - 2048, KD, T)
        vrow1 = area(11600, P)
        vrow2 = area(11728, P)
        dist = area(7936, 768)
        distb = area(11860, 192).bitcast(BF16)
        slopeb = area(7168, 512).bitcast(BF16).rearrange("p (h t) -> p h t", t=P)
        qkv = area(0, TT, 3 * D)
        qkT = area(6144, 2, 512)
        pb1 = area(7936, 2, 384)
        pT1 = area(8704, 2, 384)
        ob1 = area(9472, TT, D)
        st1 = area(11520, 2, 8)
        relu = area(0, TT, 512)
        sq = area(1024, 4, T)
        sil = area(2048, TT, T)
        gat = area(2560, TT, T)
        hin = area(0, 4, TT, D)
        hk = area(8192, TT, D)
        lev = area(10240, LEV_W)
        ML = lev[:, 0:(NL + 2) * P].rearrange("p (l t) -> p l t", t=P)
        MK = lev[:, (NL + 2) * P:LEV_W].rearrange("p (l t) -> p l t", t=P)
        spare = adaw[:].rearrange("p j (c l t) -> p (j c) l t", c=2, t=P)
        ee = [area(12416, NL + 1, P), area(13440, NL + 1, P)]
        qe = [area(14464, NL + 1, P), spare[:, 0]]
        ke = [spare[:, 1], spare[:, 2]]
        pm = spare[:, 3]
        qkTh = [area(15488, 2, T), adaacc[:].rearrange("p (j t) -> p j t", j=2)]
        am = [area(16000, 3, P), gain_b[:, 0:384].rearrange("p (j t) -> p j t", j=3)]
        ke7 = [area(16384, P), gain_b[:, 384:512]]
        ghi, glo = [x[:].rearrange("p k t -> p (k t)").rearrange("p (i n) -> p i n", i=TT) for x in (xhi, xlo)]
        MLr = hhi[:].rearrange("p k t -> p (k t)")
        MLx = hlo[:, 0, 0:P]
        hs = area(16512, 64)
        hsq = gain_b[:, 512:512 + 2 * DK].rearrange("p (i d) -> p i d", i=TT)
        kv = area(0, TT, 6, NKV, DN)
        nq = area(3072, TT, NH, DN)
        nqT = area(5120, 8, T)
        nkT = area(7168, 2, NKV, T)
        nqrT = area(9216, 8, T)
        nt1 = area(11264, 2048)
        kt2 = area(11264, 2, NKV, P)
        fl = area(5120, 2, CB // 2, NCMP, NKV)
        pT2 = area(5120, 2, 384)
        nqr = area(9216, TT, NH, DN)
        nkd = area(9216, TT, 2, NKV, 2, DN)
        hid = area(13312, 2, 2, NCMP * NKV)
        hidt = area(16080, 2, CHID)
        kcv = area(13552, 2, DN)
        kcd = area(13680, 2, DN)
        kcT = area(13808, NCMP * NKV)
        vbd = area(13872, 2, 8, DN)
        w2s = area(14896, 2, 2, DN)
        wgs = area(15152, KD, 48)
        gat3 = area(15536, TT, 48)
        knb = area(15632, 4, DN)
        nst = area(15888, 192)
        pc = area(11264, TT, NH, 16)
        pb2 = area(12544, 2, 384)
        pcT = area(16080, 4, P)
        ob2 = area(3072, TT, NH, DN)

        raw_full = [sem(f"raw_full{s}") for s in range(4)]
        hi_ready = [sem(f"hi_ready{s}") for s in range(4)]
        lo_ready = [sem(f"lo_ready{s}") for s in range(4)]
        used = [sem(f"used{s}") for s in range(4)]
        ada_full = [sem(f"ada_full{s}") for s in range(2)]
        ada_used = [sem(f"ada_used{s}") for s in range(2)]
        ada_step, ada_sum, ada_turned, ada_saved = sem("ada_step"), sem("ada_sum"), sem("ada_turned"), sem("ada_saved")
        consts_in, x_in, vec_in = sem("consts_in"), sem("x_in"), sem("vec_in")
        vec_turned, vec_saved, c_ready, ones_set = sem("vec_turned"), sem("vec_saved"), sem("c_ready"), sem("ones_set")
        gain_in, gain_free = sem("gain_in"), sem("gain_free")
        n_sq, n_ms, n_rstd, n_y, n_turned, n_affine, n_hi, n_x = [sem("n_" + s) for s in ("sq", "ms", "rstd", "y", "turned", "affine", "hi", "x")]
        aff_ready = sem("aff_ready")
        p_sq, p_ms, p_rstd, p_res = [sem("p_" + s) for s in ("sq", "ms", "rstd", "res")]
        proj_done, evac_a, evac_d = sem("proj_done"), sem("evac_a"), sem("evac_d")
        acc_done = sem("acc_done")
        up_done, act_done, gate_done, h_turned, h_sq, h_hi, h_lo = [sem(s) for s in ("up_done", "act_done", "gate_done", "h_turned", "h_sq", "h_hi", "h_lo")]
        bg_turned, bg_saved = sem("bg_turned"), sem("bg_saved")
        a_qk, a_qks, a_s, a_m, a_e, a_pt, a_pts, a_o, a_os = [sem("a_" + s) for s in ("qk", "qks", "s", "m", "e", "pt", "pts", "o", "os")]
        t_turned, t_hi, t_x = sem("t_turned"), sem("t_hi"), sem("t_x")
        lev_in, onb_in, dist_in, bias_ready = sem("lev_in"), sem("onb_in"), sem("dist_in"), sem("bias_ready")
        g_a, g_d, g_f = sem("g_a"), sem("g_d"), sem("g_f")
        r_qk, r_qks, r_e, r_ee, r_z, r_k, r_s, r_m, r_am, r_o, r_os = [
            sem("r_" + s) for s in ("qk", "qks", "e", "ee", "z", "k", "s", "m", "am", "o", "os")]
        g_hi, g_lo, ml_ready, s_zero = sem("g_hi"), sem("g_lo"), sem("ml_ready"), sem("s_zero")
        r_ms, r_rs, r_n = sem("r_ms"), sem("r_rs"), sem("r_n")
        nsa_in, knb_in = sem("nsa_in"), sem("knb_in")
        dve, actc, poolc = sem("dve_chain"), sem("act_chain"), sem("pool_chain")
        k_ = {n: sem("k_" + n) for n in ("even", "evens", "flat", "hid", "hidst", "hidT", "hids", "kc", "kcs", "sq", "rs", "kcd", "kct", "kcts",
                                         "vb", "vbs", "krope", "kT", "kTs", "g", "gs", "qsq", "qrs", "qn", "qT", "qTs", "qr", "qrT", "qrTs",
                                         "cs", "cm", "ce", "cp", "cT", "cTs", "co", "cos")}
        w_s, w_m, w_e, w_pt, w_pts, w_o, w_os = [sem("w_" + s) for s in ("s", "m", "e", "pt", "pts", "o", "os")]
        out_done = sem("out_done")

        def wait(eng, s, v):
            if not isinstance(v, int) or v > 0:
                eng.wait_ge(s, v)

        class Chain:
            def __init__(self, eng, s):
                self.eng, self.s, self.n = eng, s, 0

            def __call__(self, ins):
                self.n += 1
                ins.then_inc(self.s, 1)
                self.eng.wait_ge(self.s, self.n)

        block = ctx.enter_context(nc.Block())

        @block.sync
        def _(sp):
            def free_slot(s, n):
                if isinstance(n, int) and n == Q_CMP + 1:
                    sp.wait_ge(used[s], n)
                elif not isinstance(n, int) or n > 0:
                    wait(sp, hi_ready[s], n)
                    wait(sp, lo_ready[s], n)

            def wide(w, s, n, nb, width=512):
                free_slot(s, n)
                v = w.rearrange("(h kt p) n -> h p kt n", h=2, p=P)[s % 2]
                dst = raw[:, s, 0:4 * width].rearrange("p (k n) -> p k n", k=4)
                sp.dma_start(dst, v[:, :, bass.ds(nb * width, width)]).then_inc(raw_full[s], 32)

            def deep(w, s, n, g, kt=2):
                free_slot(s, n)
                v = w.rearrange("(r p) n -> p r n", p=P)
                dst = raw[:, s, 0:kt * D].rearrange("p (k n) -> p k n", k=kt)
                sp.dma_start(dst, v[:, bass.ds(g * kt, kt), :]).then_inc(raw_full[s], 32)

            def gated(w, s, n, fb):
                free_slot(s, n)
                v = w.rearrange("(h kt p) n -> h p kt n", h=2, p=P)[s % 2]
                dst = raw[:, s, :].rearrange("p (k n) -> p k n", k=4)
                sp.dma_start(dst[:, :, 0:256], v[:, :, bass.ds(fb * 256, 256)]).then_inc(raw_full[s], 16)
                sp.dma_start(dst[:, :, 256:512], v[:, :, bass.ds(fb * 256 + FFN, 256)]).then_inc(raw_full[s], 16)

            def ada(w, half, m, nb):
                if not isinstance(m, int) or m > 0:
                    sp.wait_ge(ada_used[half], m)
                v = w.rearrange("(h kt p) n -> h p kt n", h=2, p=P)[half]
                dst = adaw[:, half, :].rearrange("p (k n) -> p k n", k=4)
                sp.dma_start(dst, v[:, :, bass.ds(nb * 512, 512)]).then_inc(ada_full[half], 16)

            sp.dma_start(res[:], a["x"][0].rearrange("(i p) d -> p i d", p=P)).then_inc(x_in, 16)
            sp.dma_start(small[:], a["k_small"]).then_inc(consts_in, 16)
            sp.dma_start(dist, a["k_dist"]).then_inc(dist_in, 16)
            w = a["attn_w_qkv"][0]
            for s in range(4):
                wide(w, s, 0, s // 2)
            with sp.Fori(1, N_QKV) as t:
                for s in range(4):
                    wide(w, s, t + Q_QKV, 2 * t + s // 2)
            for s in range(4):
                deep(a["attn_w_o"][0], s, Q_WO, s)
            up, dn = a["w_up"][0], a["w_down"][0]
            for s in (0, 1):
                wide(up, s, Q_FF1, 0)

            def mlp1(t, l, m, nb):
                wide(up, 0, t + Q_FF1 + 1, t + 1)
                ada(a["ada_w_2"][l], 0, m, nb)
                ada(a["ada_w_2"][l], 1, m, nb)
                wide(up, 1, t + Q_FF1 + 1, t + 1)
                deep(dn, 2, t + Q_FF1, 2 * t)
                deep(dn, 3, t + Q_FF1, 2 * t + 1)
            mlp1(0, 0, 0, 0)
            with sp.Fori(1, 6) as t:
                mlp1(t, 0, t, t)
            mlp1(6, 1, 6, 0)
            ada(a["ada_w_2"][1], 0, 7, 1)
            ada(a["ada_w_2"][1], 1, 7, 1)
            deep(dn, 2, Q_FF1 + 7, 14)
            deep(dn, 3, Q_FF1 + 7, 15)
            w = a["hgrn_w_in_2"][0]
            for t, sec in enumerate((*HIN_ORDER, None)):
                for s in range(4):
                    if sec is not None:
                        wide(w, s, Q_HIN + t, 2 * sec + s // 2)
                    else:
                        deep(a["hgrn_w_out_2"][0], s, Q_HOUT, s)
                    if t and s < 2:
                        ada(a["ada_w_2"][1], s, M_L1 + 1 + t, 1 + t)

            def mlp2(layer, q0, t, ada_a=None, last=False):
                up2, dn2 = a["ffn_w_in_2"][layer], a["ffn_w_out_2"][layer]
                if not last:
                    gated(up2, 0, t + q0 + 1, t + 1)
                if ada_a:
                    ada(ada_a[0], 0, ada_a[1], ada_a[2])
                    ada(ada_a[0], 1, ada_a[1], ada_a[2])
                if not last:
                    gated(up2, 1, t + q0 + 1, t + 1)
                deep(dn2, 2, t + q0, 2 * t, kt=1)
                deep(dn2, 3, t + q0, 2 * t + 1, kt=1)

            gated(a["ffn_w_in_2"][0], 0, Q_F2A, 0)
            gated(a["ffn_w_in_2"][0], 1, Q_F2A, 0)
            sp.wait_ge(r_am, 2 * HH)
            mlp2(0, Q_F2A, 0, (a["ada_w_2"][2], M_L2, 0))
            with sp.Fori(1, 6) as t:
                mlp2(0, Q_F2A, t, (a["ada_w_2"][2], t + M_L2, t))
            with sp.Fori(6, 10) as t:
                mlp2(0, Q_F2A, t, (a["kv_ada_w_2"], t + M_L2, t - 6))
            mlp2(0, Q_F2A, 10, (a["ada_w_2"][3], M_L3, 0), last=True)
            w = a["nsa_w_kv_2"]
            for s in range(4):
                wide(w, s, Q_KV, s // 2, 384)
            for s in range(4):
                wide(w, s, Q_KV + 1, 2 + s // 2, 384)
                if s < 2:
                    ada(a["ada_w_2"][3], s, M_L3 + 1, 1)
            for s in range(4):
                wide(a["nsa_w_q_2"][0], s, Q_NQ, s // 2)
                if s < 2:
                    ada(a["ada_w_2"][3], s, M_L3 + 2, 2)
            for s in range(4):
                free_slot(s, Q_CMP)
                sp.dma_start(raw[:, s, :].rearrange("p (k n) -> p k n", k=8),
                             a["cmp_w1_2"][s // 2].rearrange("(g k p) n -> g p k n", g=2, p=P)[s % 2]).then_inc(raw_full[s], 32)
            for b in (3, 4, 5):
                for half in range(2):
                    ada(a["ada_w_2"][3], half, M_L3 + b, b)
                if b == 3:
                    for s in range(4):
                        deep(a["nsa_w_out_2"][0], s, Q_NOUT, s)
                elif b == 4:
                    for s in range(2):
                        gated(a["ffn_w_in_2"][1], s, Q_F2B, 0)
            with sp.Fori(0, 10) as t:
                mlp2(1, Q_F2B, t)
            mlp2(1, Q_F2B, 10, last=True)
            for i in range(TT):
                sp.wait_ge(p_res, 11 + i)
                sp.dma_start(out[0].rearrange("(i p) d -> p i d", p=P)[:, i, :], res[:, i, :]).then_inc(out_done, 16)
            sp.wait_ge(out_done, 32)

        @block.gpsimd
        def _(pool):
            gp = nc.gpsimd
            chain = Chain(pool, poolc)
            gp.memset(mhalf, -0.5)
            gp.memset(zrow[:], 0.0)
            chain(gp.memset(ones[:], 1.0))
            pool.nop().then_inc(ones_set, 1)
            for name, src in (("mix_pre", a["norm_mix_pre"]), ("ffn_pre", a["norm_ffn_pre"]), ("mix2", a["norm_mix_2"]),
                              ("ffn2", a["norm_ffn_2"]), ("c", a["c_2"])):
                r = src.rearrange("l (k p) -> (l k) p", p=P)
                gp.dma_start(vrow1[VR[name]:VR[name] + r.shape[0], :], r).then_inc(vec_in, 16)
            gp.dma_start(vrow1[VR["kvn"]:VR["kvn"] + 8, :], a["kv_norm_2"].rearrange("(k p) -> k p", p=P)).then_inc(vec_in, 16)
            gp.dma_start(vrow1[VR["pos"]:VR["pos"] + 32, :],
                         a["cmp_pos_2"].rearrange("j (a r) d -> (j a) (r d)", r=2)).then_inc(vec_in, 16)
            gp.dma_start(vrow2[0:72, :], a["ada_b_2"][0:3].rearrange("l (k p) -> (l k) p", p=P)).then_inc(vec_in, 16)
            gp.dma_start(vrow2[72:88, :], a["kv_ada_b_2"].rearrange("(k p) -> k p", p=P)).then_inc(vec_in, 16)
            gp.dma_start(vrow2[88:112, :], a["ada_b_2"][3:4].rearrange("l (k p) -> (l k) p", p=P)).then_inc(vec_in, 16)
            gp.dma_start(onb[:], a["hgrn_out_norm_2"][0].partition_broadcast(P)).then_inc(onb_in, 16)
            gp.dma_start(gain_b[:], a["norm_mix_post"][0].partition_broadcast(P)).then_inc(gain_in, 16)

            def rsqrt(src, dst, tmp, n, mean, done):
                chain(gp.tensor_scalar(tmp, src, mean, EPS, ALU.mult, ALU.add))
                gp.tensor_tensor(dst, tmp, n, ALU.pow).then_inc(done, 1)

            def norm(j):
                pool.wait_ge(n_sq, 2 * j + 2)
                rsqrt(ss, rstd, stat[:, 40:42], mhalf[:, 0:2], 1.0 / D, n_rstd)

            def post(k):
                pool.wait_ge(p_sq, 2 * k + 2)
                rsqrt(stat[:, 36:38], stat[:, 38:40], stat[:, 42:44], mhalf[:, 0:2], 1.0 / D, p_rstd)

            norm(0)
            post(0)
            pool.wait_ge(p_res, 2)
            gp.dma_start(gain_b[:], a["norm_ffn_post"][0].partition_broadcast(P)).then_inc(gain_in, 16)
            norm(1)
            post(1)
            pool.wait_ge(p_res, 4)
            gp.dma_start(lev, a["k_levels"]).then_inc(lev_in, 16)
            norm(2)
            pool.wait_ge(ada_used[0], M_L2)
            pool.wait_ge(ada_used[1], M_L2)
            for n in range(2 * HH):
                h, i = n // 2, n % 2
                if i == 0:
                    pool.wait_ge(r_qks, h + 1)
                pool.wait_ge(r_ee, n + 1)
                if n >= 2:
                    pool.wait_ge(r_s, n - i)
                kT = qkTh[h % 2][:, 1, i * P:(i + 1) * P]
                if i == 0:
                    gp.tensor_tensor(ke7[h % 2], ee[0][:, NL, :], kT, ALU.mult)
                gp.tensor_tensor(ke[i][:, 0:NL, :], ee[i][:, 0:NL, :], kT.unsqueeze(1).to_broadcast([P, NL, P]),
                                 ALU.mult).then_inc(r_k, 1)
            pool.wait_ge(r_ms, HH)
            rsqrt(hs[:, 0:16], hs[:, 16:32], hs[:, 32:48], mhalf[:, 0:16], 1.0 / DK, r_rs)
            norm(3)
            norm(4)
            pool.wait_ge(n_x, 24)
            pool.wait_ge(n_turned, 20)
            with nc.allow_non_contiguous_dma(reason="small operands"):
                gp.dma_start(knb[:, 0:3, :], a["nsa_k_norm_2"].rearrange("j d -> (j d)").partition_broadcast(P)
                             .rearrange("p (j d) -> p j d", d=DN)).then_inc(knb_in, 16)
                gp.dma_start(knb[:, 3, :], a["nsa_q_norm_2"][0].partition_broadcast(P)).then_inc(knb_in, 16)
                gp.dma_start(wgs, a["nsa_w_q_2"][0].rearrange("(k p) n -> p k n", p=P)[:, :, D:D + 48]).then_inc(nsa_in, 16)
                gp.dma_start(w2s, a["cmp_w2_2"].rearrange("j (h p) d -> p j h d", p=P)).then_inc(nsa_in, 16)
            pool.wait_ge(k_["sq"], 1)
            rsqrt(nst[:, 16:32], nst[:, 32:48], nst[:, 48:64], mhalf[:, 0:16], 1.0 / DN, k_["rs"])
            pool.wait_ge(k_["sq"], 2)
            rsqrt(nst[:, 64:96], nst[:, 96:128], nst[:, 128:160], mhalf[:, 0:32], 1.0 / DN, k_["rs"])
            pool.wait_ge(k_["sq"], 3)
            rsqrt(nst[0:60, 0:1], nst[0:60, 1:2], nst[0:60, 2:3], mhalf[0:60, 0:1], 1.0 / DN, k_["rs"])
            norm(5)

        @block.scalar
        def _(act):
            sc = nc.scalar
            chain = Chain(act, actc)

            def split(s, n, width=2048):
                act.wait_ge(raw_full[s], 32 * n + 32)
                if not isinstance(n, int) or n > 0:
                    act.wait_ge(used[s], n)
                sc.copy(whi[:, s, 0:width], raw[:, s, 0:width]).then_inc(hi_ready[s], 1)

            def norm(k, j, fresh=True):
                if fresh:
                    for i in range(TT):
                        if j == 0:
                            act.wait_ge(x_in, 16)
                        else:
                            act.wait_ge(p_res, 2 * (j - 1) + i + 1)
                        sc.activation(y[:, i, :], res[:, i, :], ACT.Square, accum_out=ss[:, i:i + 1]).then_inc(n_sq, 1)
                else:
                    act.wait_ge(proj_done, G_Q)
                for b in range(4):
                    act.wait_ge(n_affine, 4 * k + b + 1)
                    sc.copy(xhi[:, 2 * b:2 * b + 2, :], xf[:, 2 * b:2 * b + 2, :]).then_inc(n_hi, 1)

            def post(k):
                act.wait_ge(acc_done, k + 1)
                for i in range(TT):
                    sc.activation(y[:, i, :], psum[:, 2 * i:2 * i + 2, :].rearrange("p b n -> p (b n)"), ACT.Square,
                                  accum_out=stat[:, 36 + i:37 + i]).then_inc(p_sq, 1)

            def turn(k):
                for b in range(4):
                    act.wait_ge(t_turned, 4 * k + b + 1)
                    sc.copy(xhi[:, 2 * b:2 * b + 2, :], psum[:, 4 + b, :].rearrange("p (k t) -> p k t", k=2)).then_inc(t_hi, 1)

            def evac(g, p, dst):
                act.wait_ge(proj_done, g + 1)
                sc.copy(dst, psum[:, 2 * p, 0:dst.shape[-1]]).then_inc(evac_a, 1)

            act.wait_ge(vec_turned, 1)
            sc.copy(vcol[:], psum[:, 0, 0:96]).then_inc(vec_saved, 1)
            sc.copy(bcol[:], psum[:, 0, 128:128 + 112]).then_inc(vec_saved, 1)
            act.wait_ge(vec_saved, 1)
            sc.activation(cact[:], vcol[:, VR["c"]:VR["c"] + 8], ACT.Silu).then_inc(c_ready, 1)
            norm(0, 0)
            for s in range(4):
                split(s, Q_QKV)
            act.wait_ge(dist_in, 16)
            sc.copy(distb, dist[:, 0:384])
            sc.copy(causb[:], dist[:, 384:768])
            sc.copy(identb[:], ident)
            for h in range(H1):
                ins = sc.mul(slopeb[:, h, :], ident, 2.0 ** -(8.0 * (h + 1) / H1))
            ins.then_inc(bias_ready, 1)
            act.wait_ge(bias_ready, 1)
            with act.Fori(0, N_QKV) as t:
                for p in range(2):
                    split(2 * p, t + 1)
                    split(2 * p + 1, t + 1)
                    evac(2 * t + p, p, qkv[:, 0, bass.ds(t * 1024 + p * 512, 512)])

            for h in range(H1 + 1):
                if h < H1:
                    act.wait_ge(a_qk, h + 1)
                    if h >= 2:
                        act.wait_ge(a_s, h - 1)
                    sc.mul(qkT[:, h % 2, 0:T], psum[:, h % 2, 0:T], DH1 ** -0.5)
                    sc.copy(qkT[:, h % 2, T:2 * T], psum[:, h % 2, T:2 * T]).then_inc(a_qks, 1)
                if h >= 1:
                    g = h - 1
                    act.wait_ge(a_m, g + 1)
                    if g >= 2:
                        act.wait_ge(a_pts, g - 1)
                    m = st1[:, g % 2, :]
                    sc.activation(pb1[:, g % 2, 0:P], psum[:, 2 + g % 2, 0:P], ACT.Exp, bias=m[:, 0:1], accum_out=m[:, 2:3])
                    sc.activation(pb1[:, g % 2, P:384], psum[:, 2 + g % 2, P:384], ACT.Exp, bias=m[:, 1:2],
                                  accum_out=m[:, 3:4]).then_inc(a_e, 1)
            turn(0)
            split(0, Q_FF1)
            split(1, Q_FF1)
            post(0)
            norm(1, 1)
            split(2, Q_FF1)
            split(3, Q_FF1)

            def mlp1(t, first=False):
                split(0, t + (Q_FF1 + 1))
                act.wait_ge(up_done, t + 1)
                for i in range(TT):
                    sc.activation(relu[:, i, :], psum[:, 4 + i, :], ACT.Relu).then_inc(act_done, 1)
                split(1, t + (Q_FF1 + 1))
                if not first:
                    split(2, t + Q_FF1)
                    split(3, t + Q_FF1)
                for b in range(2):
                    act.wait_ge(h_turned, 2 * t + b + 1)
                    sc.activation(sq[:, 2 * b:2 * b + 2, :], psum[:, 6 + b, :].rearrange("p (k t) -> p k t", k=2),
                                  ACT.Square).then_inc(h_sq, 1)
                    act.wait_ge(h_sq, 2 * t + b + 1)
                    sc.copy(hhi[:, 2 * b:2 * b + 2, :], sq[:, 2 * b:2 * b + 2, :]).then_inc(h_hi, 1)
            mlp1(0, True)
            with act.Fori(1, N_FF1) as t:
                mlp1(t)
            for s in (2, 3):
                split(s, Q_HIN)
            post(1)
            norm(2, 2)
            tmp = area(12416, TT, D)

            def act_of(t):
                sec = HIN_ORDER[t]
                act.wait_ge(evac_d, G_HIN + 2 * t + 2)
                act.wait_ge(evac_a, G_HIN + 2 * t + 2)
                x = hin[:, sec, :, :]
                if sec == 1:
                    chain(sc.activation(tmp, x, ACT.Abs))
                    chain(sc.activation(tmp, tmp, ACT.Exp, scale=-1.0))
                    chain(sc.activation(tmp, tmp, ACT.Ln, bias=1.0))
                    sc.activation(hk, x, ACT.Sigmoid, scale=-1.0).then_inc(g_f, 1)
                elif sec != 2:
                    sc.activation(x, x, ACT.Silu).then_inc(g_f, 1)

            for t, sec in enumerate(HIN_ORDER):
                for p in range(2):
                    split(2 * p, Q_HIN + t + 1)
                    split(2 * p + 1, Q_HIN + t + 1)
                    evac(G_HIN + 2 * t + p, p, hin[:, sec, 0, p * 512:(p + 1) * 512])
                    if p == 0 and t:
                        act_of(t - 1)
            act_of(3)
            act.wait_ge(lev_in, 16)
            act.wait_ge(h_lo, 2 * N_FF1)
            act.wait_ge(used[3], Q_HIN)
            sc.copy(MLr, ML[:, 0:NL + 1, :].rearrange("p l t -> p (l t)"))
            sc.copy(MLx, ML[:, NL + 1, :]).then_inc(ml_ready, 1)
            act.wait_ge(g_d, 1)
            act.wait_ge(proj_done, G_KV)
            act.wait_ge(ada_turned, M_L2)
            for b in range(4):
                sc.copy(ghi[:, :, b * 256:(b + 1) * 256], hin[:, 1, :, b * 256:(b + 1) * 256]).then_inc(g_hi, 1)

            def qk_save(h):
                act.wait_ge(r_qk, h + 1)
                if h >= 2:
                    act.wait_ge(r_s, 2 * h - 2)
                sc.copy(qkTh[h % 2].rearrange("p j t -> p (j t)"), psum[:, 0, :]).then_inc(r_qks, 1)

            def exps(n):
                act.wait_ge(r_e, n + 1)
                if n >= 2:
                    act.wait_ge(r_z, n - 1)
                    act.wait_ge(r_k, n - 1)
                b = 1 + 2 * (n % 2)
                sc.activation(ee[n % 2], psum[:, b:b + 2, :].rearrange("p b (l t) -> p (b l) t", t=P), ACT.Exp).then_inc(r_ee, 1)

            def out_save(h):
                act.wait_ge(r_o, h + 1)
                wait(act, r_ms, h)
                for i in range(TT):
                    ins = sc.activation(hsq[:, i, :], psum[:, 7, (1 + i) * P:(2 + i) * P], ACT.Square,
                                        accum_out=hs[:, 8 * i + h:8 * i + h + 1])
                ins.then_inc(r_ms, 1)
                sc.copy(hin[:, 0, :, h * DK:(h + 1) * DK],
                        psum[:, 7, P:3 * P].rearrange("p (i d) -> p i d", i=2)).then_inc(r_os, 1)

            qk_save(0)
            exps(0)
            exps(1)
            for n in range(2 * HH):
                if n % 2 == 0 and n // 2 + 1 < HH:
                    qk_save(n // 2 + 1)
                if n + 2 < 2 * HH:
                    exps(n + 2)
                if n % 2 == 0 and n:
                    out_save(n // 2 - 1)
            out_save(HH - 1)
            turn(1)
            split(0, Q_F2A)
            split(1, Q_F2A)
            norm(3, 3)
            split(2, Q_F2A, 1024)
            split(3, Q_F2A, 1024)

            def mlp2(t, q0, u0, hb, first=False, nxt=2048, last=False):
                if not last:
                    split(0, t + (q0 + 1), nxt)
                act.wait_ge(up_done, t + (u0 + 1))
                for i in range(TT):
                    sc.activation(sil[:, i, :], psum[:, 4 + i, 0:256], ACT.Silu).then_inc(act_done, 1)
                if not last:
                    split(1, t + (q0 + 1), nxt)
                if not first:
                    split(2, t + q0, 1024)
                    split(3, t + q0, 1024)
                act.wait_ge(h_turned, t + (hb + 1))
                sc.copy(hhi[:, 0:2, :], psum[:, 6, :].rearrange("p (k t) -> p k t", k=2)).then_inc(h_hi, 1)
            mlp2(0, Q_F2A, U_F2A, HT_F2A, first=True)
            with act.Fori(1, N_FF2 - 1) as t:
                mlp2(t, Q_F2A, U_F2A, HT_F2A)
            mlp2(N_FF2 - 1, Q_F2A, U_F2A, HT_F2A, nxt=1536)
            for s in (2, 3):
                split(s, Q_KV, 1536)
            norm(4, 4)
            kvf = area(0, TT, 1536)
            for t in range(N_KV):
                for p in range(2):
                    for s in (2 * p, 2 * p + 1):
                        if t == 0:
                            split(s, Q_KV + 1, 1536)
                        elif p == 0:
                            split(s, Q_NQ)
                    evac(G_KV + 2 * t + p, p, kvf[:, 0, (2 * t + p) * 384:(2 * t + p + 1) * 384])
            norm(5, None, fresh=False)
            for s in (2, 3):
                split(s, Q_NQ)
            act.wait_ge(k_["even"], 1)
            sc.copy(kt2.rearrange("p j h m -> p j (h m)"), psum[:, 5:7, :]).then_inc(k_["evens"], 1)
            nqf = area(3072, TT, D)
            for p in range(2):
                evac(G_Q + p, p, nqf[:, 0, p * 512:(p + 1) * 512])
            act.wait_ge(evac_d, G_END)
            act.wait_ge(evac_a, G_END)
            act.wait_ge(k_["krope"], 1)
            sc.activation(nt1, nqf.rearrange("p i n -> p (i n)"), ACT.Square).then_inc(k_["qsq"], 1)
            act.wait_ge(k_["g"], 1)
            sc.activation(gat3, psum[:, 4, 0:96].rearrange("p (i n) -> p i n", i=2), ACT.Sigmoid).then_inc(k_["gs"], 1)
            act.wait_ge(k_["kT"], 1)
            for b in range(4):
                sc.copy(nkT.rearrange("p b h t -> p (b h) t")[:, 2 * b:2 * b + 2, :],
                        psum[:, b, :].rearrange("p (k t) -> p k t", k=2)).then_inc(k_["kTs"], 1)

            def turned_save(src, dst, b0):
                act.wait_ge(k_[src], 1)
                for b in range(4):
                    sc.copy(dst[:, 2 * b:2 * b + 2, :],
                            psum[:, b0 + b, :].rearrange("p (k t) -> p k t", k=2)).then_inc(k_[src + "s"], 1)
            act.wait_ge(k_["hid"], 1)
            sc.activation(hidt[0:60, :, :], psum[0:60, 7, :].rearrange("p (j n) -> p j n", j=2), ACT.Silu).then_inc(k_["hidst"], 1)
            turned_save("qT", nqT, 0)
            act.wait_ge(k_["hidT"], 1)
            sc.copy(hid.rearrange("p j h c -> p (j h c)"), psum[:, 4, 128:368]).then_inc(k_["hids"], 1)
            for s in range(4):
                act.nop().then_inc(hi_ready[s], 1)
                split(s, Q_NOUT)
            act.wait_ge(k_["cm"], 1)
            for i in range(TT):
                last = sc.activation(pc[:, i, :, 0:NCMP], pc[:, i, :, 0:NCMP], ACT.Exp)
            last.then_inc(k_["ce"], 1)
            act.wait_ge(k_["cT"], 1)
            sc.copy(pcT.rearrange("p j t -> p (j t)"), psum[:, 2, :]).then_inc(k_["cTs"], 1)
            turned_save("qrT", nqrT, 4)
            act.wait_ge(k_["co"], 1)
            for i in range(TT):
                sc.copy(ob2[:, i, :, :].rearrange("p h d -> p (h d)"),
                        psum[:, 4 + 2 * i:6 + 2 * i, :].rearrange("p b n -> p (b n)")).then_inc(k_["cos"], 1)
            for u in range(2 * NH):
                act.wait_ge(w_m, u + 1)
                if u >= 2:
                    act.wait_ge(w_pts, u - 1)
                m = nst[:, 8 * (u % 2):8 * (u % 2) + 8]
                sc.activation(pb2[:, u % 2, 0:P], psum[:, u % 2, 0:P], ACT.Exp, bias=m[:, 0:1], accum_out=m[:, 2:3])
                sc.activation(pb2[:, u % 2, P:384], psum[:, u % 2, P:384], ACT.Exp, bias=m[:, 1:2],
                              accum_out=m[:, 3:4]).then_inc(w_e, 1)
            turn(2)
            split(0, Q_F2B)
            split(1, Q_F2B)
            norm(6, 5)
            split(2, Q_F2B, 1024)
            split(3, Q_F2B, 1024)
            mlp2(0, Q_F2B, U_F2B, HT_F2B, first=True)
            with act.Fori(1, N_FF2 - 1) as t:
                mlp2(t, Q_F2B, U_F2B, HT_F2B)
            mlp2(N_FF2 - 1, Q_F2B, U_F2B, HT_F2B, last=True)

        @block.vector
        def _(v):
            ve = nc.vector
            chain = Chain(v, dve)

            def split(s, n, width=2048):
                v.wait_ge(hi_ready[s], n + 1)
                ve.tensor_tensor(wlo[:, s, 0:width], raw[:, s, 0:width], whi[:, s, 0:width].bitcast(F32),
                                 ALU.subtract).then_inc(lo_ready[s], 1)

            def ada(m, half):
                v.wait_ge(ada_full[half], 16 * m + 16)
                for k in range(4):
                    w = adaw[:, half, k * 512:(k + 1) * 512]
                    c = cact[:, 4 * half + k:4 * half + k + 1]
                    if k:
                        v.wait_ge(ada_step, 6 * m + 3 * half + k)
                    elif half:
                        v.wait_ge(ada_used[0], m + 1)
                    elif not isinstance(m, int) or m > 0:
                        v.wait_ge(ada_turned, m)
                    if half == 0 and k == 0:
                        ins = ve.tensor_scalar(adaacc[:], w, c, None, ALU.mult)
                    else:
                        ins = ve.scalar_tensor_tensor(adaacc[:], w, c, adaacc[:], ALU.mult, ALU.add)
                    ins.then_inc(ada_used[half] if k == 3 else ada_step, 1)

            def ada_save(m, bank=7):
                v.wait_ge(ada_turned, m + 1)
                ve.tensor_copy(adacol[:, bass.ds(m * 4, 4)], psum[:, bank, 0:4]).then_inc(ada_saved, 1)

            def mods(key, gain, upto, n=24):
                c = LCOL[key]
                v.wait_ge(ada_saved, upto)
                v.wait_ge(vec_saved, 2)
                ve.tensor_tensor(adacol[:, c:c + n], adacol[:, c:c + n], bcol[:, c:c + n], ALU.add).then_inc(aff_ready, 1)
                v.wait_ge(aff_ready, ("order", 0, 1, 2, "kv", 3).index(key))
                affine_cols(c, gain)

            def affine_cols(c, gain):
                chain(ve.tensor_copy(sh[:], adacol[:, c:c + 8]))
                chain(ve.scalar_tensor_tensor(gs[:], adacol[:, c + 8:c + 16], 1.0, vcol[:, gain:gain + 8], ALU.add, ALU.mult))

            def norm(k, j, shift=True):
                v.wait_ge(n_rstd, j + 1)
                for i in range(TT):
                    ve.tensor_scalar(y[:, i, :], res[:, i, :], rstd[:, i:i + 1], None, ALU.mult).then_inc(n_y, 1)
                affine(k, j, shift)
                low(k)

            def affine(k, j, shift=True):
                for b in range(4):
                    v.wait_ge(n_turned, 4 * j + b + 1)
                    for q in range(2):
                        kt = 2 * b + q
                        src = psum[:, 4 + b, q * T:(q + 1) * T]
                        if shift:
                            ins = ve.tensor_scalar(xf[:, kt, :], src, gs[:, kt:kt + 1], sh[:, kt:kt + 1], ALU.mult, ALU.add)
                        else:
                            ins = ve.tensor_scalar(xf[:, kt, :], src, gs[:, kt:kt + 1], None, ALU.mult)
                    ins.then_inc(n_affine, 1)

            def low(k):
                for b in range(4):
                    v.wait_ge(n_hi, 4 * k + b + 1)
                    ve.tensor_tensor(xlo[:, 2 * b:2 * b + 2, :], xf[:, 2 * b:2 * b + 2, :],
                                     xhi[:, 2 * b:2 * b + 2, :].bitcast(F32), ALU.subtract).then_inc(n_x, 1)

            def turn(k):
                for b in range(4):
                    v.wait_ge(t_hi, 4 * k + b + 1)
                    ve.tensor_tensor(xlo[:, 2 * b:2 * b + 2, :], psum[:, 4 + b, :].rearrange("p (k t) -> p k t", k=2),
                                     xhi[:, 2 * b:2 * b + 2, :].bitcast(F32), ALU.subtract).then_inc(t_x, 1)

            def evac(g, p, dst):
                v.wait_ge(proj_done, g + 1)
                ve.tensor_copy(dst, psum[:, 2 * p + 1, 0:dst.shape[-1]]).then_inc(evac_d, 1)

            def residual(k):
                v.wait_ge(acc_done, k + 1)
                if k < 2:
                    v.wait_ge(p_rstd, k + 1)
                    v.wait_ge(gain_in, 16 * k + 16)
                for i in range(TT):
                    acc = psum[:, 2 * i:2 * i + 2, :].rearrange("p b n -> p (b n)")
                    if k < 2:
                        chain(ve.scalar_tensor_tensor(y[:, i, :], acc, stat[:, 38 + i:39 + i], gain_b[:], ALU.mult, ALU.mult))
                    else:
                        chain(ve.tensor_tensor(y[:, i, :], acc, gain_b[:], ALU.mult))
                    ve.tensor_tensor(res[:, i, :], res[:, i, :], y[:, i, :], ALU.add).then_inc(p_res, 1)

            def gate_save(k, bank=4):
                v.wait_ge(bg_turned, k + 1)
                ve.tensor_copy(gain_b[:, :], psum[:, bank:bank + 2, :].rearrange("p b n -> p (b n)")).then_inc(bg_saved, 1)

            v.wait_ge(vec_saved, 1)
            chain(ve.tensor_copy(gs[:], vcol[:, 0:8]))
            norm(0, 0, shift=False)
            for s in range(4):
                split(s, Q_QKV)
            with v.Fori(0, N_QKV) as t:
                for p in range(2):
                    split(2 * p, t + 1)
                    split(2 * p + 1, t + 1)
                    evac(2 * t + p, p, qkv[:, 1, bass.ds(t * 1024 + p * 512, 512)])

            for h in range(H1 + 3):
                if 1 <= h <= H1:
                    g = h - 1
                    m = st1[:, g % 2, :]
                    v.wait_ge(a_s, g + 1)
                    if g >= 2:
                        v.wait_ge(a_e, g - 1)
                    ve.tensor_reduce(m[:, 0:1], psum[:, 2 + g % 2, 0:P], AX, ALU.max, negate=True)
                    ve.tensor_reduce(m[:, 1:2], psum[:, 2 + g % 2, P:384], AX, ALU.max, negate=True).then_inc(a_m, 1)
                if 2 <= h <= H1 + 1:
                    g = h - 2
                    m = st1[:, g % 2, :]
                    v.wait_ge(a_e, g + 1)
                    wait(v, a_os, g - 1)
                    ve.reciprocal(m[:, 4:6], m[:, 2:4])
                    v.wait_ge(a_pt, g + 1)
                    if g >= 2:
                        v.wait_ge(a_o, g - 1)
                    ve.tensor_copy(pT1[:, g % 2, :], psum[:, 4 + g % 2, 0:384]).then_inc(a_pts, 1)
                if 3 <= h:
                    g = h - 3
                    m = st1[:, g % 2, :]
                    v.wait_ge(a_o, g + 1)
                    v.wait_ge(a_pts, g + 1)
                    for i in range(TT):
                        ins = ve.tensor_scalar(ob1[:, i, g * DH1:(g + 1) * DH1], psum[:, 6 + g % 2, i * P:(i + 1) * P],
                                               m[:, 4 + i:5 + i], None, ALU.mult)
                    ins.then_inc(a_os, 1)
            turn(0)
            split(0, Q_FF1)
            split(1, Q_FF1)
            residual(0)
            chain(ve.tensor_copy(gs[:], vcol[:, 8:16]))
            norm(1, 1, shift=False)
            split(2, Q_FF1)
            split(3, Q_FF1)

            def mlp1(t, first=False):
                split(0, t + (Q_FF1 + 1))
                ada(t, 0)
                ada(t, 1)
                split(1, t + (Q_FF1 + 1))
                ada_save(t)
                if not first:
                    split(2, t + Q_FF1)
                    split(3, t + Q_FF1)
                for b in range(2):
                    v.wait_ge(h_hi, 2 * t + b + 1)
                    ve.tensor_tensor(hlo[:, 2 * b:2 * b + 2, :], sq[:, 2 * b:2 * b + 2, :],
                                     hhi[:, 2 * b:2 * b + 2, :].bitcast(F32), ALU.subtract).then_inc(h_lo, 1)
            v.wait_ge(c_ready, 1)
            mlp1(0, True)
            with v.Fori(1, N_FF1) as t:
                mlp1(t)
            for s in (2, 3):
                split(s, Q_HIN)
            residual(1)
            mods(0, VR["mix2"], 6)
            norm(2, 2)
            tmp = area(12416, TT, D)
            for t, sec in enumerate(HIN_ORDER):
                for p in range(2):
                    split(2 * p, Q_HIN + t + 1)
                    if p == 0:
                        ada(M_L1 + 2 + t, 0)
                    split(2 * p + 1, Q_HIN + t + 1)
                    evac(G_HIN + 2 * t + p, p, hin[:, sec, 1, p * 512:(p + 1) * 512])
                    if p == 0:
                        ada(M_L1 + 2 + t, 1)
                ada_save(M_L1 + 2 + t)
                if t == 1:
                    v.wait_ge(g_f, 1)
                    ve.scalar_tensor_tensor(hin[:, 1, :, :].rearrange("p i n -> p (i n)"), hin[:, 1, :, :].rearrange("p i n -> p (i n)"),
                                            0.0, tmp.rearrange("p i n -> p (i n)"), ALU.min, ALU.subtract).then_inc(g_d, 1)
            for b in range(4):
                v.wait_ge(g_hi, b + 1)
                ve.tensor_tensor(glo[:, :, b * 256:(b + 1) * 256], hin[:, 1, :, b * 256:(b + 1) * 256],
                                 ghi[:, :, b * 256:(b + 1) * 256].bitcast(F32), ALU.subtract).then_inc(g_lo, 1)

            def q_part(n):
                h, i = n // 2, n % 2
                if i == 0:
                    v.wait_ge(r_qks, h + 1)
                v.wait_ge(r_ee, n + 1)
                if n >= 2:
                    v.wait_ge(r_s, n - 1)
                w = NL + i
                ve.tensor_tensor(qe[i][:, 0:w, :], ee[i][:, 0:w, :], qkTh[h % 2][:, 0, i * P:(i + 1) * P].unsqueeze(1)
                                 .to_broadcast([P, w, P]), ALU.mult).then_inc(r_z, 1)

            v.wait_ge(ada_used[0], M_L2)
            v.wait_ge(ada_used[1], M_L2)
            hg = hin[:, 3, :, :].rearrange("p i (h d) -> p (i h) d", d=DK)
            q_part(0)
            for n in range(2 * HH):
                h, i = n // 2, n % 2
                if n + 1 < 2 * HH:
                    q_part(n + 1)
                v.wait_ge(r_s, n + 1)
                wait(v, r_am, n)
                ve.tensor_tensor(pm, psum[:, 5:7, :].rearrange("p b (l t) -> p (b l) t", t=P), MK, ALU.mult).then_inc(r_m, 1)
                v.wait_ge(r_m, n + 1)
                wait(v, r_o, h - 1)
                ins = ve.tensor_reduce(am[h % 2][:, i, :], pm.rearrange("p l t -> p t l"), AX, ALU.add)
                if i == 1:
                    ins = ve.tensor_copy(am[h % 2][:, 2, :], psum[:, 7, 0:P])
                ins.then_inc(r_am, 1)
            v.wait_ge(g_f, 3)
            v.wait_ge(onb_in, 16)
            chain(ve.tensor_tensor(hg, hg, onb[:].unsqueeze(1).to_broadcast([P, 2 * HH, DK]), ALU.mult))
            v.wait_ge(r_os, HH)
            gate_save(0, 1)
            v.wait_ge(r_rs, 1)
            for h in range(HH):
                for i in range(TT):
                    o = hin[:, 0, i, h * DK:(h + 1) * DK]
                    ins = ve.scalar_tensor_tensor(o, o, hs[:, 16 + 8 * i + h:17 + 8 * i + h], hin[:, 3, i, h * DK:(h + 1) * DK],
                                                  ALU.mult, ALU.mult)
                if h % 2:
                    ins.then_inc(r_n, 1)
            turn(1)
            mods(1, VR["ffn2"], 12)

            split(0, Q_F2A)
            split(1, Q_F2A)
            residual(2)
            gate_save(1)
            norm(3, 3)
            split(2, Q_F2A, 1024)
            split(3, Q_F2A, 1024)

            def mlp2(t, q0, hb, gb, m=None, first=False, nxt=2048, last=False):
                if not last:
                    split(0, t + (q0 + 1), nxt)
                if m is not None:
                    ada(m, 0)
                for i in range(TT):
                    v.wait_ge(act_done, 2 * t + (gb + 16 + i + 1))
                    ve.tensor_tensor(gat[:, i, :], sil[:, i, :], psum[:, 4 + i, 256:512], ALU.mult).then_inc(gate_done, 1)
                if m is not None:
                    ada(m, 1)
                if not last:
                    split(1, t + (q0 + 1), nxt)
                if not first:
                    split(2, t + q0, 1024)
                    split(3, t + q0, 1024)
                if m is not None:
                    ada_save(m)
                v.wait_ge(h_hi, t + (hb + 1))
                ve.tensor_tensor(hlo[:, 0:2, :], psum[:, 6, :].rearrange("p (k t) -> p k t", k=2),
                                 hhi[:, 0:2, :].bitcast(F32), ALU.subtract).then_inc(h_lo, 1)
            mlp2(0, Q_F2A, HT_F2A, 0, M_L2, first=True)
            with v.Fori(1, N_FF2 - 1) as t:
                mlp2(t, Q_F2A, HT_F2A, 0, t + M_L2)
            mlp2(N_FF2 - 1, Q_F2A, HT_F2A, 0, M_L3, nxt=1536)
            for s in (2, 3):
                split(s, Q_KV, 1536)
            residual(3)
            mods(2, VR["mix2"] + 8, M_L3 + 1)
            mods("kv", VR["kvn"], M_L3 + 1, 16)
            norm(4, 4)
            affine_cols(LCOL[2], VR["mix2"] + 8)
            affine(5, 4)
            kvf = area(0, TT, 1536)
            for t in range(N_KV):
                for p in range(2):
                    for s in (2 * p, 2 * p + 1):
                        if t == 0:
                            split(s, Q_KV + 1, 1536)
                        elif p == 0:
                            split(s, Q_NQ)
                        if p == 0:
                            ada(M_L3 + 1 + t, s)
                    evac(G_KV + 2 * t + p, p, kvf[:, 1, (2 * t + p) * 384:(2 * t + p + 1) * 384])
                ada_save(M_L3 + 1 + t)
            low(5)
            for s in (2, 3):
                split(s, Q_NQ)
            v.wait_ge(k_["evens"], 1)
            for j in range(2):
                for c in range(NCMP):
                    pos = vcol[:, VR["pos"] + 16 * j:VR["pos"] + 16 * j + 16].unsqueeze(2).to_broadcast([P, 16, NKV])
                    ins = ve.tensor_tensor(fl[:, j, :, c, :], kt2[:, j, :, 8 * c:8 * c + 16].rearrange("p h a -> p a h"), pos, ALU.add)
            ins.then_inc(k_["flat"], 1)
            v.wait_ge(k_["flat"], 1)
            v.wait_ge(evac_a, G_Q)
            v.wait_ge(evac_d, G_Q)
            k2 = nt1[:, 0:1024].rearrange("p (i b h d) -> p i b h d", i=2, b=2, h=4)
            for i in range(TT):
                for b in range(2):
                    ins = ve.tensor_tensor(k2[:, i, b], kv[:, i, 2 + 2 * b], kv[:, i, 2 + 2 * b], ALU.mult)
            chain(ins)
            ve.tensor_reduce(nst[:, 16:32], nt1[:, 0:1024].rearrange("p (g d) -> p g d", d=DN), AX, ALU.add).then_inc(k_["sq"], 1)
            v.wait_ge(k_["rs"], 1)
            v.wait_ge(knb_in, 32)
            rope = cst("rope").rearrange("p (i j d) -> p i j d", i=2, j=2)
            HD = DN // 2

            def turn_half(dst1, dst2, x1, x2, cos, sin, tmp1):
                ve.tensor_tensor(dst1, x1, cos, ALU.mult)
                chain(ve.tensor_tensor(tmp1, x2, sin, ALU.mult))
                ve.tensor_tensor(dst2, x2, cos, ALU.mult)
                chain(ve.tensor_tensor(dst1, dst1, tmp1, ALU.subtract))
                chain(ve.tensor_tensor(tmp1, x1, sin, ALU.mult))
                chain(ve.tensor_tensor(dst2, dst2, tmp1, ALU.add))

            for i in range(TT):
                for b in range(2):
                    r = nst[:, 32 + 8 * i + 4 * b:36 + 8 * i + 4 * b].unsqueeze(2).to_broadcast([P, NKV, DN])
                    x = kv[:, i, 2 + 2 * b, :, :]
                    chain(ve.tensor_tensor(x, x, r, ALU.mult))
                    chain(ve.tensor_tensor(x, x, knb[:, 1 + b, :].unsqueeze(1).to_broadcast([P, NKV, DN]), ALU.mult))
                    cos = rope[:, i, 0, :].unsqueeze(1).to_broadcast([P, NKV, HD])
                    sin = rope[:, i, 1, :].unsqueeze(1).to_broadcast([P, NKV, HD])
                    d = nkd[:, i, b, :, 0, :]
                    turn_half(d[:, :, 0:HD], d[:, :, HD:DN], x[:, :, 0:HD], x[:, :, HD:DN], cos, sin,
                              nt1[:, 1024:1024 + NKV * HD].rearrange("p (h d) -> p h d", h=NKV))
                    ins = ve.tensor_copy(nkd[:, i, b, :, 1, :], d)
            ins.then_inc(k_["krope"], 1)
            nqf = area(3072, TT, D)
            for p in range(2):
                evac(G_Q + p, p, nqf[:, 1, p * 512:(p + 1) * 512])
            chain(ve.tensor_scalar(knb[:, 3, :], knb[:, 3, :], DN ** -0.5, None, ALU.mult))
            v.wait_ge(k_["qsq"], 1)
            ve.tensor_reduce(nst[:, 64:96], nt1.rearrange("p (g d) -> p g d", d=DN), AX, ALU.add).then_inc(k_["sq"], 1)
            v.wait_ge(k_["rs"], 2)
            qg = nq.rearrange("p i h d -> p (i h) d")
            chain(ve.tensor_tensor(qg, qg, nst[:, 96:128].unsqueeze(2).to_broadcast([P, 2 * NH, DN]), ALU.mult))
            ve.tensor_tensor(qg, qg, knb[:, 3, :].unsqueeze(1).to_broadcast([P, 2 * NH, DN]), ALU.mult).then_inc(k_["qn"], 1)
            v.wait_ge(k_["qn"], 1)
            v.wait_ge(k_["kT"], 1)
            for i in range(TT):
                cos = rope[:, i, 0, :].unsqueeze(1).to_broadcast([P, NH, HD])
                sin = rope[:, i, 1, :].unsqueeze(1).to_broadcast([P, NH, HD])
                turn_half(nqr[:, i, :, 0:HD], nqr[:, i, :, HD:DN], nq[:, i, :, 0:HD], nq[:, i, :, HD:DN], cos, sin,
                          nt1[:, 512 * i:512 * i + 512].rearrange("p (h d) -> p h d", h=NH))
            v.nop().then_inc(k_["qr"], 1)
            v.wait_ge(k_["kc"], 1)
            ve.tensor_copy(kcv[0:60, :, :], psum[0:60, 7, 0:128].rearrange("p (j d) -> p j d", j=2)).then_inc(k_["kcs"], 1)
            v.wait_ge(k_["kcs"], 1)
            chain(ve.tensor_tensor(kcd[0:60, 0, :], kcv[0:60, 0, :], kcv[0:60, 0, :], ALU.mult))
            ve.tensor_reduce(nst[0:60, 0:1], kcd[0:60, 0, :], AX, ALU.add).then_inc(k_["sq"], 1)
            v.wait_ge(k_["vb"], 1)
            for j in range(2):
                ins = ve.tensor_tensor(vbd[:, j, :, :], psum[:, 5 + j, 0:DN].unsqueeze(1).to_broadcast([P, 8, DN]),
                                       cst("bm").unsqueeze(2).to_broadcast([P, 8, DN]), ALU.mult)
            ins.then_inc(k_["vbs"], 1)
            v.wait_ge(k_["rs"], 3)
            for j in range(2):
                ins = ve.scalar_tensor_tensor(kcd[0:60, j, :], kcv[0:60, 0, :], nst[0:60, 1:2], knb[0:60, 0, :], ALU.mult, ALU.mult)
            ins.then_inc(k_["kcd"], 1)
            v.wait_ge(k_["kct"], 1)
            ve.tensor_copy(kcT[:, :], psum[:, 7, 256:316]).then_inc(k_["kcts"], 1)
            cm = cst("cmask").rearrange("p (j i c) -> p j i c", j=2, i=2)
            v.wait_ge(k_["cs"], 1)
            chain(ve.memset(pc, 0.0))
            ng = nst[:, 128:160].rearrange("p (i h) -> p i h", i=2)
            for i in range(TT):
                x = pc[:, i, :, 0:NCMP]
                for r in range(2):
                    ins = ve.tensor_tensor(pc[:, i, r:NH:2, 0:NCMP],
                                           psum[:, 2 * i + r, 0:128].rearrange("p (h c) -> p h c", c=16)[:, :, 0:NCMP],
                                           cm[:, 0, i, :].unsqueeze(1).to_broadcast([P, NH // 2, NCMP]), ALU.add)
                chain(ins)
                chain(ve.tensor_reduce(ng[:, i, :], x, AX, ALU.max))
                ins = ve.tensor_tensor(x, x, ng[:, i, :].unsqueeze(2).to_broadcast([P, NH, NCMP]), ALU.subtract)
            ins.then_inc(k_["cm"], 1)
            gate_save(2)
            for s in (0, 1):
                v.nop().then_inc(lo_ready[s], 1)
                split(s, Q_NOUT)
            v.wait_ge(k_["ce"], 1)
            for i in range(TT):
                x = pc[:, i, :, 0:NCMP]
                chain(ve.tensor_tensor(x, x, cm[:, 1, i, :].unsqueeze(1).to_broadcast([P, NH, NCMP]), ALU.mult))
                chain(ve.tensor_reduce(ng[:, i, :], x, AX, ALU.add))
            chain(ve.tensor_scalar(ng, ng, 1e-30, None, ALU.max))
            chain(ve.reciprocal(ng, ng))
            v.wait_ge(k_["gs"], 1)
            chain(ve.tensor_tensor(ng, ng, gat3[:, :, 0:NH], ALU.mult))
            for i in range(TT):
                x = pc[:, i, :, 0:NCMP]
                ins = ve.tensor_tensor(x, x, ng[:, i, :].unsqueeze(2).to_broadcast([P, NH, NCMP]), ALU.mult)
            ins.then_inc(k_["cp"], 1)
            ada(M_L3 + 3, 0)
            ada(M_L3 + 3, 1)
            ada_save(M_L3 + 3, 3)
            for w in range(2 * NH + 2):
                if w < 2 * NH:
                    u = w
                    m = nst[:, 8 * (u % 2):8 * (u % 2) + 8]
                    v.wait_ge(w_s, u + 1)
                    if u >= 2:
                        v.wait_ge(w_e, u - 1)
                    ve.tensor_reduce(m[:, 0:1], psum[:, u % 2, 0:P], AX, ALU.max, negate=True)
                    ve.tensor_reduce(m[:, 1:2], psum[:, u % 2, P:384], AX, ALU.max, negate=True).then_inc(w_m, 1)
                if 1 <= w <= 2 * NH:
                    u = w - 1
                    hq, b = u // 2, u % 2
                    m = nst[:, 8 * (u % 2):8 * (u % 2) + 8]
                    v.wait_ge(w_e, u + 1)
                    wait(v, w_os, u - 1)
                    chain(ve.reciprocal(m[:, 4:6], m[:, 2:4]))
                    ve.tensor_tensor(m[:, 4:6], m[:, 4:6], gat3[:, :, (1 + b) * NH + hq], ALU.mult)
                    v.wait_ge(w_pt, u + 1)
                    if u >= 2:
                        v.wait_ge(w_o, u - 1)
                    ve.tensor_copy(pT2[:, u % 2, :], psum[:, 2 + u % 2, 0:384]).then_inc(w_pts, 1)
                if 2 <= w:
                    u = w - 2
                    hq = u // 2
                    m = nst[:, 8 * (u % 2):8 * (u % 2) + 8]
                    v.wait_ge(w_o, u + 1)
                    v.wait_ge(w_pts, u + 1)
                    if u == 0:
                        v.wait_ge(k_["cos"], 2)
                    if u:
                        v.wait_ge(w_os, u)
                    for i in range(TT):
                        ins = ve.scalar_tensor_tensor(ob2[:, i, hq, :], psum[:, 4 + u % 2, i * DN:(i + 1) * DN],
                                                      m[:, 4 + i:5 + i], ob2[:, i, hq, :], ALU.mult, ALU.add)
                    ins.then_inc(w_os, 1)
            turn(2)
            for s in (2, 3):
                v.nop().then_inc(lo_ready[s], 1)
                split(s, Q_NOUT)
            for b in (4, 5):
                ada(M_L3 + b, 0)
                ada(M_L3 + b, 1)
                ada_save(M_L3 + b)
            mods(3, VR["ffn2"] + 8, M_END)
            split(0, Q_F2B)
            split(1, Q_F2B)
            residual(4)
            gate_save(3)
            norm(6, 5)
            split(2, Q_F2B, 1024)
            split(3, Q_F2B, 1024)
            mlp2(0, Q_F2B, HT_F2B, 22, first=True)
            with v.Fori(1, N_FF2 - 1) as t:
                mlp2(t, Q_F2B, HT_F2B, 22)
            mlp2(N_FF2 - 1, Q_F2B, HT_F2B, 22, last=True)
            residual(5)

        @block.tensor
        def _(pe):
            te = nc.tensor

            def mm(dst, lhsT, rhs, start=True, stop=True, open_=False):
                return te.matmul(dst, lhsT, rhs, start=start, stop=stop, skip_group_check=open_)

            def three(dst, lhi, llo, s, c0, n, start, stop, open_=False):
                wh, wl = whi[:, s, c0:c0 + n], wlo[:, s, c0:c0 + n]
                mm(dst, lhi, wh, start, False, open_)
                mm(dst, lhi, wl, False, False, open_)
                return mm(dst, llo, wh, False, stop, open_)

            def norm(j, ada_upto=0, gates=0):
                wait(pe, ada_saved, ada_upto)
                wait(pe, bg_saved, gates)
                for b in range(4):
                    for i in range(TT):
                        if b == 0:
                            pe.wait_ge(n_y, 2 * j + i + 1)
                        for q in range(2):
                            kt = 2 * b + q
                            ins = te.transpose(psum[:, 4 + b, q * T + i * P:q * T + (i + 1) * P], y[:, i, kt * P:(kt + 1) * P], ident)
                    ins.then_inc(n_turned, 1)

            def turn(k, x, ready=None):
                for b in range(4):
                    if ready is not None:
                        pe.wait_ge(ready, b + 1)
                    for q in range(2):
                        for i in range(TT):
                            kt = 2 * b + q
                            ins = te.transpose(psum[:, 4 + b, q * T + i * P:q * T + (i + 1) * P], x[:, i, kt * P:(kt + 1) * P], ident)
                    ins.then_inc(t_turned, 1)

            def item_ready(s, n):
                pe.wait_ge(lo_ready[s], n + 1)

            def project(n, g, width=512):
                for p in range(2):
                    if not isinstance(g, int) or g >= 2:
                        pe.wait_ge(evac_a, g + p - 1)
                        pe.wait_ge(evac_d, g + p - 1)
                    for half in range(2):
                        s = 2 * p + half
                        item_ready(s, n)
                        for i in range(TT):
                            for k in range(4):
                                kt = 4 * half + k
                                ins = three(psum[:, 2 * p + i, 0:width], xhi[:, kt, i * P:(i + 1) * P], xlo[:, kt, i * P:(i + 1) * P],
                                            s, k * width, width, kt == 0, kt == KD - 1)
                        ins.then_inc(used[s], 1)
                    pe.wait_ge(used[2 * p + 1], n + 1)
                    pe.nop().then_inc(proj_done, 1)

            def accumulate(n, m=None):
                for s in range(4):
                    item_ready(s, n)
                    for i in range(TT):
                        for f in range(2):
                            for k in range(2):
                                kt = 2 * s + k
                                ins = three(psum[:, 2 * i + f, :], xhi[:, kt, i * P:(i + 1) * P], xlo[:, kt, i * P:(i + 1) * P],
                                            s, k * D + f * 512, 512, kt == 0, kt == KD - 1)
                    ins.then_inc(used[s], 1)
                    if s == 2 and m is not None:
                        ada(m)
                pe.wait_ge(used[3], n + 1)
                pe.nop().then_inc(acc_done, 1)

            def ada(m, bank=7):
                pe.wait_ge(ada_used[1], m + 1)
                for c in range(4):
                    ins = mm(psum[:, bank, c:c + 1], adaacc[:, c * P:(c + 1) * P], ones[:])
                ins.then_inc(ada_turned, 1)

            def gate(key, k, bank=4):
                pe.wait_ge(aff_ready, ("order", 0, 1, 2, "kv", 3).index(key))
                for kt in range(KD):
                    c = LCOL[key] + 16 + kt
                    ins = mm(psum[:, bank + kt // 4, (kt % 4) * P:(kt % 4 + 1) * P], adacol[:, c:c + 1].to_broadcast([P, P]), ident)
                ins.then_inc(bg_turned, 1)

            def open_acc():
                for b in range(4):
                    mm(psum[:, b, :], zrow[0:1, 0:P], zrow[0:1, :], True, False, True)

            pe.wait_ge(consts_in, 16)
            pe.wait_ge(vec_in, 16 * 10)
            te.transpose(psum[:, 0, 0:96], vrow1[0:96, :], ident[0:96, 0:96])
            te.transpose(psum[:, 0, 128:240], vrow2[0:112, :], ident[0:112, 0:112]).then_inc(vec_turned, 1)
            pe.wait_ge(ones_set, 1)
            norm(0)
            pe.wait_ge(n_x, 4)
            pe.wait_ge(vec_saved, 2)
            project(Q_QKV, 0)
            with pe.Fori(1, N_QKV) as t:
                project(t + Q_QKV, 2 * t)

            pe.wait_ge(bias_ready, 1)
            pe.wait_ge(evac_a, G_HIN)
            pe.wait_ge(evac_d, G_HIN)
            for h in range(H1 + 3):
                if h < H1:
                    if h >= 2:
                        pe.wait_ge(a_qks, h - 1)
                    for j in range(2):
                        for i in range(TT):
                            ins = te.transpose(psum[:, h % 2, j * T + i * P:j * T + (i + 1) * P],
                                               qkv[:, i, j * D + h * DH1:j * D + (h + 1) * DH1], ident)
                    ins.then_inc(a_qk, 1)
                if 1 <= h <= H1:
                    g = h - 1
                    pe.wait_ge(a_qks, g + 1)
                    if g >= 2:
                        pe.wait_ge(a_e, g - 1)
                    x = qkT[:, g % 2, :]
                    mm(psum[:, 2 + g % 2, 0:384], slopeb[:, g, :], distb, True, False, True)
                    mm(psum[:, 2 + g % 2, 0:P], x[:, 0:P], x[:, T:T + P], False, False, True)
                    mm(psum[:, 2 + g % 2, P:384], x[:, P:T], x[:, T:2 * T], False, True, True).then_inc(a_s, 1)
                if 2 <= h <= H1 + 1:
                    g = h - 2
                    pe.wait_ge(a_e, g + 1)
                    if g >= 2:
                        pe.wait_ge(a_pts, g - 1)
                    for b in range(3):
                        ins = te.transpose(psum[:, 4 + g % 2, b * P:(b + 1) * P], pb1[:, g % 2, b * P:(b + 1) * P], ident)
                    ins.then_inc(a_pt, 1)
                if 3 <= h:
                    g = h - 3
                    pe.wait_ge(a_pts, g + 1)
                    if g >= 2:
                        pe.wait_ge(a_os, g - 1)
                    o = psum[:, 6 + g % 2, :]
                    vv = qkv[:, :, 2 * D + g * DH1:2 * D + (g + 1) * DH1]
                    mm(o[:, 0:P], pT1[:, g % 2, 0:P], vv[:, 0, :])
                    mm(o[:, P:T], pT1[:, g % 2, P:T], vv[:, 0, :], True, False)
                    mm(o[:, P:T], pT1[:, g % 2, T:384], vv[:, 1, :], False, True).then_inc(a_o, 1)
            pe.wait_ge(a_os, H1)
            turn(0, ob1)
            pe.wait_ge(t_x, 4)
            accumulate(Q_WO)
            norm(1)
            pe.wait_ge(n_x, 8)

            def up(n, u):
                for s in range(2):
                    item_ready(s, n)
                    for i in range(TT):
                        for k in range(4):
                            kt = 4 * s + k
                            ins = three(psum[:, 4 + i, :], xhi[:, kt, i * P:(i + 1) * P], xlo[:, kt, i * P:(i + 1) * P],
                                        s, k * 512, 512, kt == 0, kt == KD - 1)
                    ins.then_inc(used[s], 1)
                pe.wait_ge(used[1], n + 1)
                pe.nop().then_inc(up_done, 1)

            def down(n, kts, last=False, slots=(2, 3)):
                for s in slots:
                    item_ready(s, n)
                    for i in range(TT):
                        for f in range(2):
                            for k in range(kts):
                                kt = kts * (s - 2) + k
                                ins = three(psum[:, 2 * i + f, :], hhi[:, kt, i * P:(i + 1) * P], hlo[:, kt, i * P:(i + 1) * P],
                                            s, k * D + f * 512, 512, False, last and kt == 2 * kts - 1, True)
                    ins.then_inc(used[s], 1)

            def hidden1(t):
                pe.wait_ge(act_done, 2 * t + 2)
                for b in range(2):
                    if b == 1:
                        pe.wait_ge(ada_saved, t + 1)
                    for q in range(2):
                        for i in range(TT):
                            kt = 2 * b + q
                            ins = te.transpose(psum[:, 6 + b, q * T + i * P:q * T + (i + 1) * P], relu[:, i, kt * P:(kt + 1) * P], ident)
                    ins.then_inc(h_turned, 1)
            open_acc()
            up(Q_FF1, 0)
            ada(0)
            hidden1(0)
            with pe.Fori(1, N_FF1) as t:
                up(t + Q_FF1, t)
                pe.wait_ge(h_lo, 2 * t)
                down(t + (Q_FF1 - 1), 2, slots=(2,))
                ada(t)
                down(t + (Q_FF1 - 1), 2, slots=(3,))
                hidden1(t)
            pe.wait_ge(h_lo, 2 * N_FF1)
            down(Q_FF1 + N_FF1 - 1, 2, last=True)
            pe.wait_ge(used[3], Q_FF1 + N_FF1)
            pe.nop().then_inc(acc_done, 1)
            norm(2, ada_upto=8)
            pe.wait_ge(n_x, 12)
            for t in range(N_HIN):
                project(Q_HIN + t, G_HIN + 2 * t)
                wait(pe, ada_saved, 8 + t)
                ada(8 + t)

            pe.wait_ge(ada_saved, M_L2)
            pe.wait_ge(evac_a, G_KV)
            pe.wait_ge(evac_d, G_KV)
            pe.wait_ge(g_f, 2)
            for b in (5, 6):
                ins = mm(psum[:, b, :], zrow[0:1, 0:P], zrow[0:1, :])
            ins.then_inc(s_zero, 1)
            pe.wait_ge(s_zero, 1)

            def heads_qk(h):
                if h:
                    pe.wait_ge(r_qks, h)
                for j, src in enumerate((hin[:, 0], hk)):
                    for i in range(TT):
                        ins = te.transpose(psum[:, 0, j * T + i * P:j * T + (i + 1) * P], src[:, i, h * DK:(h + 1) * DK], ident)
                ins.then_inc(r_qk, 1)

            def exponents(n):
                h, i = n // 2, n % 2
                if i == 0:
                    pe.wait_ge(g_lo, h // 2 + 1)
                if n >= 2:
                    pe.wait_ge(r_ee, n - 1)
                parts = [(0, MLr[:, 0:512]), (512, MLr[:, 512:1024])] if i == 0 else [(0, MLr[:, 0:512]), (512, MLr[:, 512:896]), (896, MLx)]
                e = psum[:, 1 + 2 * i:3 + 2 * i, :].rearrange("p b n -> p (b n)")
                for c0, m in parts:
                    for x in (ghi, glo):
                        ins = mm(e[:, c0:c0 + m.shape[-1]], x[:, i, h * DK:(h + 1) * DK], m, x is ghi, x is glo)
                ins.then_inc(r_e, 1)

            def second(x, m):
                return x.rearrange("p (j s r) -> p j s r", s=2, r=m)[:, :, 1, :]

            def scores(n):
                h, i = n // 2, n % 2
                pe.wait_ge(r_z, n + 1)
                pe.wait_ge(r_k, n + 1)
                wait(pe, r_m, n)
                for l, m in enumerate(LEVELS):
                    mm(second(psum[:, 5 + l // 4, (l % 4) * P:(l % 4 + 1) * P], m), ke[i][:, l, :], second(qe[i][:, l, :], m))
                if i == 1:
                    wait(pe, r_os, h)
                    mm(psum[:, 7, 0:P], ke7[h % 2], qe[1][:, NL, :])
                mm(psum[:, 6, 384:512], qkTh[h % 2][:, 1, i * P:(i + 1) * P], qkTh[h % 2][:, 0, i * P:(i + 1) * P]).then_inc(r_s, 1)

            def outputs(h):
                pe.wait_ge(r_am, 2 * h + 2)
                x, c = am[h % 2], slice(h * DK, (h + 1) * DK)
                mm(psum[:, 7, P:2 * P], x[:, 0, :], hin[:, 2, 0, c])
                mm(psum[:, 7, 2 * P:3 * P], x[:, 1, :], hin[:, 2, 1, c], True, False)
                mm(psum[:, 7, 2 * P:3 * P], x[:, 2, :], hin[:, 2, 0, c], False, True).then_inc(r_o, 1)

            heads_qk(0)
            pe.wait_ge(ml_ready, 1)
            exponents(0)
            exponents(1)
            for n in range(2 * HH):
                if n % 2 == 0 and n // 2 + 1 < HH:
                    heads_qk(n // 2 + 1)
                if n + 2 < 2 * HH:
                    exponents(n + 2)
                scores(n)
                if n % 2 == 0 and n:
                    outputs(n // 2 - 1)
            pe.wait_ge(r_ee, 2 * HH)
            gate(0, 0, 1)
            outputs(HH - 1)
            turn(1, hin[:, 0, :, :], r_n)
            pe.wait_ge(bg_saved, 1)
            pe.wait_ge(t_x, 8)
            accumulate(Q_HOUT)
            pe.wait_ge(p_res, 6)
            gate(1, 1)
            norm(3, gates=2)
            pe.wait_ge(n_x, 16)

            def mlp2_hidden(t, gb):
                pe.wait_ge(gate_done, 2 * t + (gb + 2))
                for q in range(2):
                    for i in range(TT):
                        ins = te.transpose(psum[:, 6, q * T + i * P:q * T + (i + 1) * P], gat[:, i, q * P:(q + 1) * P], ident)
                ins.then_inc(h_turned, 1)

            def mlp2(q0, u0, hb, gb, m0=None):
                open_acc()
                up(q0, u0)
                if m0 is not None:
                    ada(m0)
                mlp2_hidden(0, gb)
                with pe.Fori(1, N_FF2) as t:
                    up(t + q0, t + u0)
                    pe.wait_ge(h_lo, t + hb)
                    down(t + (q0 - 1), 1)
                    if m0 is not None:
                        pe.wait_ge(ada_saved, t + m0)
                        ada(t + m0)
                    mlp2_hidden(t, gb)
                pe.wait_ge(h_lo, hb + N_FF2)
                down(q0 + N_FF2 - 1, 1, last=True)
                pe.wait_ge(used[3], q0 + N_FF2)
                pe.nop().then_inc(acc_done, 1)

            mlp2(Q_F2A, U_F2A, HT_F2A, 0, M_L2)
            norm(4, ada_upto=M_L3 + 1)
            pe.wait_ge(n_x, 20)
            for t in range(N_KV):
                project(Q_KV + t, G_KV + 2 * t, 384)
                wait(pe, ada_saved, M_L3 + 1 + t)
                ada(M_L3 + 1 + t)
            pe.wait_ge(evac_a, G_KV + 3)
            pe.wait_ge(evac_d, G_KV + 3)
            pe.wait_ge(n_affine, 24)
            for j in range(2):
                for h in range(NKV):
                    for i in range(TT):
                        for r in range(2):
                            ins = mm(psum[64 * r:64 * r + 64, 5 + j, h * P + i * 64:h * P + i * 64 + 64],
                                     kv[:, i, j, h, :], ident[:, r:P:2])
            ins.then_inc(k_["even"], 1)
            pe.wait_ge(n_x, 24)
            project(Q_NQ, G_Q)
            pe.wait_ge(nsa_in, 32)
            for i in range(TT):
                for k in range(KD):
                    for x in (xhi, xlo):
                        ins = mm(psum[:, 4, 48 * i:48 * i + 48], x[:, k, i * P:(i + 1) * P].bitcast(F32), wgs[:, k, :],
                                 k == 0 and x is xhi, k == KD - 1 and x is xlo)
            ins.then_inc(k_["g"], 1)

            def compress(j):
                for k in range(16):
                    w1 = raw[:, 2 * j + k // 8, :].rearrange("p (k n) -> p k n", k=8)[:, k % 8, :]
                    ins = mm(psum[0:60, 7, j * CHID:(j + 1) * CHID], fl[:, j, k, :, :].rearrange("p c h -> p (c h)"), w1, k == 0, k == 15)
                    if k % 8 == 7:
                        ins.then_inc(used[2 * j + k // 8], 1)
            pe.wait_ge(k_["flat"], 1)
            for s in range(4):
                pe.wait_ge(raw_full[s], 32 * Q_CMP + 32)
            compress(0)
            pe.wait_ge(evac_a, G_END)
            pe.wait_ge(evac_d, G_END)
            pe.wait_ge(k_["krope"], 1)
            for b in range(2):
                for h in range(NKV):
                    for i in range(TT):
                        x = b * NKV + h
                        ins = te.transpose(psum[:, x // 2, (x % 2) * T + i * P:(x % 2) * T + (i + 1) * P],
                                           nkd[:, i, b, h, :, :].rearrange("p r d -> p (r d)"), ident)
            ins.then_inc(k_["kT"], 1)
            compress(1)
            pe.wait_ge(used[3], Q_CMP + 1)
            pe.nop().then_inc(k_["hid"], 1)

            def queries(src, x, b0, dst):
                pe.wait_ge(k_[src], 1)
                for a2 in range(8):
                    for i in range(TT):
                        ins = te.transpose(psum[:, b0 + a2 // 2, (a2 % 2) * T + i * P:(a2 % 2) * T + (i + 1) * P],
                                           x[:, i, 2 * a2:2 * a2 + 2, :].rearrange("p h d -> p (h d)"), ident)
                ins.then_inc(k_[dst], 1)
            pe.wait_ge(k_["kTs"], 4)
            queries("qn", nq, 0, "qT")
            pe.wait_ge(k_["hidst"], 1)
            pe.wait_ge(k_["gs"], 1)
            for j in range(2):
                for hh in range(2):
                    x = 2 * j + hh
                    ins = te.transpose(psum[:, 4, 128 + x * 60:188 + x * 60], hidt[0:60, j, hh * P:(hh + 1) * P], ident[0:60, 0:60])
            ins.then_inc(k_["hidT"], 1)
            pe.wait_ge(k_["hids"], 1)
            for j in range(2):
                for hh in range(2):
                    ins = mm(psum[0:60, 7, 64 * j:64 * j + 64], hid[:, j, hh, :], w2s[:, j, hh, :], hh == 0, hh == 1)
            ins.then_inc(k_["kc"], 1)
            pe.wait_ge(k_["kcs"], 1)
            selv = cst("selv").rearrange("p (h m) -> p h m", h=2)
            for j in range(2):
                ins = mm(psum[:, 5 + j, 0:DN], selv[0:60, j, :], kcv[0:60, 1, :])
            ins.then_inc(k_["vb"], 1)
            pe.wait_ge(k_["kcd"], 1)
            te.transpose(psum[:, 7, 256:316], kcd[0:60, :, :].rearrange("p j d -> p (j d)"), ident[0:60, 0:60]).then_inc(k_["kct"], 1)
            pe.wait_ge(k_["qTs"], 4)
            pe.wait_ge(k_["kcts"], 1)
            for i in range(TT):
                for hq in range(NH):
                    r = 64 * (hq % 2)
                    ins = mm(psum[:, 2 * i + hq % 2, hq // 2 * 16:hq // 2 * 16 + NCMP], nqT[r:r + 64, hq // 2, i * P:(i + 1) * P],
                             kcT[r:r + 64, :].rearrange("p (c h) -> p h c", h=NKV)[:, hq // NG, :])
            ins.then_inc(k_["cs"], 1)
            pe.wait_ge(k_["vbs"], 1)
            gate(2, 2)
            pe.wait_ge(bg_saved, 3)
            pe.wait_ge(ada_saved, M_L3 + 3)
            queries("qr", nqr, 4, "qrT")
            pe.wait_ge(k_["cp"], 1)
            for i in range(TT):
                for j in range(2):
                    ins = te.transpose(psum[:, 2, (2 * i + j) * P:(2 * i + j + 1) * P],
                                       pc[:, i, 8 * j:8 * j + 8, :].rearrange("p h c -> p (h c)"), ident)
            ins.then_inc(k_["cT"], 1)
            pe.wait_ge(k_["cTs"], 1)
            pe.wait_ge(k_["qrTs"], 4)
            for i in range(TT):
                for j in range(2):
                    ins = mm(psum[:, 4 + 2 * i + j, :], pcT[:, 2 * i + j, :], vbd[:, j, :, :].rearrange("p h d -> p (h d)"))
            ins.then_inc(k_["co"], 1)
            ada(M_L3 + 3, 3)
            pe.wait_ge(ada_saved, M_L3 + 4)
            for w in range(2 * NH + 2):
                if w < 2 * NH:
                    u = w
                    hq, b = u // 2, u % 2
                    r = 64 * (hq % 2)
                    if u >= 2:
                        pe.wait_ge(w_e, u - 1)
                    kT = nkT[r:r + 64, b, hq // NG, :]
                    mm(psum[:, u % 2, 0:384], identb[:], causb[:], True, False, True)
                    mm(psum[:, u % 2, 0:P], nqrT[r:r + 64, hq // 2, 0:P], kT[:, 0:P], False, False, True)
                    mm(psum[:, u % 2, P:384], nqrT[r:r + 64, hq // 2, P:T], kT, False, True, True).then_inc(w_s, 1)
                if 1 <= w <= 2 * NH:
                    u = w - 1
                    pe.wait_ge(w_e, u + 1)
                    if u >= 2:
                        pe.wait_ge(w_pts, u - 1)
                    for b in range(3):
                        ins = te.transpose(psum[:, 2 + u % 2, b * P:(b + 1) * P], pb2[:, u % 2, b * P:(b + 1) * P], ident)
                    ins.then_inc(w_pt, 1)
                if 2 <= w:
                    u = w - 2
                    hq, b = u // 2, u % 2
                    pe.wait_ge(w_pts, u + 1)
                    if u >= 2:
                        pe.wait_ge(w_os, u - 1)
                    else:
                        pe.wait_ge(k_["cos"], 2)
                    o = psum[:, 4 + u % 2, :]
                    vv = kv[:, :, 3 + 2 * b, hq // NG, :]
                    mm(o[:, 0:DN], pT2[:, u % 2, 0:P], vv[:, 0, :])
                    mm(o[:, DN:2 * DN], pT2[:, u % 2, P:T], vv[:, 0, :], True, False)
                    mm(o[:, DN:2 * DN], pT2[:, u % 2, T:384], vv[:, 1, :], False, True).then_inc(w_o, 1)
            pe.wait_ge(w_os, 2 * NH)
            turn(2, ob2.rearrange("p i h d -> p i (h d)"))
            pe.wait_ge(t_x, 12)
            accumulate(Q_NOUT, M_L3 + 4)
            pe.wait_ge(ada_saved, M_L3 + 5)
            ada(M_L3 + 5)
            pe.wait_ge(p_res, 10)
            pe.wait_ge(ada_saved, M_END)
            gate(3, 3)
            norm(5, gates=4)
            pe.wait_ge(n_x, 28)
            mlp2(Q_F2B, U_F2B, HT_F2B, 22)


_INS = ["x", "norm_mix_pre", "norm_mix_post", "norm_ffn_pre", "norm_ffn_post", "w_up", "w_down", "attn_w_qkv", "attn_w_o",
        "c_2", "ada_w_2", "ada_b_2", "norm_mix_2", "norm_ffn_2", "hgrn_w_in_2", "hgrn_out_norm_2", "hgrn_w_out_2",
        "kv_ada_w_2", "kv_ada_b_2", "kv_norm_2", "nsa_w_kv_2", "nsa_k_norm_2", "cmp_pos_2", "cmp_w1_2", "cmp_w2_2",
        "nsa_w_q_2", "nsa_q_norm_2", "nsa_w_out_2", "ffn_w_in_2", "ffn_w_out_2"]


def kernel(**inputs):
    import concourse.bacc as bacc
    from concourse.bass_utils import run_bass_kernel_spmd as run

    nc = bacc.Bacc("TRN2", target_bir_lowering=False, num_devices=1, dynamic_dma_scratch_size=2048)
    arrays, args = {}, {}
    given = {n: np.ascontiguousarray(inputs[n]) for n in _INS}
    for name, x in {**given, **constants()}.items():
        arrays["in_" + name] = x
        args[name] = nc.dram_tensor("in_" + name, x.shape, mybir.dt.from_np(x.dtype), kind="ExternalInput").ap()
    out = nc.dram_tensor("out_0", (1, T, D), F32, kind="ExternalOutput").ap()
    build(nc, args, out)
    r = run(nc, [arrays], core_ids=[0])
    return r.results[0]["out_0"]
```

```python
from contextlib import ExitStack

import numpy as np
import concourse.bass as bass
from concourse import mybir

F32 = mybir.dt.float32
F32R = mybir.dt.float32r
BF16 = mybir.dt.bfloat16
ALU = mybir.AluOpType
ACT = mybir.ActivationFunctionType
AX = mybir.AxisListType.X

P = 128
T = 256
TT = T // P
D = 1024
KD = D // P
H1, DH1 = 8, 128
FF1 = 4 * D
HH, DK = 8, 128
LEVELS = [64, 32, 16, 8, 4, 2, 1]
NL = len(LEVELS)
HIN_ORDER = (1, 0, 3, 2)
NH, NKV, NG, DN = 16, 4, 4, 64
FFN = -(-8 * D // (3 * 256)) * 256
CB, CS = 32, 16
NCMP = T // CS - CB // CS + 1
CHID = 256
EPS = 1e-6
NEG = -1e30

N_QKV, N_ACC, N_FF1, N_HIN, N_FF2, N_KV, N_Q = 3, 1, FF1 // 512, 4, FFN // 256, 2, 1
Q_QKV = 0
Q_WO = Q_QKV + N_QKV
Q_FF1 = Q_WO + N_ACC
Q_HIN = Q_FF1 + N_FF1
Q_HOUT = Q_HIN + N_HIN
Q_F2A = Q_HOUT + N_ACC
Q_KV = Q_F2A + N_FF2
Q_NQ = Q_KV + N_KV
Q_CMP = Q_NQ + N_Q
Q_NOUT = Q_CMP + 1
Q_F2B = Q_NOUT + N_ACC

ACC_END = (Q_WO, Q_FF1 + N_FF1 - 1, Q_HOUT, Q_F2A + N_FF2 - 1, Q_NOUT, Q_F2B + N_FF2 - 1)

G_HIN = 2 * N_QKV
G_KV = G_HIN + 2 * N_HIN
G_Q = G_KV + 2 * N_KV
G_END = G_Q + 2 * N_Q
HT_F2A = 2 * N_FF1
HT_F2B = HT_F2A + N_FF2

M_L0, M_L1, M_L2, M_KV, M_L3, M_END = 0, 6, 12, 18, 22, 28
A_QKV = 0
A_WO = A_QKV + N_QKV
A_FF1 = A_WO + 1
A_HIN = A_FF1 + N_FF1 - 1
A_HOUT = A_HIN + N_HIN
A_F2A = A_HOUT + 1
A_KV = A_F2A + N_FF2 - 1
assert A_KV + N_KV == M_END
LCOL = {0: 4 * M_L0, 1: 4 * M_L1, 2: 4 * M_L2, "kv": 4 * M_KV, 3: 4 * M_L3}

VR = {"mix_pre": 0, "ffn_pre": 8, "mix2": 16, "ffn2": 32, "kvn": 48, "c": 56, "pos": 64}


def constants():
    t = np.arange(P)
    ident = np.eye(P, dtype=np.float32)
    q, k = t[:, None], t[None, :]
    dist = np.concatenate([np.where(k <= q, k - q, NEG), k - (q + P) + 0 * q, np.where(k <= q, k - q, NEG)], 1)
    caus = np.concatenate([np.where(k <= q, 0, NEG), 0.0 * (k + q), np.where(k <= q, 0, NEG)], 1)
    ml = np.zeros((P, NL + 2, P), np.float32)
    mask = np.zeros((P, NL + 1, P), np.float32)
    u, x = t[:, None], t[None, :]
    for i, m in enumerate(LEVELS):
        mid = x // (2 * m) * (2 * m) + m
        second = x >= mid
        ml[:, i] = np.where(second, (u >= mid) & (u <= x), (u > x) & (u < mid))
        mask[:, i] = (u // (2 * m) == x // (2 * m)) & (u < mid) & (x >= mid)
    mask[:, NL] = ident
    ml[:, NL] = u > x
    ml[:, NL + 1] = u <= x
    inv = 1.0 / (10000.0 ** (np.arange(0, DN, 2, dtype=np.float32) / np.float32(DN)))
    ang = np.arange(T, dtype=np.float32)[:, None] * inv[None, :].astype(np.float32)
    rope = np.stack([np.cos(ang), np.sin(ang)], 1).astype(np.float32)
    rope = rope.reshape(TT, P, 2 * (DN // 2)).transpose(1, 0, 2).reshape(P, -1)
    tok = np.arange(T).reshape(TT, P).T
    seen = (np.arange(NCMP) * CS + CB - 1)[None, None, :] <= tok[:, :, None]
    cmask = np.stack([np.where(seen, 0.0, NEG), seen.astype(np.float64)], 1).reshape(P, -1)
    selv = np.zeros((P, 2, 8, 16), np.float32)
    for c in range(NCMP):
        for h in range(NKV):
            for hq in range(NH):
                if hq // NG == h:
                    selv[c * NKV + h, hq // 8, hq % 8, c] = 1
    bm = (t[:, None] // 16 == np.arange(8)[None, :]).astype(np.float32)
    f = lambda a: np.ascontiguousarray(a.reshape(P, -1), dtype=np.float32)
    return {
        "k_small": f(np.concatenate([ident, rope, cmask, bm, selv.reshape(P, -1)], 1)),
        "k_dist": f(np.concatenate([dist, caus], 1)),
        "k_levels": f(np.concatenate([ml.reshape(P, -1), mask.reshape(P, -1)], 1)),
    }


SMALL = {}
_o = 0
for _n, _w in (("ident", P), ("rope", TT * DN), ("cmask", 2 * TT * NCMP), ("bm", 8), ("selv", 256)):
    SMALL[_n] = (_o, _o + _w)
    _o += _w
SMALL_W = _o
LEV_W = (NL + 2) * P + (NL + 1) * P


def build(nc, a, out):
    with ExitStack() as ctx:
        def sb(name, shape, dt=F32):
            return ctx.enter_context(nc.sbuf_tensor(name, shape, dt))

        def sem(name):
            return ctx.enter_context(nc.semaphore(name))

        raw = sb("raw", [P, 4, 2048])
        whi = sb("whi", [P, 4, 2048], F32R)
        wlo = sb("wlo", [P, 4, 2048], F32R)
        adaw = sb("adaw", [P, 2, 2048])
        adaacc = sb("adaacc", [P, 512])
        xhi = sb("xhi", [P, KD, T], F32R)
        xlo = sb("xlo", [P, KD, T], F32R)
        hhi = sb("hhi", [P, 4, T], F32R)
        hlo = sb("hlo", [P, 4, T], F32R)
        res = sb("res", [P, TT, D])
        gain_b = sb("gain_b", [P, D])
        small = sb("small", [P, SMALL_W])
        vcol = sb("vcol", [P, 96])
        bcol = sb("bcol", [P, 4 * M_END])
        adacol = sb("adacol", [P, 4 * M_END])
        gs = sb("gs", [P, KD])
        sh = sb("sh", [P, KD])
        cact = sb("cact", [P, KD])
        ones = sb("ones", [P, 1])
        stat = sb("stat", [P, 64])
        ss = stat[:, 0:2]
        rstd = stat[:, 2:4]
        mhalf = stat[:, 4:36]
        onb = sb("onb", [P, DK])
        zrow = sb("zrow", [1, 512], BF16)
        identb = sb("identb", [P, P], BF16)
        causb = sb("causb", [P, 384], BF16)
        AR = 16592
        arena = sb("arena", [P, AR])
        psum = ctx.enter_context(nc.psum_tensor("psum", [P, 8, 512], F32))

        def cst(name):
            lo, hi_ = SMALL[name]
            return small[:, lo:hi_]
        ident = cst("ident")

        def area(lo, *shape):
            n = int(np.prod(shape))
            v = arena[:, lo:lo + n]
            if len(shape) == 1:
                return v
            names = "abcde"[:len(shape)]
            return v.rearrange(f"p ({' '.join(names)}) -> p {' '.join(names)}", **{k: s for k, s in zip(names, shape)})

        y = area(AR - 4096, TT, D)
        xf = area(AR - 2048, KD, T)
        vrow1 = area(11600, P)
        vrow2 = area(11728, P)
        dist = area(7936, 768)
        distb = area(11860, 192).bitcast(BF16)
        slopeb = area(7168, 512).bitcast(BF16).rearrange("p (h t) -> p h t", t=P)
        qkv = area(0, TT, 3 * D)
        qkT = area(6144, 2, 512)
        pb1 = area(7936, 2, 384)
        pT1 = area(8704, 2, 384)
        ob1 = area(9472, TT, D)
        st1 = area(11520, 2, 8)
        relu = area(0, TT, 512)
        sq = area(1024, 4, T)
        sil = area(2048, TT, T)
        gat = area(2560, TT, T)
        hin = area(0, 4, TT, D)
        hk = area(8192, TT, D)
        lev = area(10240, LEV_W)
        ML = lev[:, 0:(NL + 2) * P].rearrange("p (l t) -> p l t", t=P)
        MK = lev[:, (NL + 2) * P:LEV_W].rearrange("p (l t) -> p l t", t=P)
        spare = adaw[:].rearrange("p j (c l t) -> p (j c) l t", c=2, t=P)
        ee = [area(12416, NL + 1, P), area(13440, NL + 1, P)]
        qe = [area(14464, NL + 1, P), spare[:, 0]]
        ke = [spare[:, 1], spare[:, 2]]
        pm = spare[:, 3]
        qkTh = [area(15488, 2, T), adaacc[:].rearrange("p (j t) -> p j t", j=2)]
        am = [area(16000, 3, P), gain_b[:, 0:384].rearrange("p (j t) -> p j t", j=3)]
        ke7 = [area(16384, P), gain_b[:, 384:512]]
        ghi, glo = [x[:].rearrange("p k t -> p (k t)").rearrange("p (i n) -> p i n", i=TT) for x in (xhi, xlo)]
        MLr = hhi[:].rearrange("p k t -> p (k t)")
        MLx = hlo[:, 0, 0:P]
        hs = area(16512, 64)
        hsq = gain_b[:, 512:512 + 2 * DK].rearrange("p (i d) -> p i d", i=TT)
        kv = area(0, TT, 6, NKV, DN)
        nq = area(3072, TT, NH, DN)
        nqT = area(5120, 8, T)
        nkT = area(7168, 2, NKV, T)
        nqrT = area(9216, 8, T)
        nt1 = area(11264, 2048)
        kt2 = area(11264, 2, NKV, P)
        fl = area(5120, 2, CB // 2, NCMP, NKV)
        pT2 = area(5120, 2, 384)
        nqr = area(9216, TT, NH, DN)
        nkd = area(9216, TT, 2, NKV, 2, DN)
        hid = area(13312, 2, 2, NCMP * NKV)
        hidt = area(16080, 2, CHID)
        kcv = area(13552, 2, DN)
        kcd = area(13680, 2, DN)
        kcB = area(13312, NKV, 2, 16)
        vbd = area(13872, 2, 8, DN)
        w2s = area(14896, 2, 2, DN)
        wgs = area(15152, KD, 48)
        wgh, wgl = [x[:].rearrange("p k t -> p (k t)")[:, 0:KD * 48] for x in (hhi, hlo)]
        gat3 = area(15536, TT, 48)
        knb = area(15632, 4, DN)
        nst = area(15888, 192)
        pc = area(11264, TT, NH, 16)
        pb2 = area(12544, 2, 384)
        pcT = area(16080, 4, P)
        ob2 = area(3072, TT, NH, DN)

        raw_full = [sem(f"raw_full{s}") for s in range(4)]
        hi_ready = [sem(f"hi_ready{s}") for s in range(4)]
        lo_ready = [sem(f"lo_ready{s}") for s in range(4)]
        used = [sem(f"used{s}") for s in range(4)]
        ada_full = [sem(f"ada_full{s}") for s in range(2)]
        ada_used = [sem(f"ada_used{s}") for s in range(2)]
        ada_step, ada_turned, ada_saved = sem("ada_step"), sem("ada_turned"), sem("ada_saved")
        consts_in, x_in, vec_in = sem("consts_in"), [sem(f"x_in{i}") for i in range(TT)], sem("vec_in")
        vec_turned, vec_saved, c_ready, ones_set = sem("vec_turned"), sem("vec_saved"), sem("c_ready"), sem("ones_set")
        gain_in = sem("gain_in")
        n_sq, n_rstd, n_y, n_turned, n_affine, n_hi, n_x = [sem("n_" + s) for s in ("sq", "rstd", "y", "turned", "affine", "hi", "x")]
        aff_ready = sem("aff_ready")
        p_sq, p_rstd, p_res = [sem("p_" + s) for s in ("sq", "rstd", "res")]
        evac_a, evac_d = sem("evac_a"), sem("evac_d")
        acc_done = sem("acc_done")
        act_done, gate_done, h_turned, h_sq, h_hi, h_lo = [sem(s) for s in ("act_done", "gate_done", "h_turned", "h_sq", "h_hi", "h_lo")]
        bg_turned, bg_saved = sem("bg_turned"), sem("bg_saved")
        a_qk, a_qks, a_s, a_m, a_e, a_pt, a_pts, a_o, a_os = [sem("a_" + s) for s in ("qk", "qks", "s", "m", "e", "pt", "pts", "o", "os")]
        t_turned, t_hi, t_x = sem("t_turned"), sem("t_hi"), sem("t_x")
        lev_in, onb_in, dist_in, bias_ready = sem("lev_in"), sem("onb_in"), sem("dist_in"), sem("bias_ready")
        g_d, g_f = sem("g_d"), sem("g_f")
        r_qk, r_qks, r_e, r_ee, r_z, r_k, r_s, r_m, r_am, r_o, r_os = [
            sem("r_" + s) for s in ("qk", "qks", "e", "ee", "z", "k", "s", "m", "am", "o", "os")]
        r_k7 = sem("r_k7")
        g_hi, g_lo, ml_ready, s_zero = sem("g_hi"), sem("g_lo"), sem("ml_ready"), sem("s_zero")
        r_ms, r_rs, r_n = sem("r_ms"), sem("r_rs"), sem("r_n")
        nsa_in, knb_in = sem("nsa_in"), sem("knb_in")
        dve, actc, poolc = sem("dve_chain"), sem("act_chain"), sem("pool_chain")
        k_ = {n: sem("k_" + n) for n in ("even", "evens", "wgh", "wgl", "flat", "hid", "hidst", "hidT", "hids", "kc", "kcs", "sq", "rs", "kcd", "kct", "kcts",
                                         "vb", "vbs", "krope", "kT", "kTs", "g", "gs", "qsq", "qn", "qT", "qTs", "qr", "qrT", "qrTs",
                                         "cs", "cm", "ce", "cp", "cT", "cTs", "co", "cos")}
        w_s, w_m, w_e, w_pt, w_pts, w_o, w_os = [sem("w_" + s) for s in ("s", "m", "e", "pt", "pts", "o", "os")]
        out_done = sem("out_done")

        def wait(eng, s, v):
            if not isinstance(v, int) or v > 0:
                eng.wait_ge(s, v)

        class Chain:
            def __init__(self, eng, s):
                self.eng, self.s, self.n = eng, s, 0

            def __call__(self, ins):
                self.n += 1
                ins.then_inc(self.s, 1)
                self.eng.wait_ge(self.s, self.n)

        block = ctx.enter_context(nc.Block())

        @block.sync
        def _(sp):
            def free_slot(s, n):
                if isinstance(n, int) and n == Q_CMP + 1:
                    sp.wait_ge(used[s], n)
                elif not isinstance(n, int) or n > 0:
                    wait(sp, hi_ready[s], n)
                    wait(sp, lo_ready[s], n)

            def wide(w, s, n, nb, width=512):
                free_slot(s, n)
                v = w.rearrange("(h kt p) n -> h p kt n", h=2, p=P)[s % 2]
                dst = raw[:, s, 0:4 * width].rearrange("p (k n) -> p k n", k=4)
                sp.dma_start(dst, v[:, :, bass.ds(nb * width, width)]).then_inc(raw_full[s], 32)

            def deep(w, s, n, g, kt=2):
                free_slot(s, n)
                v = w.rearrange("(r p) n -> p r n", p=P)
                dst = raw[:, s, 0:kt * D].rearrange("p (k n) -> p k n", k=kt)
                sp.dma_start(dst, v[:, bass.ds(g * kt, kt), :]).then_inc(raw_full[s], 32)

            def gated(w, s, n, fb):
                free_slot(s, n)
                v = w.rearrange("(h kt p) n -> h p kt n", h=2, p=P)[s % 2]
                dst = raw[:, s, :].rearrange("p (k n) -> p k n", k=4)
                sp.dma_start(dst[:, :, 0:256], v[:, :, bass.ds(fb * 256, 256)]).then_inc(raw_full[s], 16)
                sp.dma_start(dst[:, :, 256:512], v[:, :, bass.ds(fb * 256 + FFN, 256)]).then_inc(raw_full[s], 16)

            def ada(w, half, m, nb):
                if not isinstance(m, int) or m > 0:
                    sp.wait_ge(ada_used[half], m)
                v = w.rearrange("(h kt p) n -> h p kt n", h=2, p=P)[half]
                dst = adaw[:, half, :].rearrange("p (k n) -> p k n", k=4)
                sp.dma_start(dst, v[:, :, bass.ds(nb * 512, 512)]).then_inc(ada_full[half], 16)

            def ada_block(m, half):
                w, m0 = (a["kv_ada_w_2"], M_KV) if M_KV <= m < M_L3 else (a["ada_w_2"][m // 6 if m < M_KV else 3], 6 * (m // 6) if m < M_KV else M_L3)
                ada(w, half, m, m - m0)

            sp.dma_start(small[:], a["k_small"]).then_inc(consts_in, 16)
            for i in range(TT):
                sp.dma_start(res[:, i, :], a["x"][0].rearrange("(i p) d -> p i d", p=P)[:, i, :]).then_inc(x_in[i], 16)
            for name, src in (("mix_pre", a["norm_mix_pre"]), ("ffn_pre", a["norm_ffn_pre"]), ("mix2", a["norm_mix_2"]),
                              ("ffn2", a["norm_ffn_2"]), ("c", a["c_2"])):
                r = src.rearrange("l (k p) -> (l k) p", p=P)
                sp.dma_start(vrow1[VR[name]:VR[name] + r.shape[0], :], r).then_inc(vec_in, 16)
            sp.dma_start(vrow1[VR["kvn"]:VR["kvn"] + 8, :], a["kv_norm_2"].rearrange("(k p) -> k p", p=P)).then_inc(vec_in, 16)
            sp.dma_start(vrow1[VR["pos"]:VR["pos"] + 32, :],
                         a["cmp_pos_2"].rearrange("j (a r) d -> (j a) (r d)", r=2)).then_inc(vec_in, 16)
            sp.dma_start(vrow2[0:72, :], a["ada_b_2"][0:3].rearrange("l (k p) -> (l k) p", p=P)).then_inc(vec_in, 16)
            sp.dma_start(vrow2[72:88, :], a["kv_ada_b_2"].rearrange("(k p) -> k p", p=P)).then_inc(vec_in, 16)
            sp.dma_start(vrow2[88:112, :], a["ada_b_2"][3:4].rearrange("l (k p) -> (l k) p", p=P)).then_inc(vec_in, 16)
            w = a["attn_w_qkv"][0]
            for s in range(4):
                wide(w, s, 0, s // 2)
            sp.dma_start(dist, a["k_dist"]).then_inc(dist_in, 16)
            for t in range(1, N_QKV + 1):
                for s in range(4):
                    if t < N_QKV:
                        wide(w, s, t + Q_QKV, 2 * t + s // 2)
                    else:
                        deep(a["attn_w_o"][0], s, Q_WO, s)
                    if s < 2:
                        ada_block(A_QKV + t - 1, s)
            up, dn = a["w_up"][0], a["w_down"][0]
            for half in range(2):
                ada_block(A_WO, half)
            for s in (0, 1):
                wide(up, s, Q_FF1, 0)

            def mlp1(t, l=None, back=0):
                wide(up, 0, t + Q_FF1 + 1, t + 1)
                if l is not None:
                    ada(a["ada_w_2"][l], 0, t + (A_FF1 - 1), t - back)
                    ada(a["ada_w_2"][l], 1, t + (A_FF1 - 1), t - back)
                wide(up, 1, t + Q_FF1 + 1, t + 1)
                deep(dn, 2, t + Q_FF1, 2 * t)
                deep(dn, 3, t + Q_FF1, 2 * t + 1)
            mlp1(0)
            for t in (1, 2):
                mlp1(t, 0, M_L0 - (A_FF1 - 1))
            with sp.Fori(3, N_FF1 - 1) as t:
                mlp1(t, 1, M_L1 - (A_FF1 - 1))
            w = a["hgrn_w_in_2"][0]
            wide(w, 0, Q_HIN, 2 * HIN_ORDER[0])
            for half in range(2):
                ada_block(A_FF1 + N_FF1 - 2, half)
            wide(w, 1, Q_HIN, 2 * HIN_ORDER[0])
            deep(dn, 2, Q_FF1 + 7, 14)
            deep(dn, 3, Q_FF1 + 7, 15)
            for t, sec in enumerate((*HIN_ORDER, None)):
                for s in range(4) if t else (2, 3):
                    if sec is not None:
                        wide(w, s, Q_HIN + t, 2 * sec + s // 2)
                    else:
                        deep(a["hgrn_w_out_2"][0], s, Q_HOUT, s)
                    if t and s < 2:
                        ada_block(A_HIN + t - 1, s)

            def mlp2(layer, q0, t, ada_a=None, last=False):
                up2, dn2 = a["ffn_w_in_2"][layer], a["ffn_w_out_2"][layer]
                if not last:
                    gated(up2, 0, t + q0 + 1, t + 1)
                if ada_a:
                    ada(ada_a[0], 0, ada_a[1], ada_a[2])
                    ada(ada_a[0], 1, ada_a[1], ada_a[2])
                if not last:
                    gated(up2, 1, t + q0 + 1, t + 1)
                deep(dn2, 2, t + q0, 2 * t, kt=1)
                deep(dn2, 3, t + q0, 2 * t + 1, kt=1)

            gated(a["ffn_w_in_2"][0], 0, Q_F2A, 0)
            gated(a["ffn_w_in_2"][0], 1, Q_F2A, 0)
            sp.wait_ge(r_am, 2 * HH)
            for half in range(2):
                ada_block(A_HOUT, half)
            mlp2(0, Q_F2A, 0)
            f2a = A_F2A - 1
            for t in (1, 2):
                mlp2(0, Q_F2A, t, (a["ada_w_2"][2], t + f2a, t + f2a - M_L2))
            with sp.Fori(M_KV - f2a, M_L3 - f2a) as t:
                mlp2(0, Q_F2A, t, (a["kv_ada_w_2"], t + f2a, t - (M_KV - f2a)))
            with sp.Fori(M_L3 - f2a, N_FF2 - 1) as t:
                mlp2(0, Q_F2A, t, (a["ada_w_2"][3], t + f2a, t - (M_L3 - f2a)))
            w = a["nsa_w_kv_2"]
            wide(w, 0, Q_KV, 0, 384)
            for half in range(2):
                ada_block(A_KV - 1, half)
            wide(w, 1, Q_KV, 0, 384)
            mlp2(0, Q_F2A, 10, last=True)
            for s in (2, 3):
                wide(w, s, Q_KV, s // 2, 384)
            for s in range(4):
                wide(w, s, Q_KV + 1, 2 + s // 2, 384)
                if s < 2:
                    ada_block(A_KV, s)
            for s in range(4):
                wide(a["nsa_w_q_2"][0], s, Q_NQ, s // 2)
                if s < 2:
                    ada_block(A_KV + 1, s)
            for s in range(4):
                free_slot(s, Q_CMP)
                sp.dma_start(raw[:, s, :].rearrange("p (k n) -> p k n", k=8),
                             a["cmp_w1_2"][s // 2].rearrange("(g k p) n -> g p k n", g=2, p=P)[s % 2]).then_inc(raw_full[s], 32)
            for s in range(4):
                deep(a["nsa_w_out_2"][0], s, Q_NOUT, s)
            for s in range(2):
                gated(a["ffn_w_in_2"][1], s, Q_F2B, 0)
            with sp.Fori(0, 10) as t:
                mlp2(1, Q_F2B, t)
            mlp2(1, Q_F2B, 10, last=True)
            for i in range(TT):
                sp.wait_ge(p_res, 11 + i)
                sp.dma_start(out[0].rearrange("(i p) d -> p i d", p=P)[:, i, :], res[:, i, :]).then_inc(out_done, 16)
            sp.wait_ge(out_done, 32)

        @block.gpsimd
        def _(pool):
            gp = nc.gpsimd
            chain = Chain(pool, poolc)
            gp.memset(mhalf, -0.5)
            gp.memset(zrow[:], 0.0)
            chain(gp.memset(ones[:], 1.0))
            pool.nop().then_inc(ones_set, 1)

            def rsqrt(src, dst, tmp, n, mean, done):
                chain(gp.tensor_scalar(tmp, src, mean, EPS, ALU.mult, ALU.add))
                gp.tensor_tensor(dst, tmp, n, ALU.pow).then_inc(done, 1)

            def norm(j):
                for i in range(TT):
                    pool.wait_ge(n_sq, 2 * j + i + 1)
                    rsqrt(ss[:, i:i + 1], rstd[:, i:i + 1], stat[:, 40 + i:41 + i], mhalf[:, 0:1], 1.0 / D, n_rstd)

            def post(k):
                for i in range(TT):
                    pool.wait_ge(p_sq, 2 * k + i + 1)
                    rsqrt(stat[:, 36 + i:37 + i], stat[:, 38 + i:39 + i], stat[:, 42 + i:43 + i], mhalf[:, 0:1], 1.0 / D, p_rstd)

            norm(0)
            gp.dma_start(onb[:], a["hgrn_out_norm_2"][0].partition_broadcast(P)).then_inc(onb_in, 16)
            gp.dma_start(gain_b[:], a["norm_mix_post"][0].partition_broadcast(P)).then_inc(gain_in, 16)
            post(0)
            pool.wait_ge(p_res, 2)
            gp.dma_start(gain_b[:], a["norm_ffn_post"][0].partition_broadcast(P)).then_inc(gain_in, 16)
            norm(1)
            post(1)
            pool.wait_ge(p_res, 4)
            norm(2)
            gp.dma_start(lev, a["k_levels"]).then_inc(lev_in, 16)
            pool.wait_ge(ada_used[0], A_HOUT)
            pool.wait_ge(ada_used[1], A_HOUT)
            for n in range(2 * HH):
                h, i = n // 2, n % 2
                if i == 0:
                    pool.wait_ge(r_qks, h + 1)
                pool.wait_ge(r_ee, n + 1)
                if n >= 2:
                    pool.wait_ge(r_s, n - i)
                kT = qkTh[h % 2][:, 1, i * P:(i + 1) * P]
                gp.tensor_tensor(ke[i][:, 0:NL, :], ee[i][:, 0:NL, :], kT.unsqueeze(1).to_broadcast([P, NL, P]),
                                 ALU.mult).then_inc(r_k, 1)
                if i == 0:
                    gp.tensor_tensor(ke7[h % 2], ee[0][:, NL, :], kT, ALU.mult).then_inc(r_k7, 1)
            pool.wait_ge(r_ms, HH)
            rsqrt(hs[:, 0:16], hs[:, 16:32], hs[:, 32:48], mhalf[:, 0:16], 1.0 / DK, r_rs)
            norm(3)
            norm(4)
            pool.wait_ge(n_x, 24)
            pool.wait_ge(n_turned, 20)
            with nc.allow_non_contiguous_dma(reason="small operands"):
                gp.dma_start(knb[:, 0:3, :], a["nsa_k_norm_2"].rearrange("j d -> (j d)").partition_broadcast(P)
                             .rearrange("p (j d) -> p j d", d=DN)).then_inc(knb_in, 16)
                gp.dma_start(knb[:, 3, :], a["nsa_q_norm_2"][0].partition_broadcast(P)).then_inc(knb_in, 16)
                gp.dma_start(wgs, a["nsa_w_q_2"][0].rearrange("(k p) n -> p k n", p=P)[:, :, D:D + 48]).then_inc(nsa_in, 16)
                gp.dma_start(w2s, a["cmp_w2_2"].rearrange("j (h p) d -> p j h d", p=P)).then_inc(nsa_in, 16)
            pool.wait_ge(k_["sq"], 1)
            rsqrt(nst[:, 16:32], nst[:, 32:48], nst[:, 48:64], mhalf[:, 0:16], 1.0 / DN, k_["rs"])
            pool.wait_ge(k_["sq"], 2)
            rsqrt(nst[:, 64:96], nst[:, 96:128], nst[:, 128:160], mhalf[:, 0:32], 1.0 / DN, k_["rs"])
            pool.wait_ge(k_["sq"], 3)
            rsqrt(nst[0:60, 0:1], nst[0:60, 1:2], nst[0:60, 2:3], mhalf[0:60, 0:1], 1.0 / DN, k_["rs"])
            norm(5)

        @block.scalar
        def _(act):
            sc = nc.scalar
            chain = Chain(act, actc)

            def split(s, n, width=2048):
                act.wait_ge(raw_full[s], 32 * n + 32)
                if not isinstance(n, int) or n > 0:
                    act.wait_ge(used[s], n)
                sc.copy(whi[:, s, 0:width], raw[:, s, 0:width]).then_inc(hi_ready[s], 1)

            def norm(k, j):
                for i in range(TT):
                    act.wait_ge(p_res, 2 * (j - 1) + i + 1)
                    sc.activation(y[:, i, :], res[:, i, :], ACT.Square, accum_out=ss[:, i:i + 1]).then_inc(n_sq, 1)
                norm_high(k)

            def norm_high(k):
                for b in range(4):
                    act.wait_ge(n_affine, 4 * k + b + 1)
                    sc.copy(xhi[:, 2 * b:2 * b + 2, :], xf[:, 2 * b:2 * b + 2, :]).then_inc(n_hi, 1)

            def post(k):
                for i in range(TT):
                    if i == 0:
                        act.wait_ge(acc_done, k + 1)
                    else:
                        act.wait_ge(used[3], ACC_END[k] + 1)
                    sc.activation(y[:, i, :], psum[:, 2 * i:2 * i + 2, :].rearrange("p b n -> p (b n)"), ACT.Square,
                                  accum_out=stat[:, 36 + i:37 + i]).then_inc(p_sq, 1)

            def turn(k):
                for b in range(4):
                    act.wait_ge(t_turned, 4 * k + b + 1)
                    sc.copy(xhi[:, 2 * b:2 * b + 2, :], psum[:, 4 + b, :].rearrange("p (k t) -> p k t", k=2)).then_inc(t_hi, 1)

            def evac(n, p, dst):
                act.wait_ge(used[2 * p + 1], n + 1)
                sc.copy(dst, psum[:, 2 * p, 0:dst.shape[-1]]).then_inc(evac_a, 1)

            for i in range(TT):
                act.wait_ge(x_in[i], 16)
                sc.activation(y[:, i, :], res[:, i, :], ACT.Square, accum_out=ss[:, i:i + 1]).then_inc(n_sq, 1)
            act.wait_ge(vec_turned, 1)
            sc.copy(vcol[:], psum[:, 0, 0:96]).then_inc(vec_saved, 1)
            sc.copy(bcol[:], psum[:, 0, 128:128 + 112]).then_inc(vec_saved, 1)
            split(0, Q_QKV)
            norm_high(0)
            for s in (1, 2, 3):
                split(s, Q_QKV)
            act.wait_ge(vec_saved, 1)
            sc.activation(cact[:], vcol[:, VR["c"]:VR["c"] + 8], ACT.Silu).then_inc(c_ready, 1)
            act.wait_ge(dist_in, 16)
            sc.copy(distb, dist[:, 0:384])
            sc.copy(causb[:], dist[:, 384:768])
            sc.copy(identb[:], ident)
            for h in range(H1):
                ins = sc.mul(slopeb[:, h, :], ident, 2.0 ** -(8.0 * (h + 1) / H1))
            ins.then_inc(bias_ready, 1)
            act.wait_ge(bias_ready, 1)
            with act.Fori(0, N_QKV) as t:
                for p in range(2):
                    split(2 * p, t + 1)
                    evac(t + Q_QKV, p, qkv[:, 0, bass.ds(t * 1024 + p * 512, 512)])
                    split(2 * p + 1, t + 1)

            for h in range(H1 + 1):
                if h < H1:
                    act.wait_ge(a_qk, h + 1)
                    if h >= 2:
                        act.wait_ge(a_s, h - 1)
                    sc.mul(qkT[:, h % 2, 0:T], psum[:, h % 2, 0:T], DH1 ** -0.5)
                    sc.copy(qkT[:, h % 2, T:2 * T], psum[:, h % 2, T:2 * T]).then_inc(a_qks, 1)
                if h >= 1:
                    g = h - 1
                    act.wait_ge(a_m, g + 1)
                    if g >= 2:
                        act.wait_ge(a_pts, g - 1)
                    m = st1[:, g % 2, :]
                    sc.activation(pb1[:, g % 2, 0:P], psum[:, 2 + g % 2, 0:P], ACT.Exp, bias=m[:, 0:1], accum_out=m[:, 2:3])
                    sc.activation(pb1[:, g % 2, P:384], psum[:, 2 + g % 2, P:384], ACT.Exp, bias=m[:, 1:2],
                                  accum_out=m[:, 3:4]).then_inc(a_e, 1)
            turn(0)
            split(0, Q_FF1)
            split(1, Q_FF1)
            post(0)
            norm(1, 1)
            split(2, Q_FF1)
            split(3, Q_FF1)

            def mlp1(t, first=False):
                split(0, t + (Q_FF1 + 1))
                act.wait_ge(used[1], t + (Q_FF1 + 1))
                for i in range(TT):
                    sc.activation(relu[:, i, :], psum[:, 4 + i, :], ACT.Relu).then_inc(act_done, 1)
                split(1, t + (Q_FF1 + 1))
                if not first:
                    split(2, t + Q_FF1)
                for b in range(2):
                    act.wait_ge(h_turned, 2 * t + b + 1)
                    sc.activation(sq[:, 2 * b:2 * b + 2, :], psum[:, 6 + b, :].rearrange("p (k t) -> p k t", k=2),
                                  ACT.Square).then_inc(h_sq, 1)
                    act.wait_ge(h_sq, 2 * t + b + 1)
                    sc.copy(hhi[:, 2 * b:2 * b + 2, :], sq[:, 2 * b:2 * b + 2, :]).then_inc(h_hi, 1)
                if not first:
                    split(3, t + Q_FF1)
            mlp1(0, True)
            with act.Fori(1, N_FF1) as t:
                mlp1(t)
            split(2, Q_HIN)
            post(1)
            norm(2, 2)
            split(3, Q_HIN)
            tmp = area(12416, TT, D)

            def act_of(t):
                sec = HIN_ORDER[t]
                act.wait_ge(evac_d, G_HIN + 2 * t + 2)
                act.wait_ge(evac_a, G_HIN + 2 * t + 2)
                x = hin[:, sec, :, :]
                if sec == 1:
                    chain(sc.activation(tmp, x, ACT.Abs))
                    chain(sc.activation(tmp, tmp, ACT.Exp, scale=-1.0))
                    chain(sc.activation(tmp, tmp, ACT.Ln, bias=1.0))
                    sc.activation(hk, x, ACT.Sigmoid, scale=-1.0).then_inc(g_f, 1)
                elif sec != 2:
                    sc.activation(x, x, ACT.Silu).then_inc(g_f, 1)

            for t, sec in enumerate(HIN_ORDER):
                for p in range(2):
                    split(2 * p, Q_HIN + t + 1)
                    evac(Q_HIN + t, p, hin[:, sec, 0, p * 512:(p + 1) * 512])
                    split(2 * p + 1, Q_HIN + t + 1)
                    if p == 0 and t:
                        act_of(t - 1)
            act_of(3)
            act.wait_ge(lev_in, 16)
            act.wait_ge(h_lo, 2 * N_FF1)
            act.wait_ge(used[3], Q_HIN)
            sc.copy(MLr, ML[:, 0:NL + 1, :].rearrange("p l t -> p (l t)"))
            sc.copy(MLx, ML[:, NL + 1, :]).then_inc(ml_ready, 1)
            act.wait_ge(g_d, 1)
            act.wait_ge(used[3], Q_HOUT)
            act.wait_ge(ada_turned, A_HOUT)
            for b in range(4):
                sc.copy(ghi[:, :, b * 256:(b + 1) * 256], hin[:, 1, :, b * 256:(b + 1) * 256]).then_inc(g_hi, 1)

            def qk_save(h):
                act.wait_ge(r_qk, h + 1)
                if h >= 2:
                    act.wait_ge(r_s, 2 * h - 2)
                sc.copy(qkTh[h % 2].rearrange("p j t -> p (j t)"), psum[:, 0, :]).then_inc(r_qks, 1)

            def exps(n):
                act.wait_ge(r_e, n + 1)
                if n >= 2:
                    act.wait_ge(r_z, n - 1)
                    act.wait_ge(r_k, n - 1)
                    if n % 2 == 0:
                        act.wait_ge(r_k7, n // 2)
                b = 1 + 2 * (n % 2)
                sc.activation(ee[n % 2], psum[:, b:b + 2, :].rearrange("p b (l t) -> p (b l) t", t=P), ACT.Exp).then_inc(r_ee, 1)

            def out_save(h):
                act.wait_ge(r_o, h + 1)
                wait(act, r_ms, h)
                for i in range(TT):
                    ins = sc.activation(hsq[:, i, :], psum[:, 7, (1 + i) * P:(2 + i) * P], ACT.Square,
                                        accum_out=hs[:, 8 * i + h:8 * i + h + 1])
                ins.then_inc(r_ms, 1)
                sc.copy(hin[:, 0, :, h * DK:(h + 1) * DK],
                        psum[:, 7, P:3 * P].rearrange("p (i d) -> p i d", i=2)).then_inc(r_os, 1)

            qk_save(0)
            exps(0)
            exps(1)
            for n in range(2 * HH):
                if n % 2 == 0 and n // 2 + 1 < HH:
                    qk_save(n // 2 + 1)
                if n + 2 < 2 * HH:
                    exps(n + 2)
                if n % 2 == 0 and n:
                    out_save(n // 2 - 1)
            out_save(HH - 1)
            turn(1)
            split(0, Q_F2A)
            split(1, Q_F2A)
            norm(3, 3)
            split(2, Q_F2A, 1024)
            split(3, Q_F2A, 1024)

            def mlp2(t, q0, hb, first=False, nxt=2048, last=False):
                if not last:
                    split(0, t + (q0 + 1), nxt)
                act.wait_ge(used[1], t + (q0 + 1))
                for i in range(TT):
                    sc.activation(sil[:, i, :], psum[:, 4 + i, 0:256], ACT.Silu).then_inc(act_done, 1)
                if not last:
                    split(1, t + (q0 + 1), nxt)
                if not first:
                    split(2, t + q0, 1024)
                act.wait_ge(h_turned, t + (hb + 1))
                sc.copy(hhi[:, 0:2, :], psum[:, 6, :].rearrange("p (k t) -> p k t", k=2)).then_inc(h_hi, 1)
                if not first:
                    split(3, t + q0, 1024)
            mlp2(0, Q_F2A, HT_F2A, first=True)
            with act.Fori(1, N_FF2 - 1) as t:
                mlp2(t, Q_F2A, HT_F2A)
            mlp2(N_FF2 - 1, Q_F2A, HT_F2A, nxt=1536)
            split(2, Q_KV, 1536)
            norm(4, 4)
            split(3, Q_KV, 1536)
            kvf = area(0, TT, 1536)
            for t in range(N_KV):
                for p in range(2):
                    for s in (2 * p, 2 * p + 1):
                        if t == 0:
                            split(s, Q_KV + 1, 1536)
                        elif p == 0:
                            split(s, Q_NQ)
                    evac(Q_KV + t, p, kvf[:, 0, (2 * t + p) * 384:(2 * t + p + 1) * 384])
            act.wait_ge(used[3], Q_NQ)
            norm_high(5)
            for s in (2, 3):
                split(s, Q_NQ)
            act.wait_ge(k_["even"], 1)
            sc.copy(kt2.rearrange("p j h m -> p j (h m)"), psum[:, 5:7, :]).then_inc(k_["evens"], 1)
            act.wait_ge(nsa_in, 32)
            sc.copy(wgh, wgs.rearrange("p k n -> p (k n)")).then_inc(k_["wgh"], 1)
            nqf = area(3072, TT, D)
            for p in range(2):
                evac(Q_NQ, p, nqf[:, 0, p * 512:(p + 1) * 512])
            act.wait_ge(evac_d, G_END)
            act.wait_ge(evac_a, G_END)
            act.wait_ge(k_["krope"], 1)
            sc.activation(nt1, nqf.rearrange("p i n -> p (i n)"), ACT.Square).then_inc(k_["qsq"], 1)
            act.wait_ge(k_["g"], 1)
            sc.activation(gat3, psum[:, 4, 0:96].rearrange("p (i n) -> p i n", i=2), ACT.Sigmoid).then_inc(k_["gs"], 1)
            act.wait_ge(k_["kT"], 1)
            for b in range(4):
                sc.copy(nkT.rearrange("p b h t -> p (b h) t")[:, 2 * b:2 * b + 2, :],
                        psum[:, b, :].rearrange("p (k t) -> p k t", k=2)).then_inc(k_["kTs"], 1)

            def turned_save(src, dst, b0):
                act.wait_ge(k_[src], 1)
                for b in range(4):
                    sc.copy(dst[:, 2 * b:2 * b + 2, :],
                            psum[:, b0 + b, :].rearrange("p (k t) -> p k t", k=2)).then_inc(k_[src + "s"], 1)
            act.wait_ge(k_["hid"], 1)
            sc.activation(hidt[0:60, :, :], psum[0:60, 7, :].rearrange("p (j n) -> p j n", j=2), ACT.Silu).then_inc(k_["hidst"], 1)
            turned_save("qT", nqT, 0)
            act.wait_ge(k_["hidT"], 1)
            sc.copy(hid.rearrange("p j h c -> p (j h c)"), psum[:, 4, 128:368]).then_inc(k_["hids"], 1)
            for s in range(4):
                act.nop().then_inc(hi_ready[s], 1)
                split(s, Q_NOUT)
            act.wait_ge(k_["cm"], 1)
            for i in range(TT):
                last = sc.activation(pc[:, i, :, 0:NCMP], pc[:, i, :, 0:NCMP], ACT.Exp)
            last.then_inc(k_["ce"], 1)
            act.wait_ge(k_["cT"], 1)
            sc.copy(pcT.rearrange("p j t -> p (j t)"), psum[:, 2, :]).then_inc(k_["cTs"], 1)
            turned_save("qrT", nqrT, 4)
            act.wait_ge(k_["co"], 1)
            for i in range(TT):
                sc.copy(ob2[:, i, :, :].rearrange("p h d -> p (h d)"),
                        psum[:, 4 + 2 * i:6 + 2 * i, :].rearrange("p b n -> p (b n)")).then_inc(k_["cos"], 1)
            for u in range(2 * NH):
                act.wait_ge(w_m, u + 1)
                if u >= 2:
                    act.wait_ge(w_pts, u - 1)
                m = nst[:, 8 * (u % 2):8 * (u % 2) + 8]
                sc.activation(pb2[:, u % 2, 0:P], psum[:, u % 2, 0:P], ACT.Exp, bias=m[:, 0:1], accum_out=m[:, 2:3])
                sc.activation(pb2[:, u % 2, P:384], psum[:, u % 2, P:384], ACT.Exp, bias=m[:, 1:2],
                              accum_out=m[:, 3:4]).then_inc(w_e, 1)
            turn(2)
            split(0, Q_F2B)
            split(1, Q_F2B)
            norm(6, 5)
            split(2, Q_F2B, 1024)
            split(3, Q_F2B, 1024)
            mlp2(0, Q_F2B, HT_F2B, first=True)
            with act.Fori(1, N_FF2 - 1) as t:
                mlp2(t, Q_F2B, HT_F2B)
            mlp2(N_FF2 - 1, Q_F2B, HT_F2B, last=True)

        @block.vector
        def _(v):
            ve = nc.vector
            chain = Chain(v, dve)

            def split(s, n, width=2048):
                v.wait_ge(hi_ready[s], n + 1)
                ve.tensor_tensor(wlo[:, s, 0:width], raw[:, s, 0:width], whi[:, s, 0:width].bitcast(F32),
                                 ALU.subtract).then_inc(lo_ready[s], 1)

            def ada(m, half):
                v.wait_ge(ada_full[half], 16 * m + 16)
                for k in range(4):
                    w = adaw[:, half, k * 512:(k + 1) * 512]
                    c = cact[:, 4 * half + k:4 * half + k + 1]
                    if k:
                        v.wait_ge(ada_step, 6 * m + 3 * half + k)
                    elif half:
                        v.wait_ge(ada_used[0], m + 1)
                    elif not isinstance(m, int) or m > 0:
                        v.wait_ge(ada_turned, m)
                    if half == 0 and k == 0:
                        ins = ve.tensor_scalar(adaacc[:], w, c, None, ALU.mult)
                    else:
                        ins = ve.scalar_tensor_tensor(adaacc[:], w, c, adaacc[:], ALU.mult, ALU.add)
                    ins.then_inc(ada_used[half] if k == 3 else ada_step, 1)

            def ada_save(m, bank=7):
                v.wait_ge(ada_turned, m + 1)
                ve.tensor_copy(adacol[:, bass.ds(m * 4, 4)], psum[:, bank, 0:4]).then_inc(ada_saved, 1)

            def mods(key, gain, upto, n=24):
                c = LCOL[key]
                v.wait_ge(ada_saved, upto)
                v.wait_ge(vec_saved, 2)
                ve.tensor_tensor(adacol[:, c:c + n], adacol[:, c:c + n], bcol[:, c:c + n], ALU.add).then_inc(aff_ready, 1)
                v.wait_ge(aff_ready, ("order", 0, 1, 2, "kv", 3).index(key))
                affine_cols(c, gain)

            def affine_cols(c, gain):
                chain(ve.tensor_copy(sh[:], adacol[:, c:c + 8]))
                chain(ve.scalar_tensor_tensor(gs[:], adacol[:, c + 8:c + 16], 1.0, vcol[:, gain:gain + 8], ALU.add, ALU.mult))

            def norm(k, j, shift=True):
                for i in range(TT):
                    v.wait_ge(n_rstd, 2 * j + i + 1)
                    ve.tensor_scalar(y[:, i, :], res[:, i, :], rstd[:, i:i + 1], None, ALU.mult).then_inc(n_y, 1)
                for b in range(4):
                    affine(k, j, b, shift)
                    if b:
                        low(k, b - 1)
                low(k, 3)

            def affine(k, j, b, shift=True):
                v.wait_ge(n_turned, 4 * j + b + 1)
                for q in range(2):
                    kt = 2 * b + q
                    src = psum[:, 4 + b, q * T:(q + 1) * T]
                    if shift:
                        ins = ve.tensor_scalar(xf[:, kt, :], src, gs[:, kt:kt + 1], sh[:, kt:kt + 1], ALU.mult, ALU.add)
                    else:
                        ins = ve.tensor_scalar(xf[:, kt, :], src, gs[:, kt:kt + 1], None, ALU.mult)
                ins.then_inc(n_affine, 1)

            def low(k, b):
                v.wait_ge(n_hi, 4 * k + b + 1)
                ve.tensor_tensor(xlo[:, 2 * b:2 * b + 2, :], xf[:, 2 * b:2 * b + 2, :],
                                 xhi[:, 2 * b:2 * b + 2, :].bitcast(F32), ALU.subtract).then_inc(n_x, 1)

            def turn(k):
                for b in range(4):
                    v.wait_ge(t_hi, 4 * k + b + 1)
                    ve.tensor_tensor(xlo[:, 2 * b:2 * b + 2, :], psum[:, 4 + b, :].rearrange("p (k t) -> p k t", k=2),
                                     xhi[:, 2 * b:2 * b + 2, :].bitcast(F32), ALU.subtract).then_inc(t_x, 1)

            def evac(n, p, dst):
                v.wait_ge(used[2 * p + 1], n + 1)
                ve.tensor_copy(dst, psum[:, 2 * p + 1, 0:dst.shape[-1]]).then_inc(evac_d, 1)

            def residual(k):
                if k < 2:
                    v.wait_ge(gain_in, 16 * k + 16)
                for i in range(TT):
                    if i == 0:
                        v.wait_ge(acc_done, k + 1)
                    else:
                        v.wait_ge(used[3], ACC_END[k] + 1)
                    if k < 2:
                        v.wait_ge(p_rstd, 2 * k + i + 1)
                    acc = psum[:, 2 * i:2 * i + 2, :].rearrange("p b n -> p (b n)")
                    if k < 2:
                        chain(ve.scalar_tensor_tensor(y[:, i, :], acc, stat[:, 38 + i:39 + i], gain_b[:], ALU.mult, ALU.mult))
                    else:
                        chain(ve.tensor_tensor(y[:, i, :], acc, gain_b[:], ALU.mult))
                    ve.tensor_tensor(res[:, i, :], res[:, i, :], y[:, i, :], ALU.add).then_inc(p_res, 1)

            def gate_save(k, bank=4):
                v.wait_ge(bg_turned, k + 1)
                ve.tensor_copy(gain_b[:, :], psum[:, bank:bank + 2, :].rearrange("p b n -> p (b n)")).then_inc(bg_saved, 1)

            v.wait_ge(vec_saved, 1)
            chain(ve.tensor_copy(gs[:], vcol[:, 0:8]))
            norm(0, 0, shift=False)
            for s in range(4):
                split(s, Q_QKV)
            v.wait_ge(c_ready, 1)

            def qkv_step(t):
                for p in range(2):
                    split(2 * p, t + 1)
                    if p == 0:
                        ada(t, 0)
                    evac(t + Q_QKV, p, qkv[:, 1, bass.ds(t * 1024 + p * 512, 512)])
                    split(2 * p + 1, t + 1)
                    if p == 0:
                        ada(t, 1)
                ada_save(t)
            qkv_step(0)
            with v.Fori(1, N_QKV) as t:
                qkv_step(t)

            for h in range(H1 + 3):
                if 1 <= h <= H1:
                    g = h - 1
                    m = st1[:, g % 2, :]
                    v.wait_ge(a_s, g + 1)
                    if g >= 2:
                        v.wait_ge(a_e, g - 1)
                    ve.tensor_reduce(m[:, 0:1], psum[:, 2 + g % 2, 0:P], AX, ALU.max, negate=True)
                    ve.tensor_reduce(m[:, 1:2], psum[:, 2 + g % 2, P:384], AX, ALU.max, negate=True).then_inc(a_m, 1)
                if 2 <= h <= H1 + 1:
                    g = h - 2
                    m = st1[:, g % 2, :]
                    v.wait_ge(a_e, g + 1)
                    wait(v, a_os, g - 1)
                    ve.reciprocal(m[:, 4:6], m[:, 2:4])
                    v.wait_ge(a_pt, g + 1)
                    if g >= 2:
                        v.wait_ge(a_o, g - 1)
                    ve.tensor_copy(pT1[:, g % 2, :], psum[:, 4 + g % 2, 0:384]).then_inc(a_pts, 1)
                if 3 <= h:
                    g = h - 3
                    m = st1[:, g % 2, :]
                    v.wait_ge(a_o, g + 1)
                    v.wait_ge(a_pts, g + 1)
                    for i in range(TT):
                        ins = ve.tensor_scalar(ob1[:, i, g * DH1:(g + 1) * DH1], psum[:, 6 + g % 2, i * P:(i + 1) * P],
                                               m[:, 4 + i:5 + i], None, ALU.mult)
                    ins.then_inc(a_os, 1)
            turn(0)
            ada(A_WO, 0)
            ada(A_WO, 1)
            split(0, Q_FF1)
            split(1, Q_FF1)
            ada_save(A_WO)
            residual(0)
            chain(ve.tensor_copy(gs[:], vcol[:, 8:16]))
            norm(1, 1, shift=False)
            split(2, Q_FF1)
            split(3, Q_FF1)

            def mlp1(t, first=False):
                split(0, t + (Q_FF1 + 1))
                if not first:
                    ada(t + (A_FF1 - 1), 0)
                    ada(t + (A_FF1 - 1), 1)
                split(1, t + (Q_FF1 + 1))
                if not first:
                    ada_save(t + (A_FF1 - 1))
                    split(2, t + Q_FF1)
                for b in range(2):
                    v.wait_ge(h_hi, 2 * t + b + 1)
                    ve.tensor_tensor(hlo[:, 2 * b:2 * b + 2, :], sq[:, 2 * b:2 * b + 2, :],
                                     hhi[:, 2 * b:2 * b + 2, :].bitcast(F32), ALU.subtract).then_inc(h_lo, 1)
                if not first:
                    split(3, t + Q_FF1)
            mlp1(0, True)
            with v.Fori(1, N_FF1) as t:
                mlp1(t)
            split(2, Q_HIN)
            mods(0, VR["mix2"], 6)
            residual(1)
            norm(2, 2)
            split(3, Q_HIN)
            tmp = area(12416, TT, D)
            for t, sec in enumerate(HIN_ORDER):
                for p in range(2):
                    split(2 * p, Q_HIN + t + 1)
                    if p == 0:
                        ada(A_HIN + t, 0)
                    evac(Q_HIN + t, p, hin[:, sec, 1, p * 512:(p + 1) * 512])
                    split(2 * p + 1, Q_HIN + t + 1)
                    if p == 0:
                        ada(A_HIN + t, 1)
                ada_save(A_HIN + t)
                if t == 1:
                    v.wait_ge(g_f, 1)
                    ve.scalar_tensor_tensor(hin[:, 1, :, :].rearrange("p i n -> p (i n)"), hin[:, 1, :, :].rearrange("p i n -> p (i n)"),
                                            0.0, tmp.rearrange("p i n -> p (i n)"), ALU.min, ALU.subtract).then_inc(g_d, 1)
            for b in range(4):
                v.wait_ge(g_hi, b + 1)
                ve.tensor_tensor(glo[:, :, b * 256:(b + 1) * 256], hin[:, 1, :, b * 256:(b + 1) * 256],
                                 ghi[:, :, b * 256:(b + 1) * 256].bitcast(F32), ALU.subtract).then_inc(g_lo, 1)

            def q_part(n):
                h, i = n // 2, n % 2
                if i == 0:
                    v.wait_ge(r_qks, h + 1)
                v.wait_ge(r_ee, n + 1)
                if n >= 2:
                    v.wait_ge(r_s, n - 1)
                w = NL + i
                ve.tensor_tensor(qe[i][:, 0:w, :], ee[i][:, 0:w, :], qkTh[h % 2][:, 0, i * P:(i + 1) * P].unsqueeze(1)
                                 .to_broadcast([P, w, P]), ALU.mult).then_inc(r_z, 1)

            v.wait_ge(ada_used[0], A_HOUT)
            v.wait_ge(ada_used[1], A_HOUT)
            hg = hin[:, 3, :, :].rearrange("p i (h d) -> p (i h) d", d=DK)
            q_part(0)
            for n in range(2 * HH):
                h, i = n // 2, n % 2
                if n + 1 < 2 * HH:
                    q_part(n + 1)
                v.wait_ge(r_s, n + 1)
                wait(v, r_am, n)
                ve.tensor_tensor(pm, psum[:, 5:7, :].rearrange("p b (l t) -> p (b l) t", t=P), MK, ALU.mult).then_inc(r_m, 1)
                v.wait_ge(r_m, n + 1)
                wait(v, r_o, h - 1)
                ins = ve.tensor_reduce(am[h % 2][:, i, :], pm.rearrange("p l t -> p t l"), AX, ALU.add)
                if i == 1:
                    ins = ve.tensor_copy(am[h % 2][:, 2, :], psum[:, 7, 0:P])
                ins.then_inc(r_am, 1)
            v.wait_ge(g_f, 3)
            v.wait_ge(onb_in, 16)
            chain(ve.tensor_tensor(hg, hg, onb[:].unsqueeze(1).to_broadcast([P, 2 * HH, DK]), ALU.mult))
            v.wait_ge(r_os, HH)
            gate_save(0, 1)
            v.wait_ge(r_rs, 1)
            for h in range(HH):
                for i in range(TT):
                    o = hin[:, 0, i, h * DK:(h + 1) * DK]
                    ins = ve.scalar_tensor_tensor(o, o, hs[:, 16 + 8 * i + h:17 + 8 * i + h], hin[:, 3, i, h * DK:(h + 1) * DK],
                                                  ALU.mult, ALU.mult)
                if h % 2:
                    ins.then_inc(r_n, 1)
            turn(1)
            mods(1, VR["ffn2"], 12)
            ada(A_HOUT, 0)
            ada(A_HOUT, 1)
            split(0, Q_F2A)
            split(1, Q_F2A)
            ada_save(A_HOUT)
            residual(2)
            gate_save(1)
            norm(3, 3)
            split(2, Q_F2A, 1024)
            split(3, Q_F2A, 1024)

            def mlp2(t, q0, hb, gb, m=None, first=False, nxt=2048, last=False):
                if not last:
                    split(0, t + (q0 + 1), nxt)
                if m is not None:
                    ada(m, 0)
                for i in range(TT):
                    v.wait_ge(act_done, 2 * t + (gb + 16 + i + 1))
                    ve.tensor_tensor(gat[:, i, :], sil[:, i, :], psum[:, 4 + i, 256:512], ALU.mult).then_inc(gate_done, 1)
                if m is not None:
                    ada(m, 1)
                if not last:
                    split(1, t + (q0 + 1), nxt)
                if not first:
                    split(2, t + q0, 1024)
                if m is not None:
                    ada_save(m)
                v.wait_ge(h_hi, t + (hb + 1))
                ve.tensor_tensor(hlo[:, 0:2, :], psum[:, 6, :].rearrange("p (k t) -> p k t", k=2),
                                 hhi[:, 0:2, :].bitcast(F32), ALU.subtract).then_inc(h_lo, 1)
                if not first:
                    split(3, t + q0, 1024)
            mlp2(0, Q_F2A, HT_F2A, 0, first=True)
            with v.Fori(1, N_FF2 - 1) as t:
                mlp2(t, Q_F2A, HT_F2A, 0, t + (A_F2A - 1))
            mlp2(N_FF2 - 1, Q_F2A, HT_F2A, 0, A_KV - 1, nxt=1536)
            split(2, Q_KV, 1536)
            mods(2, VR["mix2"] + 8, M_L3)
            mods("kv", VR["kvn"], M_L3, 16)
            residual(3)
            norm(4, 4)
            affine_cols(LCOL[2], VR["mix2"] + 8)
            for b in range(4):
                affine(5, 4, b)
            split(3, Q_KV, 1536)
            kvf = area(0, TT, 1536)
            for t in range(N_KV):
                for p in range(2):
                    for s in (2 * p, 2 * p + 1):
                        if t == 0:
                            split(s, Q_KV + 1, 1536)
                        elif p == 0:
                            split(s, Q_NQ)
                        if p == 0:
                            ada(A_KV + t, s)
                    evac(Q_KV + t, p, kvf[:, 1, (2 * t + p) * 384:(2 * t + p + 1) * 384])
                ada_save(A_KV + t)
            for b in range(4):
                low(5, b)
            for s in (2, 3):
                split(s, Q_NQ)
            v.wait_ge(k_["evens"], 1)
            for j in range(2):
                for c in range(NCMP):
                    pos = vcol[:, VR["pos"] + 16 * j:VR["pos"] + 16 * j + 16].unsqueeze(2).to_broadcast([P, 16, NKV])
                    ins = ve.tensor_tensor(fl[:, j, :, c, :], kt2[:, j, :, 8 * c:8 * c + 16].rearrange("p h a -> p a h"), pos, ALU.add)
            ins.then_inc(k_["flat"], 1)
            v.wait_ge(k_["flat"], 1)
            v.wait_ge(k_["wgh"], 1)
            ve.tensor_tensor(wgl, wgs.rearrange("p k n -> p (k n)"), wgh.bitcast(F32), ALU.subtract).then_inc(k_["wgl"], 1)
            v.wait_ge(evac_a, G_Q)
            v.wait_ge(evac_d, G_Q)
            k2 = nt1[:, 0:1024].rearrange("p (i b h d) -> p i b h d", i=2, b=2, h=4)
            for i in range(TT):
                for b in range(2):
                    ins = ve.tensor_tensor(k2[:, i, b], kv[:, i, 2 + 2 * b], kv[:, i, 2 + 2 * b], ALU.mult)
            chain(ins)
            ve.tensor_reduce(nst[:, 16:32], nt1[:, 0:1024].rearrange("p (g d) -> p g d", d=DN), AX, ALU.add).then_inc(k_["sq"], 1)
            v.wait_ge(k_["rs"], 1)
            v.wait_ge(knb_in, 32)
            rope = cst("rope").rearrange("p (i j d) -> p i j d", i=2, j=2)
            HD = DN // 2

            def turn_half(dst1, dst2, x1, x2, cos, sin, tmp1):
                ve.tensor_tensor(dst1, x1, cos, ALU.mult)
                chain(ve.tensor_tensor(tmp1, x2, sin, ALU.mult))
                ve.tensor_tensor(dst2, x2, cos, ALU.mult)
                chain(ve.tensor_tensor(dst1, dst1, tmp1, ALU.subtract))
                chain(ve.tensor_tensor(tmp1, x1, sin, ALU.mult))
                chain(ve.tensor_tensor(dst2, dst2, tmp1, ALU.add))

            for i in range(TT):
                for b in range(2):
                    r = nst[:, 32 + 8 * i + 4 * b:36 + 8 * i + 4 * b].unsqueeze(2).to_broadcast([P, NKV, DN])
                    x = kv[:, i, 2 + 2 * b, :, :]
                    chain(ve.tensor_tensor(x, x, r, ALU.mult))
                    chain(ve.tensor_tensor(x, x, knb[:, 1 + b, :].unsqueeze(1).to_broadcast([P, NKV, DN]), ALU.mult))
                    cos = rope[:, i, 0, :].unsqueeze(1).to_broadcast([P, NKV, HD])
                    sin = rope[:, i, 1, :].unsqueeze(1).to_broadcast([P, NKV, HD])
                    d = nkd[:, i, b, :, 0, :]
                    turn_half(d[:, :, 0:HD], d[:, :, HD:DN], x[:, :, 0:HD], x[:, :, HD:DN], cos, sin,
                              nt1[:, 1024:1024 + NKV * HD].rearrange("p (h d) -> p h d", h=NKV))
                    ins = ve.tensor_copy(nkd[:, i, b, :, 1, :], d)
            ins.then_inc(k_["krope"], 1)
            nqf = area(3072, TT, D)
            for p in range(2):
                evac(Q_NQ, p, nqf[:, 1, p * 512:(p + 1) * 512])
            gate_save(2, 5)
            chain(ve.tensor_scalar(knb[:, 3, :], knb[:, 3, :], DN ** -0.5, None, ALU.mult))
            v.wait_ge(k_["qsq"], 1)
            ve.tensor_reduce(nst[:, 64:96], nt1.rearrange("p (g d) -> p g d", d=DN), AX, ALU.add).then_inc(k_["sq"], 1)
            v.wait_ge(k_["rs"], 2)
            qg = nq.rearrange("p i h d -> p (i h) d")
            chain(ve.tensor_tensor(qg, qg, nst[:, 96:128].unsqueeze(2).to_broadcast([P, 2 * NH, DN]), ALU.mult))
            ve.tensor_tensor(qg, qg, knb[:, 3, :].unsqueeze(1).to_broadcast([P, 2 * NH, DN]), ALU.mult).then_inc(k_["qn"], 1)
            v.wait_ge(k_["qn"], 1)
            v.wait_ge(k_["kT"], 1)

            def rope_q(i):
                cos = rope[:, i, 0, :].unsqueeze(1).to_broadcast([P, NH, HD])
                sin = rope[:, i, 1, :].unsqueeze(1).to_broadcast([P, NH, HD])
                turn_half(nqr[:, i, :, 0:HD], nqr[:, i, :, HD:DN], nq[:, i, :, 0:HD], nq[:, i, :, HD:DN], cos, sin,
                          nt1[:, 512 * i:512 * i + 512].rearrange("p (h d) -> p h d", h=NH))
            rope_q(0)
            v.wait_ge(k_["kc"], 1)
            ve.tensor_copy(kcv[0:60, :, :], psum[0:60, 7, 0:128].rearrange("p (j d) -> p j d", j=2)).then_inc(k_["kcs"], 1)
            v.wait_ge(k_["kcs"], 1)
            chain(ve.tensor_tensor(kcd[0:60, 0, :], kcv[0:60, 0, :], kcv[0:60, 0, :], ALU.mult))
            ve.tensor_reduce(nst[0:60, 0:1], kcd[0:60, 0, :], AX, ALU.add).then_inc(k_["sq"], 1)
            v.wait_ge(k_["vb"], 1)
            for j in range(2):
                ins = ve.tensor_tensor(vbd[:, j, :, :], psum[:, 5 + j, 0:DN].unsqueeze(1).to_broadcast([P, 8, DN]),
                                       cst("bm").unsqueeze(2).to_broadcast([P, 8, DN]), ALU.mult)
            ins.then_inc(k_["vbs"], 1)
            v.wait_ge(k_["rs"], 3)
            for j in range(2):
                ins = ve.scalar_tensor_tensor(kcd[0:60, j, :], kcv[0:60, 0, :], nst[0:60, 1:2], knb[0:60, 0, :], ALU.mult, ALU.mult)
            ins.then_inc(k_["kcd"], 1)
            chain(ve.memset(kcB, 0.0))
            v.wait_ge(k_["kct"], 1)
            for r in range(2):
                ins = ve.tensor_copy(kcB[64 * r:64 * r + 64, :, r, 0:NCMP],
                                     psum[64 * r:64 * r + 64, 7, 256:316].rearrange("p (c h) -> p h c", h=NKV))
            ins.then_inc(k_["kcts"], 1)
            rope_q(1)
            v.nop().then_inc(k_["qr"], 1)
            cm = cst("cmask").rearrange("p (j i c) -> p j i c", j=2, i=2)
            v.wait_ge(k_["cs"], 1)
            chain(ve.memset(pc, 0.0))
            ng = nst[:, 128:160].rearrange("p (i h) -> p i h", i=2)
            for i in range(TT):
                x = pc[:, i, :, 0:NCMP]
                chain(ve.tensor_tensor(x, psum[:, i, 0:256].rearrange("p (h c) -> p h c", c=16)[:, :, 0:NCMP],
                                       cm[:, 0, i, :].unsqueeze(1).to_broadcast([P, NH, NCMP]), ALU.add))
                chain(ve.tensor_reduce(ng[:, i, :], x, AX, ALU.max))
                ins = ve.tensor_tensor(x, x, ng[:, i, :].unsqueeze(2).to_broadcast([P, NH, NCMP]), ALU.subtract)
            ins.then_inc(k_["cm"], 1)
            v.wait_ge(k_["ce"], 1)
            for i in range(TT):
                x = pc[:, i, :, 0:NCMP]
                chain(ve.tensor_tensor(x, x, cm[:, 1, i, :].unsqueeze(1).to_broadcast([P, NH, NCMP]), ALU.mult))
                chain(ve.tensor_reduce(ng[:, i, :], x, AX, ALU.add))
            chain(ve.tensor_scalar(ng, ng, 1e-30, None, ALU.max))
            chain(ve.reciprocal(ng, ng))
            v.wait_ge(k_["gs"], 1)
            chain(ve.tensor_tensor(ng, ng, gat3[:, :, 0:NH], ALU.mult))
            for i in range(TT):
                x = pc[:, i, :, 0:NCMP]
                ins = ve.tensor_tensor(x, x, ng[:, i, :].unsqueeze(2).to_broadcast([P, NH, NCMP]), ALU.mult)
            ins.then_inc(k_["cp"], 1)
            for s in (0, 1):
                v.nop().then_inc(lo_ready[s], 1)
                split(s, Q_NOUT)
            for w in range(2 * NH + 2):
                if w < 2 * NH:
                    u = w
                    m = nst[:, 8 * (u % 2):8 * (u % 2) + 8]
                    v.wait_ge(w_s, u + 1)
                    if u >= 2:
                        v.wait_ge(w_e, u - 1)
                    ve.tensor_reduce(m[:, 0:1], psum[:, u % 2, 0:P], AX, ALU.max, negate=True)
                    ve.tensor_reduce(m[:, 1:2], psum[:, u % 2, P:384], AX, ALU.max, negate=True).then_inc(w_m, 1)
                if 1 <= w <= 2 * NH:
                    u = w - 1
                    hq, b = u // 2, u % 2
                    m = nst[:, 8 * (u % 2):8 * (u % 2) + 8]
                    v.wait_ge(w_e, u + 1)
                    wait(v, w_os, u - 1)
                    chain(ve.reciprocal(m[:, 4:6], m[:, 2:4]))
                    ve.tensor_tensor(m[:, 4:6], m[:, 4:6], gat3[:, :, (1 + b) * NH + hq], ALU.mult)
                    v.wait_ge(w_pt, u + 1)
                    if u >= 2:
                        v.wait_ge(w_o, u - 1)
                    ve.tensor_copy(pT2[:, u % 2, :], psum[:, 2 + u % 2, 0:384]).then_inc(w_pts, 1)
                if 2 <= w:
                    u = w - 2
                    hq = u // 2
                    m = nst[:, 8 * (u % 2):8 * (u % 2) + 8]
                    v.wait_ge(w_o, u + 1)
                    v.wait_ge(w_pts, u + 1)
                    if u == 0:
                        v.wait_ge(k_["cos"], 2)
                    if u:
                        v.wait_ge(w_os, u)
                    for i in range(TT):
                        ins = ve.scalar_tensor_tensor(ob2[:, i, hq, :], psum[:, 4 + u % 2, i * DN:(i + 1) * DN],
                                                      m[:, 4 + i:5 + i], ob2[:, i, hq, :], ALU.mult, ALU.add)
                    ins.then_inc(w_os, 1)
            turn(2)
            for s in (2, 3):
                v.nop().then_inc(lo_ready[s], 1)
                split(s, Q_NOUT)
            mods(3, VR["ffn2"] + 8, M_END)
            split(0, Q_F2B)
            split(1, Q_F2B)
            residual(4)
            gate_save(3)
            norm(6, 5)
            split(2, Q_F2B, 1024)
            split(3, Q_F2B, 1024)
            mlp2(0, Q_F2B, HT_F2B, 2 * N_FF2, first=True)
            with v.Fori(1, N_FF2 - 1) as t:
                mlp2(t, Q_F2B, HT_F2B, 2 * N_FF2)
            mlp2(N_FF2 - 1, Q_F2B, HT_F2B, 2 * N_FF2, last=True)
            residual(5)

        @block.tensor
        def _(pe):
            te = nc.tensor

            def mm(dst, lhsT, rhs, start=True, stop=True, open_=False):
                return te.matmul(dst, lhsT, rhs, start=start, stop=stop, skip_group_check=open_)

            def three(dst, lhi, llo, s, c0, n, start, stop, open_=False):
                wh, wl = whi[:, s, c0:c0 + n], wlo[:, s, c0:c0 + n]
                mm(dst, lhi, wh, start, False, open_)
                mm(dst, lhi, wl, False, False, open_)
                return mm(dst, llo, wh, False, stop, open_)

            def norm(j, ada_upto=0, gates=0):
                wait(pe, ada_saved, ada_upto)
                wait(pe, bg_saved, gates)
                for i in range(TT):
                    pe.wait_ge(n_y, 2 * j + i + 1)
                    for kt in range(KD):
                        b, q = kt // 2, kt % 2
                        ins = te.transpose(psum[:, 4 + b, q * T + i * P:q * T + (i + 1) * P], y[:, i, kt * P:(kt + 1) * P], ident)
                        if i == TT - 1 and q == 1:
                            ins.then_inc(n_turned, 1)

            def turn(k, x, ready=None):
                for b in range(4):
                    if ready is not None:
                        pe.wait_ge(ready, b + 1)
                    for q in range(2):
                        for i in range(TT):
                            kt = 2 * b + q
                            ins = te.transpose(psum[:, 4 + b, q * T + i * P:q * T + (i + 1) * P], x[:, i, kt * P:(kt + 1) * P], ident)
                    ins.then_inc(t_turned, 1)

            def item_ready(s, n):
                pe.wait_ge(lo_ready[s], n + 1)

            def project(n, g, width=512, fresh=None):
                for p in range(2):
                    if not isinstance(g, int) or g >= 2:
                        pe.wait_ge(evac_a, g + p - 1)
                        pe.wait_ge(evac_d, g + p - 1)
                    for half in range(2):
                        s = 2 * p + half
                        item_ready(s, n)
                        if fresh is not None and p == 0:
                            pe.wait_ge(n_x, 4 * fresh + 2 * half + 2)
                        for i in range(TT):
                            for k in range(4):
                                kt = 4 * half + k
                                ins = three(psum[:, 2 * p + i, 0:width], xhi[:, kt, i * P:(i + 1) * P], xlo[:, kt, i * P:(i + 1) * P],
                                            s, k * width, width, kt == 0, kt == KD - 1)
                        ins.then_inc(used[s], 1)

            def accumulate(n, turned, m=None):
                for s in range(4):
                    item_ready(s, n)
                    pe.wait_ge(t_x, 4 * turned + s + 1)
                    for i in range(TT):
                        for f in range(2):
                            for k in range(2):
                                kt = 2 * s + k
                                ins = three(psum[:, 2 * i + f, :], xhi[:, kt, i * P:(i + 1) * P], xlo[:, kt, i * P:(i + 1) * P],
                                            s, k * D + f * 512, 512, kt == 0, kt == KD - 1)
                        if s == 3 and i == 0:
                            ins.then_inc(acc_done, 1)
                    ins.then_inc(used[s], 1)
                    if s == 2 and m is not None:
                        ada(m)

            def ada(m, bank=7):
                pe.wait_ge(ada_used[1], m + 1)
                for c in range(4):
                    ins = mm(psum[:, bank, c:c + 1], adaacc[:, c * P:(c + 1) * P], ones[:])
                ins.then_inc(ada_turned, 1)

            def gate(key, k, bank=4):
                pe.wait_ge(aff_ready, ("order", 0, 1, 2, "kv", 3).index(key))
                for kt in range(KD):
                    c = LCOL[key] + 16 + kt
                    ins = mm(psum[:, bank + kt // 4, (kt % 4) * P:(kt % 4 + 1) * P], adacol[:, c:c + 1].to_broadcast([P, P]), ident)
                ins.then_inc(bg_turned, 1)

            def open_acc():
                for b in range(4):
                    mm(psum[:, b, :], zrow[0:1, 0:P], zrow[0:1, :], True, False, True)

            pe.wait_ge(consts_in, 16)
            pe.wait_ge(vec_in, 16 * 10)
            te.transpose(psum[:, 0, 0:96], vrow1[0:96, :], ident[0:96, 0:96])
            te.transpose(psum[:, 0, 128:240], vrow2[0:112, :], ident[0:112, 0:112]).then_inc(vec_turned, 1)
            pe.wait_ge(ones_set, 1)
            norm(0)
            pe.wait_ge(vec_saved, 2)
            project(Q_QKV, 0, fresh=0)
            ada(A_QKV)
            with pe.Fori(1, N_QKV) as t:
                project(t + Q_QKV, 2 * t)
                pe.wait_ge(ada_saved, t + A_QKV)
                ada(t + A_QKV)

            pe.wait_ge(bias_ready, 1)
            pe.wait_ge(evac_a, G_HIN)
            pe.wait_ge(evac_d, G_HIN)
            for h in range(H1 + 3):
                if h < H1:
                    if h >= 2:
                        pe.wait_ge(a_qks, h - 1)
                    for j in range(2):
                        for i in range(TT):
                            ins = te.transpose(psum[:, h % 2, j * T + i * P:j * T + (i + 1) * P],
                                               qkv[:, i, j * D + h * DH1:j * D + (h + 1) * DH1], ident)
                    ins.then_inc(a_qk, 1)
                if 1 <= h <= H1:
                    g = h - 1
                    pe.wait_ge(a_qks, g + 1)
                    if g >= 2:
                        pe.wait_ge(a_e, g - 1)
                    x = qkT[:, g % 2, :]
                    mm(psum[:, 2 + g % 2, 0:384], slopeb[:, g, :], distb, True, False, True)
                    mm(psum[:, 2 + g % 2, 0:P], x[:, 0:P], x[:, T:T + P], False, False, True)
                    mm(psum[:, 2 + g % 2, P:384], x[:, P:T], x[:, T:2 * T], False, True, True).then_inc(a_s, 1)
                if 2 <= h <= H1 + 1:
                    g = h - 2
                    pe.wait_ge(a_e, g + 1)
                    if g >= 2:
                        pe.wait_ge(a_pts, g - 1)
                    for b in range(3):
                        ins = te.transpose(psum[:, 4 + g % 2, b * P:(b + 1) * P], pb1[:, g % 2, b * P:(b + 1) * P], ident)
                    ins.then_inc(a_pt, 1)
                if 3 <= h:
                    g = h - 3
                    pe.wait_ge(a_pts, g + 1)
                    if g >= 2:
                        pe.wait_ge(a_os, g - 1)
                    o = psum[:, 6 + g % 2, :]
                    vv = qkv[:, :, 2 * D + g * DH1:2 * D + (g + 1) * DH1]
                    mm(o[:, 0:P], pT1[:, g % 2, 0:P], vv[:, 0, :])
                    mm(o[:, P:T], pT1[:, g % 2, P:T], vv[:, 0, :], True, False)
                    mm(o[:, P:T], pT1[:, g % 2, T:384], vv[:, 1, :], False, True).then_inc(a_o, 1)
            pe.wait_ge(a_os, H1)
            turn(0, ob1)
            accumulate(Q_WO, 0, A_WO)
            norm(1)

            def up(n, fresh=None):
                for s in range(2):
                    item_ready(s, n)
                    if fresh is not None:
                        pe.wait_ge(n_x, 4 * fresh + 2 * s + 2)
                    for i in range(TT):
                        for k in range(4):
                            kt = 4 * s + k
                            ins = three(psum[:, 4 + i, :], xhi[:, kt, i * P:(i + 1) * P], xlo[:, kt, i * P:(i + 1) * P],
                                        s, k * 512, 512, kt == 0, kt == KD - 1)
                    ins.then_inc(used[s], 1)

            def down(n, kts, last=False, slots=(2, 3)):
                for s in slots:
                    item_ready(s, n)
                    for i in range(TT):
                        for f in range(2):
                            for k in range(kts):
                                kt = kts * (s - 2) + k
                                ins = three(psum[:, 2 * i + f, :], hhi[:, kt, i * P:(i + 1) * P], hlo[:, kt, i * P:(i + 1) * P],
                                            s, k * D + f * 512, 512, False, last and kt == 2 * kts - 1, True)
                        if last and s == 3 and i == 0:
                            ins.then_inc(acc_done, 1)
                    ins.then_inc(used[s], 1)

            def hidden1(t):
                pe.wait_ge(act_done, 2 * t + 2)
                for b in range(2):
                    if b == 1:
                        pe.wait_ge(ada_saved, t + A_FF1)
                    for q in range(2):
                        for i in range(TT):
                            kt = 2 * b + q
                            ins = te.transpose(psum[:, 6 + b, q * T + i * P:q * T + (i + 1) * P], relu[:, i, kt * P:(kt + 1) * P], ident)
                    ins.then_inc(h_turned, 1)
            open_acc()
            up(Q_FF1, fresh=1)
            hidden1(0)
            with pe.Fori(1, N_FF1) as t:
                up(t + Q_FF1)
                pe.wait_ge(h_lo, 2 * t)
                down(t + (Q_FF1 - 1), 2, slots=(2,))
                ada(t + (A_FF1 - 1))
                down(t + (Q_FF1 - 1), 2, slots=(3,))
                hidden1(t)
            pe.wait_ge(h_lo, 2 * N_FF1)
            down(Q_FF1 + N_FF1 - 1, 2, last=True)
            norm(2, ada_upto=A_HIN)
            for t in range(N_HIN):
                project(Q_HIN + t, G_HIN + 2 * t, fresh=None if t else 2)
                wait(pe, ada_saved, A_HIN + t)
                ada(A_HIN + t)

            pe.wait_ge(ada_saved, A_HOUT)
            pe.wait_ge(evac_a, G_KV)
            pe.wait_ge(evac_d, G_KV)
            pe.wait_ge(g_f, 2)
            for b in (5, 6):
                ins = mm(psum[:, b, :], zrow[0:1, 0:P], zrow[0:1, :])
            ins.then_inc(s_zero, 1)
            pe.wait_ge(s_zero, 1)

            def heads_qk(h):
                if h:
                    pe.wait_ge(r_qks, h)
                for j, src in enumerate((hin[:, 0], hk)):
                    for i in range(TT):
                        ins = te.transpose(psum[:, 0, j * T + i * P:j * T + (i + 1) * P], src[:, i, h * DK:(h + 1) * DK], ident)
                ins.then_inc(r_qk, 1)

            def exponents(n):
                h, i = n // 2, n % 2
                if i == 0:
                    pe.wait_ge(g_lo, h // 2 + 1)
                if n >= 2:
                    pe.wait_ge(r_ee, n - 1)
                parts = [(0, MLr[:, 0:512]), (512, MLr[:, 512:1024])] if i == 0 else [(0, MLr[:, 0:512]), (512, MLr[:, 512:896]), (896, MLx)]
                e = psum[:, 1 + 2 * i:3 + 2 * i, :].rearrange("p b n -> p (b n)")
                for c0, m in parts:
                    for x in (ghi, glo):
                        ins = mm(e[:, c0:c0 + m.shape[-1]], x[:, i, h * DK:(h + 1) * DK], m, x is ghi, x is glo)
                ins.then_inc(r_e, 1)

            def second(x, m):
                return x.rearrange("p (j s r) -> p j s r", s=2, r=m)[:, :, 1, :]

            def scores(n):
                h, i = n // 2, n % 2
                pe.wait_ge(r_z, n + 1)
                pe.wait_ge(r_k, n + 1)
                wait(pe, r_m, n)
                for l, m in enumerate(LEVELS):
                    mm(second(psum[:, 5 + l // 4, (l % 4) * P:(l % 4 + 1) * P], m), ke[i][:, l, :], second(qe[i][:, l, :], m))
                if i == 1:
                    wait(pe, r_os, h)
                    pe.wait_ge(r_k7, h + 1)
                    mm(psum[:, 7, 0:P], ke7[h % 2], qe[1][:, NL, :])
                mm(psum[:, 6, 384:512], qkTh[h % 2][:, 1, i * P:(i + 1) * P], qkTh[h % 2][:, 0, i * P:(i + 1) * P]).then_inc(r_s, 1)

            def outputs(h):
                pe.wait_ge(r_am, 2 * h + 2)
                x, c = am[h % 2], slice(h * DK, (h + 1) * DK)
                mm(psum[:, 7, P:2 * P], x[:, 0, :], hin[:, 2, 0, c])
                mm(psum[:, 7, 2 * P:3 * P], x[:, 1, :], hin[:, 2, 1, c], True, False)
                mm(psum[:, 7, 2 * P:3 * P], x[:, 2, :], hin[:, 2, 0, c], False, True).then_inc(r_o, 1)

            heads_qk(0)
            pe.wait_ge(ml_ready, 1)
            exponents(0)
            exponents(1)
            for n in range(2 * HH):
                if n % 2 == 0 and n // 2 + 1 < HH:
                    heads_qk(n // 2 + 1)
                if n + 2 < 2 * HH:
                    exponents(n + 2)
                scores(n)
                if n % 2 == 0 and n:
                    outputs(n // 2 - 1)
            pe.wait_ge(r_ee, 2 * HH)
            gate(0, 0, 1)
            outputs(HH - 1)
            turn(1, hin[:, 0, :, :], r_n)
            pe.wait_ge(bg_saved, 1)
            accumulate(Q_HOUT, 1, A_HOUT)
            gate(1, 1)
            norm(3, gates=2)

            def mlp2_hidden(t, gb):
                pe.wait_ge(gate_done, 2 * t + (gb + 2))
                for q in range(2):
                    for i in range(TT):
                        ins = te.transpose(psum[:, 6, q * T + i * P:q * T + (i + 1) * P], gat[:, i, q * P:(q + 1) * P], ident)
                ins.then_inc(h_turned, 1)

            def mlp2(q0, hb, gb, fresh, m0=None):
                open_acc()
                up(q0, fresh)
                mlp2_hidden(0, gb)
                with pe.Fori(1, N_FF2) as t:
                    up(t + q0)
                    pe.wait_ge(h_lo, t + hb)
                    down(t + (q0 - 1), 1)
                    if m0 is not None:
                        pe.wait_ge(ada_saved, t + m0)
                        ada(t + m0)
                    mlp2_hidden(t, gb)
                pe.wait_ge(h_lo, hb + N_FF2)
                down(q0 + N_FF2 - 1, 1, last=True)

            mlp2(Q_F2A, HT_F2A, 0, 3, A_F2A - 1)
            norm(4, ada_upto=A_KV)
            for t in range(N_KV):
                project(Q_KV + t, G_KV + 2 * t, 384, fresh=None if t else 4)
                wait(pe, ada_saved, A_KV + t)
                ada(A_KV + t)
            pe.wait_ge(evac_a, G_KV + 3)
            pe.wait_ge(evac_d, G_KV + 3)
            pe.wait_ge(n_affine, 24)
            for j in range(2):
                for h in range(NKV):
                    for i in range(TT):
                        for r in range(2):
                            ins = mm(psum[64 * r:64 * r + 64, 5 + j, h * P + i * 64:h * P + i * 64 + 64],
                                     kv[:, i, j, h, :], ident[:, r:P:2])
            ins.then_inc(k_["even"], 1)
            project(Q_NQ, G_Q, fresh=5)
            pe.wait_ge(k_["evens"], 1)
            gate(2, 2, 5)
            pe.wait_ge(k_["wgl"], 1)
            for i in range(TT):
                for k in range(KD):
                    for n, (x, w) in enumerate(((xhi, wgh), (xhi, wgl), (xlo, wgh))):
                        ins = mm(psum[:, 4, 48 * i:48 * i + 48], x[:, k, i * P:(i + 1) * P], w[:, 48 * k:48 * k + 48],
                                 k == 0 and n == 0, k == KD - 1 and n == 2)
            ins.then_inc(k_["g"], 1)

            def compress(j):
                for k in range(16):
                    w1 = raw[:, 2 * j + k // 8, :].rearrange("p (k n) -> p k n", k=8)[:, k % 8, :]
                    ins = mm(psum[0:60, 7, j * CHID:(j + 1) * CHID], fl[:, j, k, :, :].rearrange("p c h -> p (c h)"), w1, k == 0, k == 15)
                    if k % 8 == 7:
                        ins.then_inc(used[2 * j + k // 8], 1)
            pe.wait_ge(k_["flat"], 1)
            for s in range(4):
                pe.wait_ge(raw_full[s], 32 * Q_CMP + 32)
            compress(0)
            pe.wait_ge(evac_a, G_END)
            pe.wait_ge(evac_d, G_END)
            pe.wait_ge(k_["krope"], 1)
            for b in range(2):
                for h in range(NKV):
                    for i in range(TT):
                        x = b * NKV + h
                        ins = te.transpose(psum[:, x // 2, (x % 2) * T + i * P:(x % 2) * T + (i + 1) * P],
                                           nkd[:, i, b, h, :, :].rearrange("p r d -> p (r d)"), ident)
            ins.then_inc(k_["kT"], 1)
            compress(1)
            pe.wait_ge(used[3], Q_CMP + 1)
            pe.nop().then_inc(k_["hid"], 1)

            def queries(src, x, b0, dst):
                pe.wait_ge(k_[src], 1)
                for a2 in range(8):
                    for i in range(TT):
                        ins = te.transpose(psum[:, b0 + a2 // 2, (a2 % 2) * T + i * P:(a2 % 2) * T + (i + 1) * P],
                                           x[:, i, 2 * a2:2 * a2 + 2, :].rearrange("p h d -> p (h d)"), ident)
                ins.then_inc(k_[dst], 1)
            pe.wait_ge(k_["kTs"], 4)
            queries("qn", nq, 0, "qT")
            pe.wait_ge(k_["hidst"], 1)
            pe.wait_ge(k_["gs"], 1)
            for j in range(2):
                for hh in range(2):
                    x = 2 * j + hh
                    ins = te.transpose(psum[:, 4, 128 + x * 60:188 + x * 60], hidt[0:60, j, hh * P:(hh + 1) * P], ident[0:60, 0:60])
            ins.then_inc(k_["hidT"], 1)
            pe.wait_ge(k_["hids"], 1)
            for j in range(2):
                for hh in range(2):
                    ins = mm(psum[0:60, 7, 64 * j:64 * j + 64], hid[:, j, hh, :], w2s[:, j, hh, :], hh == 0, hh == 1)
            ins.then_inc(k_["kc"], 1)
            pe.wait_ge(k_["kcs"], 1)
            pe.wait_ge(bg_saved, 3)
            selv = cst("selv").rearrange("p (h m) -> p h m", h=2)
            for j in range(2):
                ins = mm(psum[:, 5 + j, 0:DN], selv[0:60, j, :], kcv[0:60, 1, :])
            ins.then_inc(k_["vb"], 1)
            pe.wait_ge(k_["kcd"], 1)
            te.transpose(psum[:, 7, 256:316], kcd[0:60, :, :].rearrange("p j d -> p (j d)"), ident[0:60, 0:60]).then_inc(k_["kct"], 1)
            pe.wait_ge(k_["qTs"], 4)
            pe.wait_ge(k_["kcts"], 1)
            for i in range(TT):
                for a2 in range(NH // 2):
                    ins = mm(psum[:, i, 32 * a2:32 * a2 + 32], nqT[:, a2, i * P:(i + 1) * P],
                             kcB[:, 2 * a2 // NG, :, :].rearrange("p r c -> p (r c)"))
            ins.then_inc(k_["cs"], 1)
            pe.wait_ge(k_["vbs"], 1)
            queries("qr", nqr, 4, "qrT")
            pe.wait_ge(k_["cp"], 1)
            for i in range(TT):
                for j in range(2):
                    ins = te.transpose(psum[:, 2, (2 * i + j) * P:(2 * i + j + 1) * P],
                                       pc[:, i, 8 * j:8 * j + 8, :].rearrange("p h c -> p (h c)"), ident)
            ins.then_inc(k_["cT"], 1)
            pe.wait_ge(k_["cTs"], 1)
            pe.wait_ge(k_["qrTs"], 4)
            for i in range(TT):
                for j in range(2):
                    ins = mm(psum[:, 4 + 2 * i + j, :], pcT[:, 2 * i + j, :], vbd[:, j, :, :].rearrange("p h d -> p (h d)"))
            ins.then_inc(k_["co"], 1)
            for w in range(2 * NH + 2):
                if w < 2 * NH:
                    u = w
                    hq, b = u // 2, u % 2
                    r = 64 * (hq % 2)
                    if u >= 2:
                        pe.wait_ge(w_e, u - 1)
                    kT = nkT[r:r + 64, b, hq // NG, :]
                    mm(psum[:, u % 2, 0:384], identb[:], causb[:], True, False, True)
                    mm(psum[:, u % 2, 0:P], nqrT[r:r + 64, hq // 2, 0:P], kT[:, 0:P], False, False, True)
                    mm(psum[:, u % 2, P:384], nqrT[r:r + 64, hq // 2, P:T], kT, False, True, True).then_inc(w_s, 1)
                if 1 <= w <= 2 * NH:
                    u = w - 1
                    pe.wait_ge(w_e, u + 1)
                    if u >= 2:
                        pe.wait_ge(w_pts, u - 1)
                    for b in range(3):
                        ins = te.transpose(psum[:, 2 + u % 2, b * P:(b + 1) * P], pb2[:, u % 2, b * P:(b + 1) * P], ident)
                    ins.then_inc(w_pt, 1)
                if 2 <= w:
                    u = w - 2
                    hq, b = u // 2, u % 2
                    pe.wait_ge(w_pts, u + 1)
                    if u >= 2:
                        pe.wait_ge(w_os, u - 1)
                    else:
                        pe.wait_ge(k_["cos"], 2)
                    o = psum[:, 4 + u % 2, :]
                    vv = kv[:, :, 3 + 2 * b, hq // NG, :]
                    mm(o[:, 0:DN], pT2[:, u % 2, 0:P], vv[:, 0, :])
                    mm(o[:, DN:2 * DN], pT2[:, u % 2, P:T], vv[:, 0, :], True, False)
                    mm(o[:, DN:2 * DN], pT2[:, u % 2, T:384], vv[:, 1, :], False, True).then_inc(w_o, 1)
            pe.wait_ge(w_os, 2 * NH)
            turn(2, ob2.rearrange("p i h d -> p i (h d)"))
            accumulate(Q_NOUT, 2)
            gate(3, 3)
            norm(5, gates=4)
            mlp2(Q_F2B, HT_F2B, 2 * N_FF2, 6)


_INS = ["x", "norm_mix_pre", "norm_mix_post", "norm_ffn_pre", "norm_ffn_post", "w_up", "w_down", "attn_w_qkv", "attn_w_o",
        "c_2", "ada_w_2", "ada_b_2", "norm_mix_2", "norm_ffn_2", "hgrn_w_in_2", "hgrn_out_norm_2", "hgrn_w_out_2",
        "kv_ada_w_2", "kv_ada_b_2", "kv_norm_2", "nsa_w_kv_2", "nsa_k_norm_2", "cmp_pos_2", "cmp_w1_2", "cmp_w2_2",
        "nsa_w_q_2", "nsa_q_norm_2", "nsa_w_out_2", "ffn_w_in_2", "ffn_w_out_2"]


def kernel(**inputs):
    import concourse.bacc as bacc
    from concourse.bass_utils import run_bass_kernel_spmd as run

    nc = bacc.Bacc("TRN2", target_bir_lowering=False, num_devices=1, dynamic_dma_scratch_size=2048)
    arrays, args = {}, {}
    given = {n: np.ascontiguousarray(inputs[n]) for n in _INS}
    for name, x in {**given, **constants()}.items():
        arrays["in_" + name] = x
        args[name] = nc.dram_tensor("in_" + name, x.shape, mybir.dt.from_np(x.dtype), kind="ExternalInput").ap()
    out = nc.dram_tensor("out_0", (1, T, D), F32, kind="ExternalOutput").ap()
    build(nc, args, out)
    r = run(nc, [arrays], core_ids=[0])
    return r.results[0]["out_0"]
```
